# Optimizing a Trainium2 kernel written in Bass

```python
import jax, jax.numpy as jnp
from jax import lax
import numpy as np

D_MODEL = 1024
BATCH = 1
SEQ = 256
DEPTH = 1
DEC_BATCH = 8
DEC_SEQ = 4
PAST_LEN = 2048
PAGE_SIZE = 128

MIX_DIM = D_MODEL
RWKV_DIM = MIX_DIM // 2
HEAD_DIM = 64
RWKV_HEADS = RWKV_DIM // HEAD_DIM
CONV_DIM = MIX_DIM - RWKV_DIM
CONV_WIDTH = 31
DECAY_LORA = 64
AAA_LORA = 64
GATE_LORA = 128
VRES_LORA = 32
SHIFT_DIM = 3 * RWKV_DIM + DECAY_LORA + AAA_LORA + GATE_LORA
PROJ_DIM = SHIFT_DIM + 2 * CONV_DIM
N_EXPERTS = 32
TOP_K = 4
D_FF = D_MODEL
SWIGLU_LIMIT = 7.0
SWIGLU_ALPHA = 1.702
EXPERT_BLOCK = 128
LN_EPS = 1e-5
GN_EPS = 64e-5
DEEPNORM_ALPHA = (2 * DEPTH) ** 0.25
DEEPNORM_BETA = (8 * DEPTH) ** -0.25

kernel_name = "rwkv7_conformer_conv_moe_deepnorm_adaln_step"

def _layernorm(x, g, b, eps=LN_EPS):
    xf = x.astype(jnp.float32)
    mu = xf.mean(-1, keepdims=True)
    var = jnp.square(xf - mu).mean(-1, keepdims=True)
    return ((xf - mu) * lax.rsqrt(var + eps)).astype(x.dtype) * g + b

def _heads(t):
    return t.reshape(t.shape[:-1] + (RWKV_HEADS, HEAD_DIM))

def _wkv_scan(S0, r, w, k, v, a, b):
    def step(S, inp):
        r_t, w_t, k_t, v_t, a_t, b_t = inp
        sa = jnp.einsum('bhij,bhj->bhi', S, a_t)
        S = S * w_t[:, :, None, :] + sa[..., None] * b_t[:, :, None, :] + v_t[..., None] * k_t[:, :, None, :]
        return S, jnp.einsum('bhij,bhj->bhi', S, r_t)
    xs = tuple(jnp.moveaxis(t.astype(jnp.float32), 1, 0) for t in (r, w, k, v, a, b))
    S, ys = lax.scan(step, S0.astype(jnp.float32), xs)
    return jnp.moveaxis(ys, 0, 1), S

def _mixer(h, l, v_first, S0, shift0, conv0, p):
    B, T, _ = h.shape
    z = h @ p['w_in'][l]
    zs, zc = z[..., :SHIFT_DIM], z[..., SHIFT_DIM:]
    zs_prev = jnp.concatenate([shift0[:, None, :].astype(zs.dtype), zs[:, :-1]], axis=1)
    zm = zs + (zs_prev - zs) * p['tm_mu'][l]
    new_shift = zs[:, -1]
    i1, i2, i3 = RWKV_DIM, 2 * RWKV_DIM, 3 * RWKV_DIM
    i4 = i3 + DECAY_LORA
    i5 = i4 + AAA_LORA
    r, k, v = zm[..., :i1], zm[..., i1:i2], zm[..., i2:i3]
    zw, za, zg = zm[..., i3:i4], zm[..., i4:i5], zm[..., i5:]
    w_log = -jax.nn.softplus(-(p['w0'][l] + jnp.tanh(zw) @ p['w2'][l])) - 0.5
    decay = jnp.exp(-jnp.exp(w_log.astype(jnp.float32)))
    a = jax.nn.sigmoid(p['a0'][l] + za @ p['a2'][l])
    g = jax.nn.sigmoid(zg) @ p['g2'][l]
    if l == 0:
        v_first = v
    else:
        vg = jax.nn.sigmoid(p['v0'][l - 1] + (v @ p['v1'][l - 1]) @ p['v2'][l - 1])
        v = v + (v_first - v) * vg
    kk = _heads((k * p['k_k'][l]).astype(jnp.float32))
    kk = kk * lax.rsqrt(jnp.maximum(jnp.sum(kk * kk, -1, keepdims=True), 1e-24))
    k = k * (1 + (a - 1) * p['k_a'][l])
    rh, kh, vh, ah = _heads(r), _heads(k), _heads(v), _heads(a)
    y, S = _wkv_scan(S0, rh, _heads(decay), kh, vh, -kk, kk * ah.astype(jnp.float32))
    ym = y.mean(-1, keepdims=True)
    yv = jnp.square(y - ym).mean(-1, keepdims=True)
    y = ((y - ym) * lax.rsqrt(yv + GN_EPS)).astype(h.dtype)
    y = y * _heads(p['lnx_g'][l]) + _heads(p['lnx_b'][l])
    y = y + jnp.sum(rh * kh * p['r_k'][l], -1, keepdims=True) * vh
    y = y.reshape(B, T, RWKV_DIM) * g
    u = zc[..., :CONV_DIM] * jax.nn.sigmoid(zc[..., CONV_DIM:])
    u_ext = jnp.concatenate([conv0.astype(u.dtype), u], axis=1)
    cv = lax.conv_general_dilated(u_ext, p['conv_w'][l][:, None, :], window_strides=(1,), padding='VALID',
                                  dimension_numbers=('NWC', 'WIO', 'NWC'),
                                  feature_group_count=CONV_DIM) + p['conv_b'][l]
    new_conv = u_ext[:, -(CONV_WIDTH - 1):]
    cv = jax.nn.silu(_layernorm(cv, p['conv_ln_g'][l], p['conv_ln_b'][l]))
    out = jnp.concatenate([y, cv], axis=-1) @ p['w_out'][l]
    return out, v_first, S.astype(h.dtype), new_shift, new_conv

def _moe(h, router_w, router_b, w_gu, b_gu, w_dn, b_dn):
    T, D = h.shape
    TK = T * TOP_K
    logits = (h @ router_w + router_b).astype(jnp.float32)
    top_v, top_i = lax.top_k(logits, TOP_K)
    gates = jax.nn.softmax(top_v, axis=-1).reshape(TK)
    flat_e = top_i.reshape(TK).astype(jnp.int32)
    flat_tok = jnp.arange(TK, dtype=jnp.int32) // TOP_K
    order = jnp.argsort(flat_e)
    e_sorted, tok_sorted, gate_sorted = flat_e[order], flat_tok[order], gates[order]
    counts = jnp.bincount(flat_e, length=N_EXPERTS).astype(jnp.int32)
    padded = (counts + EXPERT_BLOCK - 1) // EXPERT_BLOCK * EXPERT_BLOCK
    padded_end = jnp.cumsum(padded)
    padded_start = padded_end - padded
    start = jnp.cumsum(counts) - counts
    dest = padded_start[e_sorted] + jnp.arange(TK, dtype=jnp.int32) - start[e_sorted]
    n_blocks = -(-TK // EXPERT_BLOCK) + N_EXPERTS
    n_rows = n_blocks * EXPERT_BLOCK
    row_tok = jnp.full((n_rows,), T, jnp.int32).at[dest].set(tok_sorted)
    h_pad = jnp.concatenate([h, jnp.zeros((1, D), h.dtype)], axis=0)
    xb = h_pad[row_tok].reshape(n_blocks, EXPERT_BLOCK, D)
    block_start = jnp.arange(n_blocks, dtype=jnp.int32) * EXPERT_BLOCK
    block_e = jnp.minimum(jnp.searchsorted(padded_end, block_start, side='right'), N_EXPERTS - 1)

    def expert_block(args):
        xblk, e = args
        gu = xblk @ w_gu[e] + b_gu[e]
        gate = jnp.minimum(gu[..., :D_FF], SWIGLU_LIMIT)
        lin = jnp.clip(gu[..., D_FF:], -SWIGLU_LIMIT, SWIGLU_LIMIT)
        act = gate * jax.nn.sigmoid(SWIGLU_ALPHA * gate) * (lin + 1)
        return act @ w_dn[e] + b_dn[e]

    yb = lax.map(expert_block, (xb, block_e)).reshape(n_rows, D)
    y_sorted = yb[dest] * gate_sorted[:, None].astype(h.dtype)
    return jax.ops.segment_sum(y_sorted, tok_sorted, num_segments=T)

def _trunk(x, c, wkv0, shift0, conv0, p):
    B, T, D = x.shape
    v_first = None
    new_wkv, new_shift, new_conv = [], [], []
    cs = jax.nn.silu(c)
    for l in range(DEPTH):
        mod = (cs @ p['ada_w'][l] + p['ada_b'][l])[:, None, :]
        sh1, sc1, g1, sh2, sc2, g2 = jnp.split(mod, 6, axis=-1)
        h = x * (1 + sc1) + sh1
        mix, v_first, S, shf, cnv = _mixer(h, l, v_first, wkv0[l], shift0[l], conv0[l], p)
        x = _layernorm(DEEPNORM_ALPHA * x + g1 * mix, p['ln1_g'][l], p['ln1_b'][l])
        h = x * (1 + sc2) + sh2
        ff = _moe(h.reshape(B * T, D), p['router_w'][l], p['router_b'][l], p['w_gu'][l], p['b_gu'][l],
                  p['w_dn'][l], p['b_dn'][l]).reshape(B, T, D)
        x = _layernorm(DEEPNORM_ALPHA * x + g2 * ff, p['ln2_g'][l], p['ln2_b'][l])
        new_wkv.append(S)
        new_shift.append(shf)
        new_conv.append(cnv)
    return x, jnp.stack(new_wkv), jnp.stack(new_shift), jnp.stack(new_conv)

def setup_inputs(seed: int = 0) -> dict:
    key = jax.random.key(seed)
    ks = jax.random.split(key, 40)
    f32 = jnp.float32
    nrm = lambda k, shape, s: jax.random.normal(k, shape, f32) * s
    L, E = DEPTH, N_EXPERTS
    return {
        'x_prompt': nrm(ks[0], (BATCH, SEQ, D_MODEL), 1.0),
        'x_sample': nrm(ks[1], (DEC_BATCH, DEC_SEQ, D_MODEL), 1.0),
        'state_wkv': nrm(ks[2], (L, DEC_BATCH, RWKV_HEADS, HEAD_DIM, HEAD_DIM), 0.3),
        'state_shift': nrm(ks[3], (L, DEC_BATCH, SHIFT_DIM), 1.0),
        'state_conv': nrm(ks[4], (L, DEC_BATCH, CONV_WIDTH - 1, CONV_DIM), 0.5),
        'c_prompt': nrm(ks[5], (BATCH, D_MODEL), 1.0),
        'c_sample': nrm(ks[6], (DEC_BATCH, D_MODEL), 1.0),
        'w_in': nrm(ks[7], (L, D_MODEL, PROJ_DIM), D_MODEL ** -0.5),
        'tm_mu': jax.random.uniform(ks[8], (L, SHIFT_DIM), f32),
        'w0': jax.random.uniform(ks[9], (L, RWKV_DIM), f32, -4.0, 0.0),
        'w2': nrm(ks[10], (L, DECAY_LORA, RWKV_DIM), 0.1),
        'a0': nrm(ks[11], (L, RWKV_DIM), 0.1),
        'a2': nrm(ks[12], (L, AAA_LORA, RWKV_DIM), 0.1),
        'g2': nrm(ks[13], (L, GATE_LORA, RWKV_DIM), GATE_LORA ** -0.5),
        'v0': nrm(ks[14], (L - 1, RWKV_DIM), 0.1),
        'v1': nrm(ks[15], (L - 1, RWKV_DIM, VRES_LORA), RWKV_DIM ** -0.5),
        'v2': nrm(ks[16], (L - 1, VRES_LORA, RWKV_DIM), 0.1),
        'k_k': 0.85 + nrm(ks[17], (L, RWKV_DIM), 0.05),
        'k_a': 1.0 + nrm(ks[18], (L, RWKV_DIM), 0.05),
        'r_k': nrm(ks[19], (L, RWKV_HEADS, HEAD_DIM), 0.1),
        'lnx_g': 1.0 + nrm(ks[20], (L, RWKV_DIM), 0.05),
        'lnx_b': nrm(ks[21], (L, RWKV_DIM), 0.02),
        'conv_w': nrm(ks[22], (L, CONV_WIDTH, CONV_DIM), CONV_WIDTH ** -0.5),
        'conv_b': nrm(ks[23], (L, CONV_DIM), 0.02),
        'conv_ln_g': 1.0 + nrm(ks[24], (L, CONV_DIM), 0.05),
        'conv_ln_b': nrm(ks[25], (L, CONV_DIM), 0.02),
        'w_out': nrm(ks[26], (L, MIX_DIM, D_MODEL), MIX_DIM ** -0.5 * DEEPNORM_BETA),
        'ada_w': nrm(ks[27], (L, D_MODEL, 6 * D_MODEL), D_MODEL ** -0.5),
        'ada_b': nrm(ks[28], (L, 6 * D_MODEL), 0.02),
        'ln1_g': 1.0 + nrm(ks[29], (L, D_MODEL), 0.05),
        'ln1_b': nrm(ks[30], (L, D_MODEL), 0.02),
        'ln2_g': 1.0 + nrm(ks[31], (L, D_MODEL), 0.05),
        'ln2_b': nrm(ks[32], (L, D_MODEL), 0.02),
        'router_w': nrm(ks[33], (L, D_MODEL, E), D_MODEL ** -0.5),
        'router_b': nrm(ks[34], (L, E), 0.01),
        'w_gu': nrm(ks[35], (L, E, D_MODEL, 2 * D_FF), D_MODEL ** -0.5),
        'b_gu': nrm(ks[36], (L, E, 2 * D_FF), 0.02),
        'w_dn': nrm(ks[37], (L, E, D_FF, D_MODEL), D_FF ** -0.5 * DEEPNORM_BETA),
        'b_dn': nrm(ks[38], (L, E, D_MODEL), 0.02),
    }

def reference(x_prompt, x_sample, state_wkv, state_shift, state_conv, c_prompt, c_sample,
              w_in, tm_mu, w0, w2, a0, a2, g2, v0, v1, v2, k_k, k_a, r_k, lnx_g, lnx_b,
              conv_w, conv_b, conv_ln_g, conv_ln_b, w_out, ada_w, ada_b,
              ln1_g, ln1_b, ln2_g, ln2_b, router_w, router_b, w_gu, b_gu, w_dn, b_dn):
    p = {'w_in': w_in, 'tm_mu': tm_mu, 'w0': w0, 'w2': w2, 'a0': a0, 'a2': a2, 'g2': g2,
         'v0': v0, 'v1': v1, 'v2': v2, 'k_k': k_k, 'k_a': k_a, 'r_k': r_k,
         'lnx_g': lnx_g, 'lnx_b': lnx_b, 'conv_w': conv_w, 'conv_b': conv_b,
         'conv_ln_g': conv_ln_g, 'conv_ln_b': conv_ln_b, 'w_out': w_out,
         'ada_w': ada_w, 'ada_b': ada_b, 'ln1_g': ln1_g, 'ln1_b': ln1_b,
         'ln2_g': ln2_g, 'ln2_b': ln2_b, 'router_w': router_w, 'router_b': router_b,
         'w_gu': w_gu, 'b_gu': b_gu, 'w_dn': w_dn, 'b_dn': b_dn}
    Bp = x_prompt.shape[0]
    dt = x_prompt.dtype
    wkv0 = jnp.zeros((DEPTH, Bp, RWKV_HEADS, HEAD_DIM, HEAD_DIM), dt)
    shift0 = jnp.zeros((DEPTH, Bp, SHIFT_DIM), dt)
    conv0 = jnp.zeros((DEPTH, Bp, CONV_WIDTH - 1, CONV_DIM), dt)
    y_prompt, wkv_p, shift_p, conv_p = _trunk(x_prompt, c_prompt, wkv0, shift0, conv0, p)
    y_sample, wkv_s, shift_s, conv_s = _trunk(x_sample, c_sample, state_wkv, state_shift, state_conv, p)
    return (y_prompt, y_sample, wkv_p, wkv_s, shift_p, shift_s, conv_p, conv_s)


_drawn_inputs = setup_inputs


def setup_inputs(seed=0):
    import zlib

    import numpy as np

    out = dict(_drawn_inputs(seed))
    spreads = {}
    factors = {'lnx_g': 4.547,
     'lnx_b': 9.387,
     'conv_b': 2.84,
     'conv_ln_g': 3.779,
     'conv_ln_b': 11.228,
     'ln2_b': 2.746,
     'router_b': 3.583,
     'b_gu': 8.0,
     'b_dn': 8.0}
    for name, (base, spread) in spreads.items():
        noise = np.random.default_rng([zlib.crc32(name.encode()), seed]).standard_normal(out[name].shape)
        drawn = base * np.exp(spread * noise) if base else spread * noise
        out[name] = __import__('jax').numpy.asarray(drawn.astype(out[name].dtype))
    for name, factor in factors.items():
        out[name] = (out[name] * factor).astype(out[name].dtype)
    return out
```

```python
from contextlib import ExitStack

import concourse.bass as bass
from concourse import mybir

F32 = mybir.dt.float32
I32 = mybir.dt.int32
U32 = mybir.dt.uint32
ALU = mybir.AluOpType
ACT = mybir.ActivationFunctionType
AX = mybir.AxisListType.X

P = 128
D = 1024
KD = D // P
NPR = 256
NB, NT = 8, 4
NS = NB * NT
N = NPR + NS
TILES = [(0, P), (P, P), (NPR, NS)]
H, HD = 8, 64
CH = 4
SH = 14
ZB = 22
EXT = 1 + NPR + NB * (1 + NT)
TAPS = 31
PC = TAPS - 1 + NPR
SC = TAPS - 1 + NT
UW = PC + NB * SC
L = 32
E = 32
FF = D
C = 64
MAXIT = E + (N * 4) // (C + 1)
ALPHA = 2.0 ** 0.25
C0 = 0.6065306597126334
LN_EPS, GN_EPS = 1e-5, 64e-5
LIMIT, SWI = 7.0, 1.702


def columns(*widths):
    at, table = 0, {}
    for name, width in widths:
        table[name] = at
        at += width
    return table, at


PAR, NPAR = columns(("mu", SH), ("w0", CH), ("a0", CH), ("kk", CH), ("ka", CH), ("rk", CH), ("lg", CH), ("lb", CH),
                    ("cw", CH * TAPS), ("cb", CH), ("cg", CH), ("cbt", CH), ("adab", 2 * KD))
CST, NCST = columns(("ident", P), ("tri", 2 * P), ("low", P), ("tri_s", 2 * NS), ("low_s", NS), ("scan", N),
                    ("head", P), ("c512", P), ("sel", P + NS), ("before", P), ("ones", P), ("iota32", E),
                    ("slot", C), ("bmask", NB))


def rounds(t):
    return 4 if t < 2 else 1


def psum_units():
    names = ["modT", "row0", "row1"] + [f"z{b}" for b in range(ZB)]
    names += [f"{x}{b}" for x in "wag" for b in range(CH)] + [f"kk{b}" for b in range(CH)]
    names += [f"rk{b}" for b in range(CH)]
    names += [f"{x}tok{t}" for t in range(3) for x in "bkva"]
    for t in range(3):
        names += [f"G{t}_{h}" for h in range(H)] + [f"A{t}_{g}" for g in range(2)]
        for m in range(1, rounds(t) + 1):
            names += [f"N{t}_{m}_{g}" for g in range(2)]
            if m < rounds(t):
                names += [f"NT{t}_{m}_{g}" for g in range(2)]
            names += [f"TT{t}_{m}_{g}" for g in range(2)]
        names += [f"W{t}", f"ZA{t}", f"ZV{t}"]
        if t < 2:
            for q in range(4):
                names += [f"U{t}_{q}_0", f"U{t}_{q}_1", f"Y{t}_{q}_0", f"Y{t}_{q}_1", f"S{t}_{q}"]
        else:
            names += ["UY0", "UY1", "Us"] + [f"Ss{b}" for b in range(CH)]
        names += [f"Y{t}"]
    names += [f"gm{b}" for b in range(CH)] + [f"gv{b}" for b in range(CH)] + ["cm", "cv"]
    for t in range(3):
        names += [f"{x}_{t}_{j}" for x in ("g1", "mix") for j in range(2)]
    for t in range(3):
        names += [f"{x}_{t}_{j}" for x in ("sc2", "sh2", "g2") for j in range(2)]
        names += [f"hT{t}_{j}" for j in range(2)] + [f"lg{t}"]
    names += ["rank0", "rank1", "rank2", "count", "gt0", "gt1", "gt2"]
    return {n: (i % 8, i // 8) for i, n in enumerate(names)}


class Counted:

    def __init__(self, eng, step):
        self.eng, self.step, self.n = eng, step, {}

    def __call__(self, ins, sem=None, wait=True):
        sem = self.step if sem is None else sem
        self.n[sem.name] = self.n.get(sem.name, 0) + 1
        ins.then_inc(sem, 1)
        if wait:
            self.eng.wait_ge(sem, self.n[sem.name])


def build(nc, io):
    unit = psum_units()
    with ExitStack() as ctx:
        def sem(name):
            return ctx.enter_context(nc.semaphore(name))

        arena = ctx.enter_context(nc.sbuf_tensor("arena", [P, 53000], F32))
        cumi = ctx.enter_context(nc.sbuf_tensor("cumi", [P, E + 1], I32))
        top_i = ctx.enter_context(nc.sbuf_tensor("top_i", [P, 3, 8], U32))
        slot_i = ctx.enter_context(nc.sbuf_tensor("slot_i", [P, 12], U32))
        ps = ctx.enter_context(nc.psum_tensor("ps", [P, 8, 512], F32))
        y_dram = nc.dram_tensor("y_slots", (MAXIT * C, D), F32, kind="Internal").ap()
        res_dram = nc.dram_tensor("residual", (2, 3, P, D), F32, kind="Internal").ap()

        def at(off, *shape):
            n = 1
            for s in shape:
                n *= s
            a = arena[:, off:off + n]
            if len(shape) == 2:
                a = a.rearrange("p (a b) -> p a b", a=shape[0])
            if len(shape) == 3:
                a = a.rearrange("p (a b c) -> p a b c", a=shape[0], b=shape[1])
            return a

        W = CH * N
        gu = [at(0, KD, 2 * FF), at(16384, KD, 2 * FF)]
        dn = at(32768, KD, D)
        o = 40960
        par = at(o, NPAR)
        o += NPAR
        cst = at(o, NCST)
        o += NCST
        h2 = at(o, 3, D)
        o += 3 * D
        gslot = at(o, 3, E)
        o += 3 * E
        gates = at(o, 3, 4)
        o += 12
        gT = at(o, N)
        o += N
        small = at(o, 400)
        o += 400
        moe0 = o
        b_gu = at(o, 2 * FF)
        o += 2 * FF
        hTe = at(o, KD, C)
        o += KD * C
        pick = at(o, 3, C)
        o += 3 * C
        sel_e = at(o, C)
        o += C
        gateS, sigS, linS, actS, yS = [at(o + 512 * i, 512) for i in range(5)]
        actT = at(o + 2560, 4, P)
        assert o + 3072 <= 53000
        hT = at(0, KD, N)
        zs = at(2304, SH, EXT)
        zm = at(6462, SH, N)
        ue = at(10560, CH, UW)
        cat = at(12800, KD, N)
        rows = at(15104, 2, 512)
        adab = at(16128, 2, 512)
        aT, gate, kp, EI, bonus, bt, kt = [at(17152 + i * W, CH, N) for i in range(7)]
        usg, lact, YT, ysq, yrs = bonus, kt, kp, bt, kt
        AR = at(25216, CH, 2, N)
        bb, kb, t1, t2 = [at(27520 + i * W, CH, N) for i in range(4)]
        cvsq, cvsg = at(25216, CH, N), at(25216 + W, CH, N)
        sg, kkn, cumI, EE, EN = [at(i * W, CH, N) for i in range(5)]
        tok = {x: at(i * 1536, 3, 512) for i, x in enumerate("bkva")}
        W1, ZV, Ut, ZAT = [at(6462 + i * 512, 512) for i in range(4)]
        ZR, Utr = at(6462 + 1536, CH, 2, NS), at(6462 + 1792, CH, NS)
        ST0 = at(8510, CH, NB, HD)
        MK0 = 27520
        nbuf = [moe0 + i * 1024 for i in range(6)]
        masked = [at(MK0 + 1024, 2, 2, NB * HD), at(moe0, 2, 2, NB * HD)]
        dprev = at(32128, N)
        cs, cT, modT = at(32416, KD, 9), at(32488, KD, 9), at(32560, 16, 9)
        ST, STd = at(16128, CH, HD), at(16384, CH, HD)
        zero = at(16640, 512)
        ada_buf = [at(32768 + i * 4096, KD, 512) for i in range(2)]
        win_buf = [at(32768 + i * 1024, KD, P) for i in range(8)]
        w_out = at(32768, KD, D)
        lora = at(moe0 + 512, 2, 512)
        shift_in = at(moe0, SH, NB)
        shift_out = at(moe0 + 6144, SH, 9)
        omk = small[:, 0:CH]
        xin, lnp, xa, tA = at(0, 3, D), at(3072, 2, D), at(5120, 3, D), at(8192, 3, D)
        h2T, rw, rb = at(17152, KD, N), at(19456, KD, E), at(19712, E)
        oh, mk, lgt, Gd = at(19744, 12, E), at(20128, 3, E), at(20224, 3, E), at(20320, 3, E)
        g2b = at(20480, 3, D)
        ohs = at(23552, 12, E)
        stats = small[:, 4:16].rearrange("p (a b) -> p a b", a=2)
        mv, rstd, nmr = small[:, 16:18], small[:, 18:19], small[:, 19:20]
        top_v, idxf, e4, esum = small[:, 20:28], small[:, 28:36], small[:, 36:40], small[:, 40:41]
        cnt, npf, npt, cumf = small[:, 48:80], small[:, 80:112], small[:, 112:144], small[:, 144:177]
        sidx, slotv = small[:, 180:192], small[:, 192:288]
        yg, bdn = at(0, 12, D), at(12288, D)
        fx, fr, fg, fln = at(13312, 3, D), at(16384, 3, D), at(19456, 3, D), at(22528, 2, D)

        def c_(name, w, n=P, p0=0):
            return cst[p0:p0 + n, CST[name]:CST[name] + w]

        def p_(name, i):
            return par[:, PAR[name] + i:PAR[name] + i + 1]

        ident = c_("ident", P)

        def smp(a):
            return a.rearrange("p (b t) -> p b t", b=NB)

        filled = [sem(f"bank{b}_filled") for b in range(8)]
        emptied = [sem(f"bank{b}_emptied") for b in range(8)]
        (zero_ready, ring_free, var_ready, root_ready, params_in, x_in, rows_in, ada_used, states_in, lora_in, wkv_in, wout_in, tail_in, moe_in, csig_ready, cs_ready,
         h_ready, zm_ready, tanh_ready, gsig_ready, u_ready, sq_ready, rk_ready, cum_ready, exp_ready, tilde_ready,
         st_ready, tt0_ready, zr_ready, um_ready, conv_done, ysq_ready, yc_ready, cvc_ready, cvsq_ready, cvn_ready,
         cvsg_ready, cat_ready, x1_ready, h2_ready, delta_ready, e4_ready, mask_ready, gd_ready, shift_ready,
         table_ready, rows_ready, stored, spilled, vstep, astep) = [sem(n) for n in (
             "zero_ready ring_free var_ready root_ready params_in x_in rows_in ada_used states_in lora_in wkv_in wout_in tail_in moe_in csig_ready cs_ready "
             "h_ready zm_ready tanh_ready gsig_ready u_ready sq_ready rk_ready cum_ready exp_ready tilde_ready "
             "st_ready tt0_ready zr_ready um_ready conv_done ysq_ready yc_ready cvc_ready cvsq_ready cvn_ready "
             "cvsg_ready cat_ready x1_ready h2_ready delta_ready e4_ready mask_ready gd_ready shift_ready "
             "table_ready rows_ready stored spilled vector_step scalar_step").split()]
        ada_in = [sem(f"ada_in{i}") for i in range(2)]
        win_in = [sem(f"win_in{i}") for i in range(8)]
        gu_in = [[sem(f"gu{s}_in{c}") for c in range(4)] for s in range(2)]
        dn_in = [sem(f"dn_in{c}") for c in range(2)]
        (slot_ready, pick_ready, gathered, hTe_ready, gu_done, gate_ready, lin_ready, sig_ready, prod_ready, act_ready,
         act_turned, actT_ready, dn_done, y_out, y_stored, final_in, bias_ready, out_ready, fstep) = [
             sem(n) for n in ("slot_ready pick_ready gathered hTe_ready gu_done gate_ready lin_ready sig_ready "
                              "prod_ready act_ready act_turned actT_ready dn_done y_out y_stored final_in bias_ready "
                              "out_ready final_step").split()]
        rowsg_in = [sem(f"rows_gathered{t}") for t in range(3)]

        def evicted(eng, name):
            b, i = unit[name]
            eng.wait_ge(emptied[b], i + 1)

        def arrived(eng, name):
            b, i = unit[name]
            eng.wait_ge(filled[b], i + 1)
            return ps[:, b, :]

        def read(ins, name):
            ins.then_inc(emptied[unit[name][0]], 1)
            return name

        block = ctx.enter_context(nc.Block())

        @block.sync
        def _(sp):
            sp.dma_start(cst, io["cst"]).then_inc(params_in, 16)
            sp.dma_start(par, io["par"]).then_inc(params_in, 16)
            sp.dma_start(cT, io["cT"]).then_inc(params_in, 16)
            sp.dma_start(hT, io["xT"]).then_inc(x_in, 16)
            for j in range(4):
                sp.dma_start(adab[32 * j:32 * j + 9, :, :], io["adab_rows"][j]).then_inc(rows_in, 16)
            used = 0
            for n in range(12):
                if n >= 2:
                    if n - 2 in (3, 7):
                        arrived(sp, {3: "modT", 7: "row0"}[n - 2])
                    else:
                        used += 1
                        sp.wait_ge(ada_used, used)
                sp.dma_start(ada_buf[n % 2], io["ada"][n]).then_inc(ada_in[n % 2], 16)
            arrived(sp, "row1")
            for b in range(ZB):
                if b >= 8:
                    arrived(sp, f"z{b - 8}")
                sp.dma_start(win_buf[b % 8], io["win"][b]).then_inc(win_in[b % 8], 16)
                if b == 1:
                    sp.dma_start(lora, io["lora"]).then_inc(lora_in, 16)
                    sp.dma_start(shift_in, io["shiftT"]).then_inc(states_in, 16)
                    sp.dma_start(ue[:, :, 0:TAPS - 1], io["conv0"]).then_inc(states_in, 16)
                    for c in range(CH):
                        sp.dma_start(ue[:, c, PC:UW].rearrange("p (b s) -> p b s", b=NB)[:, :, 0:TAPS - 1],
                                     io["convs"][:, c, :, :]).then_inc(states_in, 16)
            arrived(sp, f"z{ZB - 1}")
            sp.dma_start(w_out, io["w_out"]).then_inc(wout_in, 16)
            sp.wait_ge(zero_ready, 1)
            for j in range(2):
                sp.dma_start(y_dram[E * C:MAXIT * C, 512 * j:512 * j + 512].rearrange("(p a) n -> p a n", p=64),
                             zero[0:64, :].unsqueeze(1).to_broadcast([64, MAXIT - E, 512])).then_inc(y_stored, 16)
            sp.wait_ge(shift_ready, 2)
            sp.dma_start(io["shift_out"], shift_out).then_inc(stored, 16)
            sp.wait_ge(u_ready, 2 * CH)
            sp.dma_start(io["conv_p"], ue[:, :, NPR:PC]).then_inc(stored, 16)
            for c in range(CH):
                sp.dma_start(io["conv_s"][:, c, :, :],
                             ue[:, c, PC:UW].rearrange("p (b s) -> p b s", b=NB)[:, :, NT:SC]).then_inc(stored, 16)
            evicted(sp, "vtok2")
            sp.dma_start(ST0, io["wkvT"]).then_inc(wkv_in, 16)
            evicted(sp, "S1_3")
            sp.dma_start(io["wkv_p"], ST).then_inc(stored, 16)
            for b in range(CH):
                evicted(sp, f"Ss{b}")
            sp.dma_start(io["wkv_s"], ST0).then_inc(stored, 16)
            sp.wait_ge(cat_ready, 2 * CH)
            sp.wait_ge(stored, 16 * 8)
            for t, (a, n) in enumerate(TILES):
                sp.dma_start(xin[0:n, t, :], io["x"][a:a + n, :]).then_inc(tail_in, 16)
            for i in range(2):
                sp.dma_start(lnp[:, i, :], io["ln"][i:i + 1, :].to_broadcast([P, D])).then_inc(tail_in, 16)
            sp.dma_start(rw, io["rw"]).then_inc(tail_in, 16)
            sp.dma_start(rb[0:1, :], io["rb"]).then_inc(tail_in, 16)
            for t, (a, n) in enumerate(TILES):
                sp.wait_ge(x1_ready, t + 1)
                sp.dma_start(res_dram[0, t, 0:n, :], xa[0:n, t, :]).then_inc(spilled, 16)
            for t, (a, n) in enumerate(TILES):
                for j in range(2):
                    evicted(sp, f"g2_{t}_{j}")
                sp.dma_start(res_dram[1, t, 0:n, :], g2b[0:n, t, :]).then_inc(spilled, 16)
            sp.dma_start(b_gu[0:E, :], io["b_gu"]).then_inc(moe_in, 16)
            sp.wait_ge(spilled, 16 * 6)
            for n in ("rank2", "count", "gt0", "gt1", "gt2"):
                evicted(sp, n)
            sp.wait_ge(table_ready, 4)
            wg, wd = io["w_gu"], io["w_dn"]

            def load_gu(s, e):
                for c in range(4):
                    sp.dma_start(gu[s][:, 2 * c:2 * c + 2, :],
                                 wg[bass.ds(e, 1), 256 * c:256 * c + 256, :].rearrange("e (k p) n -> p (e k) n", p=P)
                                 ).then_inc(gu_in[s][c], 16)

            def load_dn(e):
                for c in range(2):
                    sp.dma_start(dn[:, 4 * c:4 * c + 4, :],
                                 wd[bass.ds(e, 1), 512 * c:512 * c + 512, :].rearrange("e (k p) n -> p (e k) n", p=P)
                                 ).then_inc(dn_in[c], 16)

            load_gu(0, 0)
            load_dn(0)
            load_gu(1, 1)
            items = sp.value_load(cumi[0:1, 1:2], min_val=0, max_val=MAXIT)
            sp.wait_ge(dn_done, items)
            load_dn(1)
            with sp.Fori(1, E // 2) as pair:
                e = pair * 2
                for s in range(2):
                    through = sp.value_load(cumi[0:1, bass.ds(e + (s - 1), 1)], min_val=0, max_val=MAXIT)
                    sp.wait_ge(gu_done, through)
                    load_gu(s, e + s)
                    through = sp.value_load(cumi[0:1, bass.ds(e + s, 1)], min_val=0, max_val=MAXIT)
                    sp.wait_ge(dn_done, through)
                    load_dn(e + s)
            total = sp.value_load(cumi[0:1, E:E + 1], min_val=0, max_val=MAXIT)
            sp.wait_ge(dn_done, total)
            for t, (a, n) in enumerate(TILES):
                sp.dma_start(fx[0:n, t, :], res_dram[0, t, 0:n, :]).then_inc(final_in, 16)
                sp.dma_start(fg[0:n, t, :], res_dram[1, t, 0:n, :]).then_inc(final_in, 16)
            for i in range(2):
                sp.dma_start(fln[:, i, :], io["ln"][2 + i:3 + i, :].to_broadcast([P, D])).then_inc(final_in, 16)
            sp.dma_start(bdn[0:E, :], io["b_dn"]).then_inc(final_in, 16)
            for t, (a, n) in enumerate(TILES):
                sp.wait_ge(out_ready, t + 1)
                sp.dma_start(io["y"][a:a + n, :], fr[0:n, t, :]).then_inc(stored, 16)
            sp.wait_ge(stored, 16 * 11)

        @block.gpsimd
        def _(pool):
            pool.wait_ge(table_ready, 4)
            total = pool.value_load(cumi[0:1, E:E + 1], min_val=0, max_val=MAXIT)
            mark = small[:, 314:315]
            nc.gpsimd.memset(mark, 0.0).then_inc(ring_free, 1)
            pool.wait_ge(ring_free, 1)
            pool.wait_ge(dn_done, total)
            nc.gpsimd.tensor_tensor(mark, mark, mark, ALU.add).then_inc(ring_free, 1)
            pool.wait_ge(ring_free, 2)
            pool.wait_ge(y_stored, total * 32 + 32)
            nc.gpsimd.tensor_tensor(mark, mark, mark, ALU.add).then_inc(ring_free, 1)
            pool.wait_ge(ring_free, 3)
            for t, (a, n) in enumerate(TILES):
                for k in range(4):
                    pool.indirect_dma_start(
                        out=yg[0:n, 4 * t + k, :], out_offset=None, in_=y_dram[:, :],
                        in_offset=bass.IndirectOffsetOnAxis(ap=slot_i[0:n, 4 * t + k:4 * t + k + 1], axis=0),
                    ).then_inc(rowsg_in[t], 16)

        @block.tensor
        def _(pe):
            def open_(name):
                b, i = unit[name]
                if i:
                    pe.wait_ge(emptied[b], i)
                return ps[:, b, :]

            def close(ins, name):
                ins.then_inc(filled[unit[name][0]], 1)

            def mm(out, lhsT, rhs, first=True, last=True):
                return nc.tensor.matmul(out, lhsT, rhs, start=first, stop=last)

            def turn(out, src, n=P):
                return nc.tensor.transpose(out, src, ident[0:n, 0:n])

            pe.wait_ge(cs_ready, 1)
            q = open_("modT")
            for n in range(12):
                pe.wait_ge(ada_in[n % 2], 16 * (n // 2 + 1))
                if n < 4:
                    for m in range(4):
                        c9 = (4 * n + m) * 9
                        for k in range(KD):
                            last = mm(q[:, c9:c9 + 9], ada_buf[n % 2][:, k, P * m:P * m + P], cs[:, k, :],
                                      k == 0, k == KD - 1)
                else:
                    r, j = divmod(n - 4, 4)
                    if j == 0:
                        q = open_(f"row{r}")
                    for k in range(KD):
                        last = mm(q[32 * j:32 * j + 9, :], cs[:, k, :], ada_buf[n % 2][:, k, :], k == 0, k == KD - 1)
                if n in (3, 7, 11):
                    close(last, {3: "modT", 7: "row0", 11: "row1"}[n])
                else:
                    last.then_inc(ada_used, 1)
            pe.wait_ge(h_ready, 1)
            for b in range(ZB):
                q = open_(f"z{b}")
                pe.wait_ge(win_in[b % 8], 16 * (b // 8 + 1))
                for k in range(KD):
                    last = mm(q[:, 0:N], win_buf[b % 8][:, k, :], hT[:, k, :], k == 0, k == KD - 1)
                close(last, f"z{b}")
            pe.wait_ge(lora_in, 16)
            pe.wait_ge(tanh_ready, 1)
            for b in range(CH):
                close(mm(open_(f"w{b}")[:, 0:N], lora[0:64, 0, P * b:P * b + P], lact[0:64, 0, :]), f"w{b}")
            for b in range(CH):
                close(mm(open_(f"a{b}")[:, 0:N], lora[64:128, 0, P * b:P * b + P], zm[64:128, 12, :]), f"a{b}")
            pe.wait_ge(gsig_ready, 1)
            for b in range(CH):
                close(mm(open_(f"g{b}")[:, 0:N], lora[:, 1, P * b:P * b + P], lact[:, 1, :]), f"g{b}")
            head = c_("head", P)
            pe.wait_ge(sq_ready, 1)
            for b in range(CH):
                close(mm(open_(f"kk{b}")[:, 0:N], head, t2[:, b, :]), f"kk{b}")
            pe.wait_ge(rk_ready, CH)
            for b in range(CH):
                close(mm(open_(f"rk{b}")[:, 0:N], head, t2[:, b, :]), f"rk{b}")
            pe.wait_ge(tilde_ready, 1)
            src = {"b": bb, "k": kb, "v": zm[:, 2 * CH:3 * CH, :], "a": AR[:, :, 0, :]}
            for t, (a, n) in enumerate(TILES):
                for x in "bkva":
                    q = open_(f"{x}tok{t}")
                    for b in range(CH):
                        last = turn(q[0:n, P * b:P * b + P], src[x][:, b, a:a + n])
                    close(last, f"{x}tok{t}")
            for x in "bkva":
                evicted(pe, f"{x}tok2")
            for t, (a, n) in enumerate(TILES):
                mkt = at(MK0, H, 4 * n)
                Nb, NTb, TTb = [[at(nbuf[2 * x + y], 2, CH, n) for y in range(2)] for x in range(3)]
                for h in range(H):
                    g, b = h % 2, h // 2
                    pr = slice(64 * g, 64 * g + 64)
                    q = open_(f"G{t}_{h}")
                    for i, x in enumerate((bt, kt)):
                        last = mm(q[0:n, 2 * n * i:2 * n * (i + 1)].rearrange("p (a b) -> p a b", a=2),
                                  x[pr, b, a:a + n], AR[pr, b, :, a:a + n])
                    close(last, f"G{t}_{h}")
                for g in range(2):
                    pr = slice(64 * g, 64 * g + 64)
                    q = open_(f"A{t}_{g}")
                    for b in range(CH):
                        last = mm(q[0:n, n * b:n * b + n], AR[pr, b, 0, a:a + n], bt[pr, b, a:a + n])
                    close(last, f"A{t}_{g}")
                for h in range(H):
                    evicted(pe, f"G{t}_{h}")
                for m in range(1, rounds(t) + 1):
                    for g in range(2):
                        evicted(pe, f"A{t}_{g}" if m == 1 else f"N{t}_{m - 1}_{g}")
                        if m > 1:
                            evicted(pe, f"NT{t}_{m - 1}_{g}")
                        q = open_(f"N{t}_{m}_{g}")
                        for b in range(CH):
                            NTp = mkt[0:n, 2 * b + g, 0:n] if m == 1 else NTb[(m - 1) % 2][0:n, g, b, :]
                            last = mm(q[0:n, n * b:n * b + n], NTp, Nb[(m - 1) % 2][0:n, g, b, :])
                        close(last, f"N{t}_{m}_{g}")
                    for g in range(2):
                        if m == rounds(t):
                            break
                        q = open_(f"NT{t}_{m}_{g}")
                        for b in range(CH):
                            NTp = mkt[0:n, 2 * b + g, 0:n] if m == 1 else NTb[(m - 1) % 2][0:n, g, b, :]
                            last = mm(q[0:n, n * b:n * b + n], Nb[(m - 1) % 2][0:n, g, b, :], NTp)
                        close(last, f"NT{t}_{m}_{g}")
                    for g in range(2):
                        evicted(pe, f"N{t}_{m}_{g}")
                        if m == 1:
                            pe.wait_ge(tt0_ready, 2 * t + g + 1)
                        else:
                            evicted(pe, f"TT{t}_{m - 1}_{g}")
                        q = open_(f"TT{t}_{m}_{g}")
                        for b in range(CH):
                            last = mm(q[0:n, n * b:n * b + n], Nb[m % 2][0:n, g, b, :],
                                      TTb[(m - 1) % 2][0:n, g, b, :])
                        close(last, f"TT{t}_{m}_{g}")
                TTf = TTb[rounds(t) % 2]
                q = open_(f"W{t}")
                for h in range(H):
                    last = mm(q[0:n, HD * h:HD * h + HD], mkt[0:n, h, 2 * n:3 * n], tok["v"][0:n, t, HD * h:HD * h + HD])
                close(last, f"W{t}")
                for g in range(2):
                    evicted(pe, f"TT{t}_{rounds(t)}_{g}")
                q = open_(f"ZA{t}")
                for h in range(H):
                    g, b = h % 2, h // 2
                    last = mm(q[64 * g:64 * g + 64, n * b:n * b + n], tok["a"][0:n, t, HD * h:HD * h + HD],
                              TTf[0:n, g, b, :])
                close(last, f"ZA{t}")
                evicted(pe, f"W{t}")
                q = open_(f"ZV{t}")
                for h in range(H):
                    last = mm(q[0:n, HD * h:HD * h + HD], TTf[0:n, h % 2, h // 2, :], W1[0:n, HD * h:HD * h + HD])
                close(last, f"ZV{t}")
                evicted(pe, f"ZA{t}")
                if t < 2:
                    for c in range(4):
                        rq = slice(32 * c, 32 * c + 32)
                        if t == 0 and c == 0:
                            pe.wait_ge(st_ready, 1)
                        else:
                            evicted(pe, f"S{t}_{c - 1}" if c else f"S{t - 1}_3")
                        for g in range(2):
                            pr = slice(64 * g, 64 * g + 64)
                            q = open_(f"U{t}_{c}_{g}")
                            for b in range(CH):
                                last = mm(q[rq, HD * b:HD * b + HD], ZAT[pr, P * b + 32 * c:P * b + 32 * c + 32],
                                          ST[pr, b, :])
                            close(last, f"U{t}_{c}_{g}")
                        for g in range(2):
                            pr = slice(64 * g, 64 * g + 64)
                            q = open_(f"Y{t}_{c}_{g}")
                            for b in range(CH):
                                last = mm(q[pr, L * b:L * b + L], ST[pr, b, :],
                                          AR[pr, b, 1, a + 32 * c:a + 32 * c + 32])
                            close(last, f"Y{t}_{c}_{g}")
                        for g in range(2):
                            evicted(pe, f"U{t}_{c}_{g}")
                        q = open_(f"S{t}_{c}")
                        for h in range(H):
                            g, b = h % 2, h // 2
                            hs = slice(HD * h, HD * h + HD)
                            o_ = q[64 * g:64 * g + 64, HD * b:HD * b + HD]
                            mm(o_, tok["b"][rq, t, hs], Ut[rq, hs], True, False)
                            last = mm(o_, tok["k"][rq, t, hs], tok["v"][rq, t, hs], False, True)
                        close(last, f"S{t}_{c}")
                else:
                    pe.wait_ge(wkv_in, 16)
                    pe.wait_ge(zr_ready, 1)
                    for g in range(2):
                        pr = slice(64 * g, 64 * g + 64)
                        q = open_(f"UY{g}")
                        qv = q[:, 0:2 * CH * NS].rearrange("p (b a n) -> p b a n", b=CH, a=2)
                        for b in range(CH):
                            for s in range(NB):
                                last = mm(qv[pr, b, :, NT * s:NT * s + NT], ST0[pr, b, s, :],
                                          ZR[pr, b, :, NT * s:NT * s + NT])
                        close(last, f"UY{g}")
                    for g in range(2):
                        evicted(pe, f"UY{g}")
                    q = open_("Us")
                    for b in range(CH):
                        last = turn(q[0:NS, P * b:P * b + P], Utr[:, b, :])
                    close(last, "Us")
                    for b in range(CH):
                        pe.wait_ge(um_ready, 4 * b + 4)
                        q = open_(f"Ss{b}")
                        for g in range(2):
                            hs = slice(HD * (2 * b + g), HD * (2 * b + g) + HD)
                            o_ = q[64 * g:64 * g + 64, :]
                            mm(o_, tok["b"][0:NS, t, hs], masked[b % 2][0:NS, 0, g, :], True, False)
                            last = mm(o_, tok["k"][0:NS, t, hs], masked[b % 2][0:NS, 1, g, :], False, True)
                        close(last, f"Ss{b}")
                q = open_(f"Y{t}")
                for h in range(H):
                    g, b = h % 2, h // 2
                    hs = slice(HD * h, HD * h + HD)
                    o_ = q[64 * g:64 * g + 64, n * b:n * b + n]
                    mm(o_, Ut[0:n, hs], mkt[0:n, h, n:2 * n], True, False)
                    last = mm(o_, tok["v"][0:n, t, hs], mkt[0:n, h, 3 * n:4 * n], False, True)
                close(last, f"Y{t}")
            for t in range(3):
                evicted(pe, f"Y{t}")
            for b in range(CH):
                close(mm(open_(f"gm{b}")[:, 0:N], head, YT[:, b, :]), f"gm{b}")
            for b in range(CH):
                pe.wait_ge(ysq_ready, b + 1)
                close(mm(open_(f"gv{b}")[:, 0:N], head, ysq[:, b, :]), f"gv{b}")
            pe.wait_ge(conv_done, 2 * CH * TAPS)
            q = open_("cm")
            for b in range(CH):
                last = mm(q[:, 0:N], c_("c512", P), cat[:, CH + b, :], b == 0, b == CH - 1)
            close(last, "cm")
            pe.wait_ge(cvsq_ready, 1)
            q = open_("cv")
            for b in range(CH):
                last = mm(q[:, 0:N], c_("c512", P), cvsq[:, b, :], b == 0, b == CH - 1)
            close(last, "cv")

            def spread(name, r, j, t):
                n = TILES[t][1]
                s = c_("sel", P + NS, 9, 32 * j)[:, 0:n] if t < 2 else c_("sel", P + NS, 9, 32 * j)[:, P:P + NS]
                close(mm(open_(name)[0:n, :], s, rows[32 * j:32 * j + 9, r, :]), name)

            pe.wait_ge(rows_ready, 8)
            pe.wait_ge(wout_in, 16)
            pe.wait_ge(cat_ready, 2 * CH)
            for t, (a, n) in enumerate(TILES):
                for j in range(2):
                    spread(f"g1_{t}_{j}", 0, j, t)
                for j in range(2):
                    q = open_(f"mix_{t}_{j}")
                    for k in range(KD):
                        last = mm(q[0:n, :], cat[:, k, a:a + n], w_out[:, k, 512 * j:512 * j + 512], k == 0, k == KD - 1)
                    close(last, f"mix_{t}_{j}")
            pe.wait_ge(tail_in, 16 * 7)
            for t, (a, n) in enumerate(TILES):
                for j in range(2):
                    spread(f"sc2_{t}_{j}", 1, j, t)
                for j in range(2):
                    spread(f"sh2_{t}_{j}", 0, 2 + j, t)
                for j in range(2):
                    spread(f"g2_{t}_{j}", 1, 2 + j, t)
                for j in range(2):
                    evicted(pe, f"sh2_{t}_{j}")
                    q = open_(f"hT{t}_{j}")
                    for b in range(4):
                        last = turn(q[:, n * b:n * b + n], h2[0:n, t, 512 * j + P * b:512 * j + P * b + P], n)
                    close(last, f"hT{t}_{j}")
                for j in range(2):
                    evicted(pe, f"hT{t}_{j}")
                q = open_(f"lg{t}")
                for k in range(KD):
                    mm(q[0:n, 0:E], h2T[:, k, a:a + n], rw[:, k, :], k == 0, False)
                close(mm(q[0:n, 0:E], c_("ones", n, 1), rb[0:1, :], False, True), f"lg{t}")
            pe.wait_ge(mask_ready, 3)
            for t, (a, n) in enumerate(TILES):
                q = open_(f"rank{t}")
                for s in range(t):
                    mm(q[0:n, 0:E], c_("ones", n), mk[:, s, :], s == 0, False)
                close(mm(q[0:n, 0:E], c_("before", n, n), mk[0:n, t, :], t == 0, True), f"rank{t}")
            q = open_("count")
            for t, (a, n) in enumerate(TILES):
                last = mm(q[:, 0:E], c_("ones", P, n), mk[0:n, t, :], t == 0, t == 2)
            close(last, "count")
            pe.wait_ge(gd_ready, 3)
            for t, (a, n) in enumerate(TILES):
                close(turn(open_(f"gt{t}")[0:E, 0:n], Gd[0:n, t, :], n), f"gt{t}")
            for name in list(unit)[-8:]:
                evicted(pe, name)
            pe.wait_ge(table_ready, 4)
            pe.wait_ge(moe_in, 16)
            qG, qT, qY = ps[:, 0, :], ps[:, 3, :], ps[:, 4, :]
            with pe.Fori(0, E // 2) as pair:
                e = pair * 2
                for s in range(2):
                    first = pe.value_load(cumi[0:1, bass.ds(e + s, 1)], min_val=0, max_val=MAXIT)
                    end = pe.value_load(cumi[0:1, bass.ds(e + (s + 1), 1)], min_val=0, max_val=MAXIT)
                    with pe.Fori(first, end) as it:
                        pe.wait_ge(pick_ready, it * 2 + 2)
                        for d in range(KD):
                            for t, (a, n) in enumerate(TILES):
                                last = mm(qG[:, C * d:C * d + C], h2[0:n, t, P * d:P * d + P], pick[0:n, t, :],
                                          t == 0, t == 2)
                        last.then_inc(gathered, 1)
                        pe.wait_ge(gate_ready, it + 1)
                        pe.wait_ge(lin_ready, it + 1)
                        for x in range(2):
                            for j in range(2):
                                mm(ps[64 * j:64 * j + 64, 1 + x, :], sel_e[0:E, :],
                                   b_gu[0:E, FF * x + 512 * j:FF * x + 512 * j + 512], True, False)
                        pe.wait_ge(hTe_ready, it + 1)
                        for k in range(KD):
                            if k % 2 == 0:
                                pe.wait_ge(gu_in[s][k // 2], e * 8 + 16)
                            for x in range(2):
                                for j in range(2):
                                    last = mm(ps[64 * j:64 * j + 64, 1 + x, :], hTe[:, k, :],
                                              gu[s][:, k, FF * x + 512 * j:FF * x + 512 * j + 512], False, k == KD - 1)
                        last.then_inc(gu_done, 1)
                        pe.wait_ge(act_ready, it + 1)
                        for b in range(4):
                            last = turn(qT[:, P * b:P * b + P], actS[:, P * b:P * b + P])
                        last.then_inc(act_turned, 1)
                        pe.wait_ge(actT_ready, it + 1)
                        pe.wait_ge(y_out, it + 1)
                        for k in range(KD):
                            if k % 4 == 0:
                                pe.wait_ge(dn_in[k // 4], e * 16 + 16 * (s + 1))
                            for j in range(2):
                                last = mm(qY[64 * j:64 * j + 64, :], actT[:, k % 4, C * (k // 4):C * (k // 4) + C],
                                          dn[:, k, 512 * j:512 * j + 512], k == 0, k == KD - 1)
                        last.then_inc(dn_done, 1)
            total = pe.value_load(cumi[0:1, E:E + 1], min_val=0, max_val=MAXIT)
            pe.wait_ge(y_out, total + 1)
            pe.wait_ge(final_in, 16 * 9)
            for t, (a, n) in enumerate(TILES):
                for j in range(2):
                    mm(ps[0:n, 2 * t + j, :], gT[0:E, a:a + n], bdn[0:E, 512 * j:512 * j + 512]).then_inc(bias_ready, 1)

        @block.scalar
        def _(act):
            run = Counted(act, astep)
            f = nc.scalar.activation
            roots = []

            def root(x):
                roots.append(0)
                act.wait_ge(var_ready, len(roots))
                run(f(x, x, ACT.Sqrt), root_ready, wait=False)

            act.wait_ge(params_in, 48)
            run(f(cs, cT, ACT.Sigmoid), csig_ready, wait=False)
            act.wait_ge(x_in, 16)
            for b in range(ZB):
                q = arrived(act, f"z{b}")
                if b < SH:
                    run(nc.scalar.copy(zs[:, b, 1:1 + NPR], q[:, 0:NPR]), wait=False)
                    read(nc.scalar.copy(smp_ext(zs[:, b, 1 + NPR:EXT])[:, :, 1:1 + NT], smp(q[:, NPR:N])), f"z{b}")
                elif b % 2 == 0:
                    read(f(usg[:, (b - SH) // 2, :], q[:, 0:N], ACT.Sigmoid), f"z{b}")
            act.wait_ge(zm_ready, SH)
            run(f(lact[0:64, 0, :], zm[0:64, 12, :], ACT.Tanh), tanh_ready, wait=False)
            run(f(lact[:, 1, :], zm[:, 13, :], ACT.Sigmoid), gsig_ready, wait=False)
            for b in range(CH):
                read(f(sg[:, b, :], arrived(act, f"w{b}")[:, 0:N], ACT.Sigmoid, bias=p_("w0", b)), f"w{b}")
            for b in range(CH):
                read(f(aT[:, b, :], arrived(act, f"a{b}")[:, 0:N], ACT.Sigmoid, bias=p_("a0", b)), f"a{b}")
            for b in range(CH):
                read(nc.scalar.copy(gate[:, b, :], arrived(act, f"g{b}")[:, 0:N]), f"g{b}")
            root(kkn)
            act.wait_ge(cum_ready, 1)
            run(f(EI, cumI, ACT.Exp, scale=-C0), exp_ready, wait=False)
            run(f(EE, EE, ACT.Exp, scale=-C0), exp_ready, wait=False)
            run(f(EN, cumI, ACT.Exp, scale=C0), exp_ready, wait=False)
            for t, (a, n) in enumerate(TILES):
                for i, x in enumerate("bkva"):
                    if i % 2 == 0:
                        read(nc.scalar.copy(tok[x][0:n, t, :], arrived(act, f"{x}tok{t}")[0:n, :]), f"{x}tok{t}")
            for t, (a, n) in enumerate(TILES):
                Nb, NTb = [[at(nbuf[2 * x + y], 2, CH * n) for y in range(2)] for x in range(2)]
                for m in range(1, rounds(t) + 1):
                    for g in range(2):
                        u = f"N{t}_{m}_{g}"
                        read(nc.scalar.copy(Nb[m % 2][0:n, g, :], arrived(act, u)[0:n, 0:CH * n]), u)
                    for g in range(2):
                        if m < rounds(t):
                            u = f"NT{t}_{m}_{g}"
                            read(nc.scalar.copy(NTb[m % 2][0:n, g, :], arrived(act, u)[0:n, 0:CH * n]), u)
                read(nc.scalar.copy(W1[0:n, :], arrived(act, f"W{t}")[0:n, :]), f"W{t}")
                q = arrived(act, f"ZA{t}")
                if t < 2:
                    read(nc.scalar.copy(ZAT, q), f"ZA{t}")
                    for c in range(4):
                        for g in range(2):
                            pr = slice(64 * g, 64 * g + 64)
                            u = f"Y{t}_{c}_{g}"
                            read(nc.scalar.copy(YT[pr, :, a + L * c:a + L * c + L],
                                                arrived(act, u)[pr, 0:CH * L].rearrange("p (b n) -> p b n", b=CH)), u)
                else:
                    read(nc.scalar.copy(ZR[:, :, 0, :], q[:, 0:CH * n].rearrange("p (b n) -> p b n", b=CH)), f"ZA{t}")
                    for g in range(2):
                        pr = slice(64 * g, 64 * g + 64)
                        qv = arrived(act, f"UY{g}")[:, 0:2 * CH * NS].rearrange("p (b a n) -> p b a n", b=CH, a=2)
                        run(nc.scalar.copy(Utr[pr, :, :], qv[pr, :, 0, :]), wait=False)
                        read(nc.scalar.copy(YT[pr, :, NPR:N], qv[pr, :, 1, :]), f"UY{g}")
            for b in range(CH):
                act.wait_ge(yc_ready, b + 1)
                run(f(ysq[:, b, :], YT[:, b, :], ACT.Square), ysq_ready, wait=False)
            root(yrs)
            act.wait_ge(cvc_ready, 1)
            run(f(cvsq, cat[:, CH:2 * CH, :], ACT.Square), cvsq_ready, wait=False)
            root(yrs[:, 0, :])
            for b in range(CH):
                act.wait_ge(cvn_ready, b + 1)
                run(f(cvsg[:, b, :], cat[:, CH + b, :], ACT.Sigmoid), cvsg_ready, wait=False)
            act.wait_ge(tail_in, 16 * 7)
            for t, (a, n) in enumerate(TILES):
                for j in range(2):
                    u = f"g1_{t}_{j}"
                    read(nc.scalar.copy(tA[0:n, t, 512 * j:512 * j + 512], arrived(act, u)[0:n, :]), u)
                root(rstd[0:n, :])
            for t, (a, n) in enumerate(TILES):
                for j in range(2):
                    u = f"g2_{t}_{j}"
                    read(nc.scalar.copy(g2b[0:n, t, 512 * j:512 * j + 512], arrived(act, u)[0:n, :]), u)
                for j in range(2):
                    u = f"hT{t}_{j}"
                    read(nc.scalar.copy(h2T[:, 4 * j:4 * j + 4, a:a + n],
                                        arrived(act, u)[:, 0:4 * n].rearrange("p (b n) -> p b n", b=4)), u)
                act.wait_ge(delta_ready, t + 1)
                run(f(e4[0:n, :], e4[0:n, :], ACT.Exp), e4_ready, wait=False)
            for t, (a, n) in enumerate(TILES):
                read(nc.scalar.copy(gT[0:E, a:a + n], arrived(act, f"gt{t}")[0:E, 0:n]), f"gt{t}")
            nc.scalar.copy(small[:, 315:316], small[:, 313:314]).then_inc(y_out, 1)
            act.wait_ge(table_ready, 4)
            with act.Fori(0, E) as e:
                first = act.value_load(cumi[0:1, bass.ds(e, 1)], min_val=0, max_val=MAXIT)
                end = act.value_load(cumi[0:1, bass.ds(e + 1, 1)], min_val=0, max_val=MAXIT)
                with act.Fori(first, end) as it:
                    act.wait_ge(gathered, it + 1)
                    nc.scalar.copy(hTe, ps[:, 0, :].rearrange("p (k c) -> p k c", k=KD)).then_inc(hTe_ready, 1)
                    act.wait_ge(gate_ready, it + 2)
                    f(sigS, gateS, ACT.Sigmoid, scale=SWI).then_inc(sig_ready, 1)
                    act.wait_ge(dn_done, it + 1)
                    act.wait_ge(y_stored, it * 32 + 32)
                    nc.scalar.copy(yS, ps[:, 4, :]).then_inc(y_out, 1)
                    act.wait_ge(y_out, it + 2)
                    for j in range(2):
                        act.dma_start(y_dram[bass.ds(it * C, C), 512 * j:512 * j + 512],
                                      yS[64 * j:64 * j + 64, :]).then_inc(y_stored, 16)
            for t, (a, n) in enumerate(TILES):
                root(rstd[0:n, :])

        @block.vector
        def _(dve):
            run = Counted(dve, vstep)
            V = nc.vector
            tt, ts, stt = V.tensor_tensor, V.tensor_scalar, V.scalar_tensor_tensor

            def free(ins, name):
                read(ins, name)
                evicted(dve, name)

            def invert_root(x, count=run):
                count(V.memset(small[:, 313:314], 0.0), var_ready, wait=False)
                roots.append(0)
                dve.wait_ge(root_ready, len(roots))
                count(V.reciprocal(x, x))

            roots = []
            run(V.memset(zs[:, :, 0:1], 0.0))
            run(V.memset(gslot, -1.0))
            dve.wait_ge(params_in, 48)
            dve.wait_ge(csig_ready, 1)
            run(tt(cs, cs, cT, ALU.mult), cs_ready)
            run(ts(omk, par[:, PAR["ka"]:PAR["ka"] + CH], -1.0, 1.0, ALU.mult, ALU.add))
            ab = par[:, PAR["adab"]:PAR["adab"] + 16].unsqueeze(2).to_broadcast([P, 16, 9])
            free(tt(modT, arrived(dve, "modT")[:, 0:144].rearrange("p (a b) -> p a b", a=16), ab, ALU.add), "modT")
            run(ts(modT[:, 8:16, :], modT[:, 8:16, :], 1.0, None, ALU.add))
            dve.wait_ge(x_in, 16)
            for k in range(KD):
                run(ts(hT[:, k, 0:NPR], hT[:, k, 0:NPR], modT[:, 8 + k, 0:1], modT[:, k, 0:1], ALU.mult, ALU.add),
                    wait=False)
            for k in range(KD):
                hs = smp(hT[:, k, NPR:N])
                run(tt(hs, hs, modT[:, 8 + k, 1:9].unsqueeze(2).to_broadcast([P, NB, NT]), ALU.mult))
                run(tt(hs, hs, modT[:, k, 1:9].unsqueeze(2).to_broadcast([P, NB, NT]), ALU.add),
                    h_ready if k == KD - 1 else None)
            dve.wait_ge(rows_in, 64)
            for r in range(2):
                q = arrived(dve, f"row{r}")
                for j in range(4):
                    s = slice(32 * j, 32 * j + 9)
                    ins = tt(rows[s, r, :], q[s, :], adab[s, r, :], ALU.add)
                    if j == 3:
                        free(ins, f"row{r}")
                    else:
                        run(ins, wait=False)
            run(V.memset(zero, 0.0), zero_ready, wait=False)
            for j in range(8):
                run(V.memset(small[:, 300 + j:301 + j], 0.0), rows_ready, wait=False)
            dve.wait_ge(states_in, 16 * 6)
            zse = [smp_ext(zs[:, b, 1 + NPR:EXT]) for b in range(SH)]
            for b in range(SH):
                run(V.tensor_copy(zse[b][:, :, 0], shift_in[:, b, :]), wait=(b == SH - 1))
            for b in range(SH):
                evicted(dve, f"z{b}")
                run(tt(dprev[:, 0:NPR], zs[:, b, 0:NPR], zs[:, b, 1:1 + NPR], ALU.subtract), wait=False)
                run(tt(smp(dprev[:, NPR:N]), zse[b][:, :, 0:NT], zse[b][:, :, 1:1 + NT], ALU.subtract))
                run(stt(zm[:, b, 0:NPR], dprev[:, 0:NPR], p_("mu", b), zs[:, b, 1:1 + NPR], ALU.mult, ALU.add), wait=False)
                run(stt(smp(zm[:, b, NPR:N]), smp(dprev[:, NPR:N]), p_("mu", b), zse[b][:, :, 1:1 + NT], ALU.mult,
                        ALU.add), zm_ready)
            run(V.tensor_copy(shift_out[:, :, 0], zs[:, :, NPR]), shift_ready, wait=False)
            zse_all = zs[:, :, 1 + NPR:EXT].rearrange("p c (b t) -> p c b t", b=NB)
            run(V.tensor_copy(shift_out[:, :, 1:9], zse_all[:, :, :, NT]), shift_ready, wait=False)
            for c in range(CH):
                evicted(dve, f"z{SH + 2 * c}")
                u = f"z{SH + 2 * c + 1}"
                q = arrived(dve, u)
                run(tt(ue[:, c, TAPS - 1:PC], q[:, 0:NPR], usg[:, c, 0:NPR], ALU.mult), u_ready)
                us = ue[:, c, PC:UW].rearrange("p (b s) -> p b s", b=NB)
                run(tt(us[:, :, TAPS - 1:SC], smp(q[:, NPR:N]), smp(usg[:, c, NPR:N]), ALU.mult), u_ready)
                read(V.memset(small[:, 310:311], 0.0), u)
            def windows(c, k):
                us = ue[:, c, PC:UW].rearrange("p (b s) -> p b s", b=NB)
                return ((cat[:, CH + c, 0:NPR], ue[:, c, bass.ds(k, NPR)]),
                        (smp(cat[:, CH + c, NPR:N]), us[:, :, bass.ds(k, NT)]))

            for c in range(CH):
                w = PAR["cw"] + c * TAPS
                for y, u in windows(c, 0):
                    ts(y, u, par[:, w:w + 1], p_("cb", c), ALU.mult, ALU.add).then_inc(conv_done, 1)
            with dve.Fori(1, TAPS) as k:
                dve.wait_ge(conv_done, k * 8)
                for c in range(CH):
                    w = PAR["cw"] + c * TAPS
                    for y, u in windows(c, k):
                        stt(y, u, par[:, bass.ds(k + w, 1)], y, ALU.mult, ALU.add).then_inc(conv_done, 1)
            r_, k_, v_ = zm[:, 0:CH, :], zm[:, CH:2 * CH, :], zm[:, 2 * CH:3 * CH, :]
            for b in range(CH):
                run(ts(t1[:, b, :], k_[:, b, :], p_("kk", b), None, ALU.mult))
            run(tt(t2, t1, t1, ALU.mult), sq_ready)
            for b in range(CH):
                u = f"kk{b}"
                free(ts(kkn[:, b, :], arrived(dve, u)[:, 0:N], 1e-24 / HD, None, ALU.max), u)
            invert_root(kkn)
            run(stt(kkn, kkn, 0.125, t1, ALU.mult, ALU.mult))
            for b in range(CH):
                evicted(dve, f"a{b}")
                run(ts(kp[:, b, :], aT[:, b, :], p_("ka", b), omk[:, b:b + 1], ALU.mult, ALU.add))
            run(tt(kp, kp, k_, ALU.mult))
            for b in range(CH):
                run(stt(t2[:, b, :], r_[:, b, :], p_("rk", b), kp[:, b, :], ALU.mult, ALU.mult), rk_ready)
            for b in range(CH):
                evicted(dve, f"w{b}")
                run(V.tensor_tensor_scan(cumI[:, b, :], c_("scan", N), sg[:, b, :], 0.0, ALU.mult, ALU.add))
            run(tt(EE, cumI, sg, ALU.subtract), cum_ready)
            for b in range(CH):
                u = f"rk{b}"
                free(stt(bonus[:, b, :], arrived(dve, u)[:, 0:N], float(HD), v_[:, b, :], ALU.mult, ALU.mult), u)
            run(tt(t1, kkn, aT, ALU.mult))
            dve.wait_ge(exp_ready, 3)
            run(stt(AR[:, :, 0, :], kkn, -1.0, EE, ALU.mult, ALU.mult), wait=False)
            run(tt(AR[:, :, 1, :], r_, EI, ALU.mult), wait=False)
            run(tt(bt, t1, EN, ALU.mult), wait=False)
            evicted(dve, f"g{CH - 1}")
            run(tt(kt, kp, EN, ALU.mult))
            for b in range(CH):
                for x, y in ((bb, bt), (kb, kt)):
                    lp = EI[:, b, L - 1:NPR:L].unsqueeze(2).to_broadcast([P, NPR // L, L])
                    ls = EI[:, b, NPR + NT - 1:N:NT].unsqueeze(2).to_broadcast([P, NB, NT])
                    run(tt(x[:, b, 0:NPR].rearrange("p (c l) -> p c l", l=L),
                           y[:, b, 0:NPR].rearrange("p (c l) -> p c l", l=L), lp, ALU.mult), wait=False)
                    run(tt(smp(x[:, b, NPR:N]), smp(y[:, b, NPR:N]), ls, ALU.mult))
            run(V.memset(ST, 0.0), tilde_ready)
            run(V.memset(STd, 0.0), st_ready)
            for t, (a, n) in enumerate(TILES):
                for i, x in enumerate("bkva"):
                    if i % 2:
                        free(V.tensor_copy(tok[x][0:n, t, :], arrived(dve, f"{x}tok{t}")[0:n, :]), f"{x}tok{t}")
            for t, (a, n) in enumerate(TILES):
                mkt = at(MK0, H, 4 * n)
                tri = c_("tri", 2 * n, n) if t < 2 else c_("tri_s", 2 * n, n)
                low = c_("low", n, n) if t < 2 else c_("low_s", n, n)
                N0 = at(nbuf[0], 2, CH, n)
                TTb = [at(nbuf[4 + y], 2, CH, n) for y in range(2)]
                for h in range(H):
                    u = f"G{t}_{h}"
                    free(tt(mkt[0:n, h, :].rearrange("p (a b) -> p a b", a=2),
                            arrived(dve, u)[0:n, 0:4 * n].rearrange("p (a b) -> p a b", a=2),
                            tri.unsqueeze(1).to_broadcast([n, 2, 2 * n]), ALU.mult), u)
                for g in range(2):
                    u = f"A{t}_{g}"
                    free(tt(N0[0:n, g, :, :], arrived(dve, u)[0:n, 0:CH * n].rearrange("p (b j) -> p b j", b=CH),
                            low.unsqueeze(1).to_broadcast([n, CH, n]), ALU.mult), u)
                for g in range(2):
                    run(tt(TTb[0][0:n, g, :, :], mkt[0:n, g:H:2, 0:n],
                           ident[0:n, 0:n].unsqueeze(1).to_broadcast([n, CH, n]), ALU.add), tt0_ready)
                for m in range(1, rounds(t) + 1):
                    for g in range(2):
                        u = f"TT{t}_{m}_{g}"
                        free(tt(TTb[m % 2][0:n, g, :, :], TTb[(m - 1) % 2][0:n, g, :, :],
                                arrived(dve, u)[0:n, 0:CH * n].rearrange("p (b j) -> p b j", b=CH), ALU.add), u)
                if t == 2:
                    run(V.tensor_copy(ZR[:, :, 1, :], AR[:, :, 1, NPR:N]), zr_ready)
                free(V.tensor_copy(ZV[0:n, :], arrived(dve, f"ZV{t}")[0:n, :]), f"ZV{t}")
                if t < 2:
                    for c in range(4):
                        rq = slice(32 * c, 32 * c + 32)
                        end = a + L * c + L - 1
                        run(tt(STd, ST, EI[:, :, end:end + 1].to_broadcast([P, CH, HD]), ALU.mult))
                        for g in range(2):
                            u = f"U{t}_{c}_{g}"
                            hv = "p (b g v) -> p g b v"
                            free(tt(Ut[rq, :].rearrange(hv, g=2, v=HD)[:, g],
                                    ZV[rq, :].rearrange(hv, g=2, v=HD)[:, g],
                                    arrived(dve, u)[rq, 0:CH * HD].rearrange("p (b v) -> p b v", b=CH), ALU.add), u)
                        u = f"S{t}_{c}"
                        free(tt(ST, STd, arrived(dve, u)[:, 0:CH * HD].rearrange("p (b v) -> p b v", b=CH), ALU.add), u)
                else:
                    free(tt(Ut[0:NS, :], ZV[0:NS, :], arrived(dve, "Us")[0:NS, :], ALU.add), "Us")
                    bm = c_("bmask", NB, NS).unsqueeze(2).to_broadcast([NS, NB, HD])
                    for b in range(CH):
                        if b >= 2:
                            arrived(dve, f"Ss{b - 2}")
                        for i, x in enumerate((Ut[0:NS, :], tok["v"][0:NS, 2, :])):
                            for g in range(2):
                                hs = slice(HD * (2 * b + g), HD * (2 * b + g) + HD)
                                run(tt(masked[b % 2][0:NS, i, g, :].rearrange("p (s v) -> p s v", s=NB),
                                       x[:, hs].unsqueeze(1).to_broadcast([NS, NB, HD]), bm, ALU.mult), um_ready)
                    for b in range(CH):
                        lam = EI[:, b, NPR + NT - 1:N:NT].unsqueeze(2).to_broadcast([P, NB, HD])
                        run(tt(ST0[:, b, :, :], ST0[:, b, :, :], lam, ALU.mult))
                        u = f"Ss{b}"
                        free(tt(ST0[:, b, :, :], ST0[:, b, :, :],
                                arrived(dve, u).rearrange("p (s v) -> p s v", s=NB), ALU.add), u)
                if t < 2:
                    for c in range(4):
                        for g in range(2):
                            evicted(dve, f"Y{t}_{c}_{g}")
                else:
                    for g in range(2):
                        evicted(dve, f"UY{g}")
                free(tt(YT[:, :, a:a + n], YT[:, :, a:a + n],
                        arrived(dve, f"Y{t}")[:, 0:CH * n].rearrange("p (b n) -> p b n", b=CH), ALU.add), f"Y{t}")
            for b in range(CH):
                free(tt(YT[:, b, :], YT[:, b, :], arrived(dve, f"gm{b}")[:, 0:N], ALU.subtract), f"gm{b}")
                run(V.memset(small[:, 311:312], 0.0), yc_ready, wait=False)
            for b in range(CH):
                free(ts(yrs[:, b, :], arrived(dve, f"gv{b}")[:, 0:N], GN_EPS, None, ALU.add), f"gv{b}")
            invert_root(yrs)
            for b in range(CH):
                run(tt(YT[:, b, :], YT[:, b, :], yrs[:, b, :], ALU.mult))
                run(ts(YT[:, b, :], YT[:, b, :], p_("lg", b), p_("lb", b), ALU.mult, ALU.add))
                run(tt(YT[:, b, :], YT[:, b, :], bonus[:, b, :], ALU.add))
                run(tt(cat[:, b, :], YT[:, b, :], gate[:, b, :], ALU.mult), cat_ready)
            dve.wait_ge(conv_done, 2 * CH * TAPS)
            cv = cat[:, CH:2 * CH, :]
            free(tt(cv, cv, arrived(dve, "cm")[:, 0:N].unsqueeze(1).to_broadcast([P, CH, N]), ALU.subtract), "cm")
            run(V.memset(small[:, 312:313], 0.0), cvc_ready, wait=False)
            free(ts(yrs[:, 0, :], arrived(dve, "cv")[:, 0:N], LN_EPS, None, ALU.add), "cv")
            invert_root(yrs[:, 0, :])
            run(tt(cv, cv, yrs[:, 0:1, :].to_broadcast([P, CH, N]), ALU.mult))
            for b in range(CH):
                run(ts(cv[:, b, :], cv[:, b, :], p_("cg", b), p_("cbt", b), ALU.mult, ALU.add), cvn_ready)
            for b in range(CH):
                dve.wait_ge(cvsg_ready, b + 1)
                run(tt(cv[:, b, :], cv[:, b, :], cvsg[:, b, :], ALU.mult), cat_ready)

            def norm(x, n, g, b, step):
                for j in range(2):
                    step(V.bn_stats(stats[0:n, j, :], x[:, 512 * j:512 * j + 512]))
                step(V.bn_aggr(mv[0:n, :], stats[0:n, :, :]))
                step(ts(rstd[0:n, :], mv[0:n, 1:2], LN_EPS, None, ALU.add))
                invert_root(rstd[0:n, :], step)
                step(stt(nmr[0:n, :], mv[0:n, 0:1], -1.0, rstd[0:n, :], ALU.mult, ALU.mult))
                step(ts(x, x, rstd[0:n, :], nmr[0:n, :], ALU.mult, ALU.add))
                step(tt(x, x, g[0:n, :], ALU.mult))
                return tt(x, x, b[0:n, :], ALU.add)

            dve.wait_ge(tail_in, 16 * 7)
            for t, (a, n) in enumerate(TILES):
                for j in range(2):
                    js = slice(512 * j, 512 * j + 512)
                    evicted(dve, f"g1_{t}_{j}")
                    u = f"mix_{t}_{j}"
                    free(tt(tA[0:n, t, js], tA[0:n, t, js], arrived(dve, u)[0:n, :], ALU.mult), u)
                run(stt(xa[0:n, t, :], xin[0:n, t, :], ALPHA, tA[0:n, t, :], ALU.mult, ALU.add))
                run(norm(xa[0:n, t, :], n, lnp[:, 0, :], lnp[:, 1, :], run), x1_ready)
            for t, (a, n) in enumerate(TILES):
                for j in range(2):
                    js = slice(512 * j, 512 * j + 512)
                    u = f"sc2_{t}_{j}"
                    free(stt(h2[0:n, t, js], arrived(dve, u)[0:n, :], 1.0, xa[0:n, t, js], ALU.add, ALU.mult), u)
                for j in range(2):
                    js = slice(512 * j, 512 * j + 512)
                    u = f"sh2_{t}_{j}"
                    free(tt(h2[0:n, t, js], h2[0:n, t, js], arrived(dve, u)[0:n, :], ALU.add), u)
                u = f"lg{t}"
                free(V.tensor_copy(lgt[0:n, t, :], arrived(dve, u)[0:n, 0:E]), u)
                run(V.max(top_v[0:n, :], lgt[0:n, t, :]))
                run(V.max_index(top_i[0:n, t, :], top_v[0:n, :], lgt[0:n, t, :]))
                run(V.tensor_copy(idxf[0:n, :], top_i[0:n, t, :]))
                run(ts(e4[0:n, :], top_v[0:n, 0:4], top_v[0:n, 0:1], None, ALU.subtract), delta_ready)
                o4 = oh[0:n, 4 * t:4 * t + 4, :]
                run(tt(o4, c_("iota32", E, n).unsqueeze(1).to_broadcast([n, 4, E]),
                       idxf[0:n, 0:4].unsqueeze(2).to_broadcast([n, 4, E]), ALU.is_equal))
                run(tt(mk[0:n, t, :], o4[:, 0, :], o4[:, 1, :], ALU.add))
                run(tt(mk[0:n, t, :], mk[0:n, t, :], o4[:, 2, :], ALU.add))
                run(tt(mk[0:n, t, :], mk[0:n, t, :], o4[:, 3, :], ALU.add), mask_ready)
                dve.wait_ge(e4_ready, t + 1)
                run(V.tensor_reduce(esum[0:n, :], e4[0:n, :], AX, ALU.add))
                run(V.reciprocal(esum[0:n, :], esum[0:n, :]))
                run(ts(gates[0:n, t, :], e4[0:n, :], esum[0:n, :], None, ALU.mult))
                run(ts(Gd[0:n, t, :], o4[:, 0, :], gates[0:n, t, 0:1], None, ALU.mult))
                for k in range(1, 4):
                    run(stt(Gd[0:n, t, :], o4[:, k, :], gates[0:n, t, k:k + 1], Gd[0:n, t, :], ALU.mult, ALU.add),
                        gd_ready if k == 3 else None)
            free(V.tensor_copy(cnt, arrived(dve, "count")[:, 0:E]), "count")
            run(ts(npf, cnt, float(C), 1.0, ALU.is_gt, ALU.add))
            for i in range(2, (N - 1) // C + 1):
                run(ts(npt, cnt, float(C * i), None, ALU.is_gt))
                run(tt(npf, npf, npt, ALU.add))
            run(V.memset(cumf[:, 0:1], 0.0))
            run(V.tensor_tensor_scan(cumf[:, 1:E + 1], c_("ones", E), npf, 0.0, ALU.mult, ALU.add))
            for t, (a, n) in enumerate(TILES):
                s = slotv[0:n, 0:E]
                u = f"rank{t}"
                free(stt(s, cumf[0:n, 0:E], float(C), arrived(dve, u)[0:n, 0:E], ALU.mult, ALU.add), u)
                run(stt(gslot[0:n, t, :], s, 1.0, mk[0:n, t, :], ALU.add, ALU.mult))
                run(ts(gslot[0:n, t, :], gslot[0:n, t, :], -1.0, None, ALU.add))
                o4 = ohs[0:n, 4 * t:4 * t + 4, :]
                run(tt(o4, oh[0:n, 4 * t:4 * t + 4, :], s.unsqueeze(1).to_broadcast([n, 4, E]), ALU.mult))
                run(V.tensor_reduce(sidx[0:n, 4 * t:4 * t + 4], o4, AX, ALU.add))
                run(V.tensor_copy(slot_i[0:n, 4 * t:4 * t + 4], sidx[0:n, 4 * t:4 * t + 4]), table_ready)
            run(V.tensor_copy(cumi[:, :], cumf), table_ready)
            slot = c_("slot", C)
            for i, m in enumerate((gate_ready, lin_ready)):
                V.memset(small[:, 316 + i:317 + i], 0.0).then_inc(m, 1)
            with dve.Fori(0, E) as e:
                first = dve.value_load(cumi[0:1, bass.ds(e, 1)], min_val=0, max_val=MAXIT)
                end = dve.value_load(cumi[0:1, bass.ds(e + 1, 1)], min_val=0, max_val=MAXIT)
                with dve.Fori(first, end) as it:
                    ts(slot, slot, float(C), None, ALU.add).then_inc(slot_ready, 1)
                    dve.wait_ge(slot_ready, it + 1)
                    tt(pick, gslot[:, :, bass.ds(e, 1)].to_broadcast([P, 3, C]),
                       slot.unsqueeze(1).to_broadcast([P, 3, C]), ALU.is_equal).then_inc(pick_ready, 1)
                    V.tensor_copy(sel_e[0:E, :], cst[0:E, bass.ds(e + CST["ident"], 1)].to_broadcast([E, C])
                                  ).then_inc(pick_ready, 1)
                    dve.wait_ge(gu_done, it + 1)
                    ts(gateS, ps[:, 1, :], LIMIT, None, ALU.min).then_inc(gate_ready, 1)
                    ts(linS, ps[:, 2, :], LIMIT, -LIMIT, ALU.min, ALU.max).then_inc(lin_ready, 1)
                    dve.wait_ge(sig_ready, it + 1)
                    tt(gateS, gateS, sigS, ALU.mult).then_inc(prod_ready, 1)
                    dve.wait_ge(prod_ready, it + 1)
                    stt(actS, linS, 1.0, gateS, ALU.add, ALU.mult).then_inc(act_ready, 1)
                    dve.wait_ge(act_turned, it + 1)
                    V.tensor_copy(actT, ps[:, 3, :].rearrange("p (b c) -> p b c", b=4)).then_inc(actT_ready, 1)
            fin = Counted(dve, fstep)
            dve.wait_ge(final_in, 16 * 9)
            for t, (a, n) in enumerate(TILES):
                dve.wait_ge(bias_ready, 2 * t + 2)
                dve.wait_ge(rowsg_in[t], 64)
                for k in range(4):
                    for j in range(2):
                        js = slice(512 * j, 512 * j + 512)
                        fin(stt(fr[0:n, t, js], yg[0:n, 4 * t + k, js], gates[0:n, t, k:k + 1],
                                ps[0:n, 2 * t + j, :] if k == 0 else fr[0:n, t, js], ALU.mult, ALU.add))
                fin(tt(fr[0:n, t, :], fr[0:n, t, :], fg[0:n, t, :], ALU.mult))
                fin(stt(fr[0:n, t, :], fx[0:n, t, :], ALPHA, fr[0:n, t, :], ALU.mult, ALU.add))
                fin(norm(fr[0:n, t, :], n, fln[:, 0, :], fln[:, 1, :], fin), out_ready)


def smp_ext(a):
    return a.rearrange("p (b t) -> p b t", b=NB)


def kernel(**inputs):
    import numpy as np
    import concourse.bacc as bacc
    from concourse.bass_utils import run_bass_kernel_spmd

    x = {k: np.asarray(v) for k, v in inputs.items()}
    f = np.float32

    def blocks(v):
        v = v.reshape(v.shape[:-1] + (-1, P))
        return np.moveaxis(v, (-1, -2), (0, 1))

    cst = np.zeros((P, NCST), f)

    def put(name, a):
        cst[0:a.shape[0], CST[name]:CST[name] + a.shape[1]] = a

    i = np.arange(P)
    same = (i[:, None] // L) == (i[None, :] // L)
    put("ident", np.eye(P, dtype=f))
    put("tri", np.concatenate([same & (i[:, None] < i[None, :]), same & (i[:, None] <= i[None, :])], 1).astype(f))
    put("low", (same & (i[:, None] > i[None, :])).astype(f))
    j = np.arange(NS)
    same_s = (j[:, None] // NT) == (j[None, :] // NT)
    put("tri_s", np.concatenate([same_s & (j[:, None] < j[None, :]), same_s & (j[:, None] <= j[None, :])], 1).astype(f))
    put("low_s", (same_s & (j[:, None] > j[None, :])).astype(f))
    reset = np.ones(N, f)
    reset[0:NPR:L] = 0
    reset[NPR:N:NT] = 0
    put("scan", np.tile(reset, (P, 1)))
    put("head", ((i[:, None] // HD) == (i[None, :] // HD)).astype(f) / f(HD))
    put("c512", np.full((P, P), 1.0 / 512, f))
    sel = np.zeros((P, P + NS), f)
    for g in range(4):
        sel[32 * g, 0:P] = 1
        for b in range(NB):
            sel[32 * g + 1 + b, P + NT * b:P + NT * b + NT] = 1
    put("sel", sel)
    put("before", (i[:, None] < i[None, :]).astype(f))
    put("ones", np.ones((P, P), f))
    put("iota32", np.tile(np.arange(E, dtype=f), (P, 1)))
    put("slot", np.tile(np.arange(C, dtype=f) - C, (P, 1)))
    put("bmask", ((j[:, None] // NT) == np.arange(NB)[None, :]).astype(f))

    par = np.concatenate([blocks(x["tm_mu"][0]), blocks(x["w0"][0]), blocks(x["a0"][0]), blocks(x["k_k"][0]),
                          blocks(x["k_a"][0]), blocks(x["r_k"][0].reshape(-1)), blocks(x["lnx_g"][0]),
                          blocks(x["lnx_b"][0]), blocks(x["conv_w"][0]).reshape(P, -1), blocks(x["conv_b"][0]),
                          blocks(x["conv_ln_g"][0]), blocks(x["conv_ln_b"][0]), blocks(x["ada_b"][0][0:2 * D])], 1)
    tokens = np.concatenate([x["x_prompt"].reshape(NPR, D), x["x_sample"].reshape(NS, D)])
    cond = np.concatenate([x["c_prompt"], x["c_sample"]])

    def cols(w, width):
        return w.reshape(KD, P, -1, width).transpose(2, 1, 0, 3)

    win = cols(x["w_in"][0], P)
    order = list(range(SH)) + [b for c in range(CH) for b in (SH + CH + c, SH + c)]
    ada_b = x["ada_b"][0].reshape(12, 512)
    arrays = {
        "cst": cst, "par": par, "cT": blocks(cond), "xT": blocks(tokens), "x": tokens,
        "adab_rows": np.stack([np.tile(ada_b[[4 + g, 8 + g]][None], (9, 1, 1)) for g in range(4)]),
        "ada": cols(x["ada_w"][0], 512), "win": win[order],
        "lora": np.stack([np.concatenate([x["w2"][0], x["a2"][0]]), x["g2"][0]], 1),
        "shiftT": blocks(x["state_shift"][0]),
        "conv0": np.zeros((P, CH, TAPS - 1), f),
        "convs": blocks(x["state_conv"][0]),
        "w_out": x["w_out"][0].reshape(KD, P, D).transpose(1, 0, 2),
        "wkvT": x["state_wkv"][0].reshape(NB, CH, 2, HD, HD).transpose(2, 4, 1, 0, 3).reshape(P, CH, NB, HD),
        "ln": np.stack([x["ln1_g"][0], x["ln1_b"][0], x["ln2_g"][0], x["ln2_b"][0]]),
        "rw": x["router_w"][0].reshape(KD, P, E).transpose(1, 0, 2), "rb": x["router_b"],
        "w_gu": x["w_gu"][0], "b_gu": x["b_gu"][0], "w_dn": x["w_dn"][0], "b_dn": x["b_dn"][0],
    }
    outs = {"y": (N, D), "wkv_p": (P, CH, HD), "wkv_s": (P, CH, NB, HD), "shift_out": (P, SH, 9),
            "conv_p": (P, CH, TAPS - 1), "conv_s": (P, CH, NB, TAPS - 1)}
    nc = bacc.Bacc("TRN2", target_bir_lowering=False, num_devices=1)
    arrays = {f"in_{k}": np.ascontiguousarray(v) for k, v in arrays.items()}
    io = {k[3:]: nc.dram_tensor(k, v.shape, mybir.dt.from_np(v.dtype), kind="ExternalInput").ap()
          for k, v in arrays.items()}
    for k, shape in outs.items():
        io[k] = nc.dram_tensor(f"out_{k}", shape, F32, kind="ExternalOutput").ap()
    build(nc, io)
    r = run_bass_kernel_spmd(nc, [arrays], core_ids=[0]).results[0]
    r = {k: np.asarray(r[f"out_{k}"]) for k in outs}
    y = r["y"]
    wkv_p = r["wkv_p"].reshape(2, HD, CH, HD).transpose(2, 0, 3, 1).reshape(1, 1, H, HD, HD)
    wkv_s = r["wkv_s"].reshape(2, HD, CH, NB, HD).transpose(3, 2, 0, 4, 1).reshape(1, NB, H, HD, HD)
    shift = r["shift_out"].transpose(2, 1, 0).reshape(9, SH * P)
    conv_p = r["conv_p"].transpose(2, 1, 0).reshape(1, 1, TAPS - 1, CH * P)
    conv_s = r["conv_s"].transpose(2, 3, 1, 0).reshape(1, NB, TAPS - 1, CH * P)
    c = np.ascontiguousarray
    return (c(y[0:NPR].reshape(1, NPR, D)), c(y[NPR:N].reshape(NB, NT, D)), c(wkv_p), c(wkv_s),
            c(shift[0:1].reshape(1, 1, -1)), c(shift[1:9].reshape(1, NB, -1)), c(conv_p), c(conv_s))
```

```python
from contextlib import ExitStack

import concourse.bass as bass
from concourse import mybir

F32 = mybir.dt.float32
I32 = mybir.dt.int32
U32 = mybir.dt.uint32
ALU = mybir.AluOpType
ACT = mybir.ActivationFunctionType
AX = mybir.AxisListType.X

P = 128
D = 1024
KD = D // P
NPR = 256
NB, NT = 8, 4
NS = NB * NT
N = NPR + NS
TILES = [(0, P), (P, P), (NPR, NS)]
H, HD = 8, 64
CH = 4
SH = 14
ZB = 22
EXT = 1 + NPR + NB * (1 + NT)
TAPS = 31
PC = TAPS - 1 + NPR
SC = TAPS - 1 + NT
UW = PC + NB * SC
L = 32
E = 32
FF = D
C = 64
MAXIT = E + (N * 4) // (C + 1)
END_BANKS = [0, 3, 4, 5, 6, 7]
ALPHA = 2.0 ** 0.25
C0 = 0.6065306597126334
WB = 6
NORM_STEPS = [("stats", 0), ("stats", 1), ("factors", 0), ("stats", 2), ("factors", 1), ("out", 0), ("factors", 2),
              ("out", 1), ("out", 2)]
LN_EPS, GN_EPS = 1e-5, 64e-5
LIMIT, SWI = 7.0, 1.702


def columns(*widths):
    at, table = 0, {}
    for name, width in widths:
        table[name] = at
        at += width
    return table, at


PAR, NPAR = columns(("mu", SH), ("w0", CH), ("a0", CH), ("kk", CH), ("ka", CH), ("rk", CH), ("lg", CH), ("lb", CH),
                    ("cw", CH * TAPS), ("cb", CH), ("cg", CH), ("cbt", CH), ("adab", 2 * KD))
CST, NCST = columns(("ident", P), ("tri", 2 * P), ("low", P), ("tri_s", 2 * NS), ("low_s", NS), ("scan", N),
                    ("head", P), ("c512", P), ("sel", P + NS), ("before", P), ("ones", P), 
                    ("slot", C), ("bmask", NB), ("item", MAXIT + 1))


def rounds(t):
    return 4 if t < 2 else 1


def psum_units():
    names = ["first"] + [f"modT{j}" for j in range(4)] + [f"z{b}" for b in range(ZB)]
    names += [f"{x}{b}" for x in "wag" for b in range(CH)] + [f"kk{b}" for b in range(CH)] + ["row0"]
    names += [f"rk{b}" for b in range(CH)] + ["row1"]
    names += [f"{x}tok{t}" for t in range(3) for x in "bkva"]
    for t in range(3):
        names += [f"G{t}_{h}" for h in range(H)] + [f"A{t}_{g}" for g in range(2)]
        for m in range(1, rounds(t) + 1):
            names += [f"N{t}_{m}_{g}" for g in range(2)]
            if m < rounds(t):
                names += [f"NT{t}_{m}_{g}" for g in range(2)]
            names += [f"TT{t}_{m}_{g}" for g in range(2)]
        names += [f"W{t}", f"ZA{t}", f"ZV{t}"]
        if t < 2:
            for q in range(4):
                names += [f"U{t}_{q}_0", f"U{t}_{q}_1", f"Y{t}_{q}_0", f"Y{t}_{q}_1", f"S{t}_{q}"]
        else:
            names += ["UY0", "UY1", "Us"] + [f"Ss{b}" for b in range(CH)]
        names += [f"Y{t}"]
    names += [f"gm{b}" for b in range(CH)] + ["cm"] + [f"gv{b}" for b in range(CH)] + ["cv"]
    for t in range(3):
        names += [f"{x}_{t}_{j}" for x in ("g1", "mix") for j in range(2)]
    for t in range(3):
        names += [f"{x}_{t}_{j}" for x in ("sc2", "sh2") for j in range(2)]
        names += [f"hT{t}_{j}" for j in range(2)] + [f"lg{t}"]
    names += ["rank0", "rank1", "rank2", "count", "gt0", "gt1", "gt2"]
    return {n: (i % 8, i // 8) for i, n in enumerate(names)}


class Counted:

    def __init__(self, eng, step):
        self.eng, self.step, self.n = eng, step, {}

    def __call__(self, ins, sem=None, wait=True):
        sem = self.step if sem is None else sem
        self.n[sem.name] = self.n.get(sem.name, 0) + 1
        ins.then_inc(sem, 1)
        if wait:
            self.eng.wait_ge(sem, self.n[sem.name])


def build(nc, io):
    unit = psum_units()
    with ExitStack() as ctx:
        def sem(name):
            return ctx.enter_context(nc.semaphore(name))

        arena = ctx.enter_context(nc.sbuf_tensor("arena", [P, 53000], F32))
        cumi = ctx.enter_context(nc.sbuf_tensor("cumi", [P, E + 1], I32))
        item_i = ctx.enter_context(nc.sbuf_tensor("item_i", [P, MAXIT + 1], I32))
        top_i = ctx.enter_context(nc.sbuf_tensor("top_i", [P, 3, 8], U32))
        slot_i = ctx.enter_context(nc.sbuf_tensor("slot_i", [P, 12], U32))
        ps = ctx.enter_context(nc.psum_tensor("ps", [P, 8, 512], F32))
        y_dram = nc.dram_tensor("y_slots", (MAXIT * C, D), F32, kind="Internal").ap()
        res_dram = nc.dram_tensor("residual", (3, P, D), F32, kind="Internal").ap()
        gate2_dram = nc.dram_tensor("gate2_rows", (9, 2, 512), F32, kind="Internal").ap()

        def at(off, *shape):
            n = 1
            for s in shape:
                n *= s
            a = arena[:, off:off + n]
            if len(shape) == 2:
                a = a.rearrange("p (a b) -> p a b", a=shape[0])
            if len(shape) == 3:
                a = a.rearrange("p (a b c) -> p a b c", a=shape[0], b=shape[1])
            return a

        W = CH * N
        gu = [at(16384, KD, 2 * FF), at(0, KD, 2 * FF)]
        dn = at(32768, KD, D)
        o = 40960
        par = at(o, NPAR)
        o += NPAR
        cst = at(o, NCST)
        o += NCST
        h2 = at(o, 3, D)
        o += 3 * D
        gslot = at(o, 3, E)
        o += 3 * E
        gates = at(o, 3, 4)
        o += 12
        gT = at(o, N)
        o += N
        small = at(o, 400)
        o += 400
        moe0 = o
        b_gu = at(o, 2 * FF)
        o += 2 * FF
        hTe = at(o, 4, P)
        o += 4 * P
        pick = at(o, 3, C)
        o += 3 * C
        sel_e = at(o, C)
        o += C
        gateS, sigS, linS, actS, yS = [at(o + 512 * i, 512) for i in range(5)]
        actT = at(o + 2560, 4, P)
        gS = at(40960 + NPAR + CST["tri"], 512)
        item_m, item_f = at(o, MAXIT + 1, E), at(o + 2048, MAXIT + 1)
        assert o + 3072 <= 53000
        hT = at(0, KD, N)
        zs = at(2304, SH, EXT)
        zm = at(6462, SH, N)
        ue = at(10560, CH, UW)
        cat = at(12800, KD, N)
        rows = at(15104, 2, 512)
        adab = at(16128, 2, 512)
        aT, gate, kp, EI, bonus, bt, kt = [at(17152 + i * W, CH, N) for i in range(7)]
        usg, lact, YT, ysq, yrs = bonus, kt, kp, bt, kt
        AR = at(25216, CH, 2, N)
        bb, kb, t1, t2 = [at(27520 + i * W, CH, N) for i in range(4)]
        cvsq, cvsg = at(25216, CH, N), at(25216 + W, CH, N)
        sg, kkn, cumI, EE, EN = [at(i * W, CH, N) for i in range(5)]
        tok = {x: at(i * 1536, 3, 512) for i, x in enumerate("bkva")}
        W1, ZV, Ut, ZAT = [at(6462 + i * 512, 512) for i in range(4)]
        ZR, Utr = at(6462 + 1536, CH, 2, NS), at(6462 + 1792, CH, NS)
        ST0 = at(8510, CH, NB, HD)
        MK0 = 27520
        nbuf = [moe0 + i * 1024 for i in range(6)]
        masked = [at(MK0 + 1024, 2, 2, NB * HD), at(moe0, 2, 2, NB * HD)]
        dprev = at(32128, N)
        cs, cT, modT = at(32416, KD, 9), at(32488, KD, 9), at(32560, 16, 9)
        ST, STd = at(16128, CH, HD), at(16384, CH, HD)
        zero = h2[:, 2, 0:512]
        cvp = h2[:, 0:2, :].rearrange("p a b -> p (a b)")[:, 0:W].rearrange("p (c n) -> p c n", c=CH)
        ada_buf = [at(32768 + i * 4096, KD, 512) for i in range(2)]
        win_buf = [at(25216 + i * 1024, KD, P) for i in range(WB)]
        w_out = at(32768, KD, D)
        lora = at(moe0 + 512, 2, 512)
        shift_in = at(moe0, SH, NB)
        shift_out = at(moe0 + 6144, SH, 9)
        cvr = at(MK0, N)
        omk = small[:, 0:CH]
        xin, lnp, xa, tA = at(0, 3, D), at(3072, 2, D), at(5120, 3, D), at(8192, 3, D)
        oh, mk, lgt, Gd, ohs = at(11264, 12, E), at(11648, 3, E), at(11744, 3, E), at(11840, 3, E), at(moe0 + 2 * FF, 12, E)
        rw, rb, h2T = at(12288, KD, E), at(12544, E), at(moe0, KD, N)
        stats = small[:, 320:356].rearrange("p (t a b) -> p t a b", t=3, a=2)
        mv, rstd, nmr = small[:, 356:362].rearrange("p (t a) -> p t a", t=3), small[:, 362:365], small[:, 365:368]
        top_v, idxf, e4, esum = small[:, 20:28], small[:, 28:36], small[:, 36:40], small[:, 40:41]
        cnt, npf, npt, cumf = small[:, 48:80], small[:, 80:112], small[:, 112:144], small[:, 144:177]
        sidx, slotv = small[:, 180:192], small[:, 192:288]
        yg, fr = at(0, 12, D), at(12288, 3, D)
        fx, fg, fln, bdn, g2r = at(16384, 3, D), at(19456, 3, D), at(22528, 2, D), at(24576, D), at(25600, 2, 512)
        dgate = at(26624, 12, P)

        def c_(name, w, n=P, p0=0):
            return cst[p0:p0 + n, CST[name]:CST[name] + w]

        def p_(name, i):
            return par[:, PAR[name] + i:PAR[name] + i + 1]

        ident = c_("ident", P)

        def smp(a):
            return a.rearrange("p (b t) -> p b t", b=NB)

        filled = [sem(f"bank{b}_filled") for b in range(8)]
        emptied = [sem(f"bank{b}_emptied") for b in range(8)]
        (cond_in, sum_ready, norm_ready, normed, gate2_ready, gate2_read, dgate_ready, prod_done, router_in, zero_ready, ring_free, var_ready, root_ready, params_in, x_in, rows_in, ada_used, states_in, lora_in, wkv_in, wout_in, tail_in, moe_in, csig_ready, cs_ready,
         h_ready, zm_ready, tanh_ready, gsig_ready, u_ready, sq_ready, rk_ready, cum_ready, exp_ready, tilde_ready,
         st_ready, tt0_ready, zr_ready, um_ready, conv_done, ysq_ready, yc_ready, cvc_ready, cvsq_ready, cvn_ready,
         cvsg_ready, cat_ready, x1_ready, h2_ready, delta_ready, e4_ready, mask_ready, gd_ready, shift_ready,
         table_ready, stored, spilled, vstep, astep) = [sem(n) for n in (
             "cond_in sum_ready norm_ready normed gate2_ready gate2_read dgate_ready conv_products router_in zero_ready ring_free var_ready root_ready params_in x_in rows_in ada_used states_in lora_in wkv_in wout_in tail_in moe_in csig_ready cs_ready "
             "h_ready zm_ready tanh_ready gsig_ready u_ready sq_ready rk_ready cum_ready exp_ready tilde_ready "
             "st_ready tt0_ready zr_ready um_ready conv_done ysq_ready yc_ready cvc_ready cvsq_ready cvn_ready "
             "cvsg_ready cat_ready x1_ready h2_ready delta_ready e4_ready mask_ready gd_ready shift_ready "
             "table_ready stored spilled vector_step scalar_step").split()]
        ada_in = [sem(f"ada_in{i}") for i in range(2)]
        win_in = [sem(f"win_in{i}") for i in range(WB)]
        gu_in = [[sem(f"gu{s}_in{c}") for c in range(4)] for s in range(2)]
        dn_in = [sem(f"dn_in{c}") for c in range(2)]
        (slot_ready, pick_ready, sel_ready, gathered, rows_read, tokens_turned, hTe_ready, gu_done, gate_ready, lin_ready, sig_ready, prod_ready, act_ready,
         act_turned, actT_ready, dn_done, y_out, y_stored, final_in, bias_ready, out_ready, fstep) = [
             sem(n) for n in ("slot_ready pick_ready sel_ready gathered rows_read tokens_turned hTe_ready gu_done gate_ready lin_ready sig_ready "
                              "prod_ready act_ready act_turned actT_ready dn_done y_out y_stored final_in bias_ready "
                              "out_ready final_step").split()]
        rowsg_in = [sem(f"rows_gathered{t}") for t in range(3)]

        def evicted(eng, name):
            b, i = unit[name]
            eng.wait_ge(emptied[b], i + 1)

        def arrived(eng, name):
            b, i = unit[name]
            eng.wait_ge(filled[b], i + 1)
            return ps[:, b, :]

        def read(ins, name):
            ins.then_inc(emptied[unit[name][0]], 1)
            return name

        block = ctx.enter_context(nc.Block())

        @block.sync
        def _(sp):
            sp.dma_start(cT, io["cT"]).then_inc(cond_in, 16)

            def load_ada(n):
                if n >= 2:
                    if n - 2 in (3, 7):
                        arrived(sp, {3: "first", 7: "row0"}[n - 2])
                    else:
                        sp.wait_ge(ada_used, n - 1 - (n > 5) - (n > 9))
                sp.dma_start(ada_buf[n % 2], io["ada"][n]).then_inc(ada_in[n % 2], 16)

            for n in range(2):
                load_ada(n)
            sp.dma_start(cst, io["cst"]).then_inc(params_in, 16)
            sp.dma_start(par, io["par"]).then_inc(params_in, 16)
            sp.dma_start(hT, io["xT"]).then_inc(x_in, 16)
            for n in range(2, 4):
                load_ada(n)
            for b in range(ZB):
                if b >= WB:
                    arrived(sp, f"z{b - WB}")
                sp.dma_start(win_buf[b % WB], io["win"][b]).then_inc(win_in[b % WB], 16)
                if b == WB - 1:
                    load_ada(4)
                    load_ada(5)
                    sp.dma_start(lora, io["lora"]).then_inc(lora_in, 16)
                    sp.dma_start(shift_in, io["shiftT"]).then_inc(states_in, 16)
                    sp.dma_start(ue[:, :, 0:TAPS - 1], io["conv0"]).then_inc(states_in, 16)
                    for c in range(CH):
                        sp.dma_start(ue[:, c, PC:UW].rearrange("p (b s) -> p b s", b=NB)[:, :, 0:TAPS - 1],
                                     io["convs"][:, c, :, :]).then_inc(states_in, 16)
            for j in range(4):
                sp.dma_start(adab[32 * j:32 * j + 9, :, :], io["adab_rows"][j]).then_inc(rows_in, 16)
            sp.wait_ge(zero_ready, 1)
            for j in range(2):
                sp.dma_start(y_dram[E * C:MAXIT * C, 512 * j:512 * j + 512].rearrange("(p a) n -> p a n", p=64),
                             zero[0:64, :].unsqueeze(1).to_broadcast([64, MAXIT - E, 512])).then_inc(y_stored, 16)
            sp.wait_ge(shift_ready, 2)
            sp.dma_start(io["shift_out"], shift_out).then_inc(stored, 16)
            sp.wait_ge(u_ready, 2 * CH)
            sp.dma_start(io["conv_p"], ue[:, :, NPR:PC]).then_inc(stored, 16)
            for c in range(CH):
                sp.dma_start(io["conv_s"][:, c, :, :],
                             ue[:, c, PC:UW].rearrange("p (b s) -> p b s", b=NB)[:, :, NT:SC]).then_inc(stored, 16)
            for n in range(6, 12):
                load_ada(n)
            arrived(sp, "row1")
            sp.dma_start(w_out, io["w_out"]).then_inc(wout_in, 16)
            evicted(sp, "row1")
            for j in range(2):
                sp.dma_start(gate2_dram[:, j, :], rows[32 * (2 + j):32 * (2 + j) + 9, 1, :]).then_inc(spilled, 16)
            evicted(sp, "vtok2")
            sp.dma_start(ST0, io["wkvT"]).then_inc(wkv_in, 16)
            evicted(sp, "S1_3")
            sp.dma_start(io["wkv_p"], ST).then_inc(stored, 16)
            for b in range(CH):
                evicted(sp, f"Ss{b}")
            sp.dma_start(io["wkv_s"], ST0).then_inc(stored, 16)
            sp.wait_ge(cat_ready, 2 * CH)
            sp.wait_ge(stored, 16 * 8)
            for t, (a, n) in enumerate(TILES):
                sp.dma_start(xin[0:n, t, :], io["x"][a:a + n, :]).then_inc(tail_in, 16)
            for i in range(2):
                sp.dma_start(lnp[:, i, :], io["ln"][i:i + 1, :].to_broadcast([P, D])).then_inc(tail_in, 16)
            sp.dma_start(rw, io["rw"]).then_inc(tail_in, 16)
            sp.dma_start(rb[0:1, :], io["rb"]).then_inc(tail_in, 16)
            wg, wd = io["w_gu"], io["w_dn"]

            def load_gu(s, e, chunks=range(4)):
                for c in chunks:
                    sp.dma_start(gu[s][:, 2 * c:2 * c + 2, :],
                                 wg[bass.ds(e, 1), 256 * c:256 * c + 256, :].rearrange("e (k p) n -> p (e k) n", p=P)
                                 ).then_inc(gu_in[s][c], 16)

            def load_dn(e):
                for c in range(2):
                    sp.dma_start(dn[:, 4 * c:4 * c + 4, :],
                                 wd[bass.ds(e, 1), 512 * c:512 * c + 512, :].rearrange("e (k p) n -> p (e k) n", p=P)
                                 ).then_inc(dn_in[c], 16)

            load_gu(0, 0)
            arrived(sp, "mix_2_1")
            load_dn(0)
            for t, (a, n) in enumerate(TILES):
                sp.wait_ge(x1_ready, t + 1)
                sp.dma_start(res_dram[t, 0:n, :], xa[0:n, t, :]).then_inc(spilled, 16)
            arrived(sp, "lg2")
            sp.dma_start(b_gu[0:E, :], io["b_gu"]).then_inc(moe_in, 16)
            sp.wait_ge(spilled, 16 * 5)
            load_gu(1, 1, (0, 1, 3))
            sp.wait_ge(table_ready, 5)
            for n in ("gt0", "gt1", "gt2"):
                arrived(sp, n)
            load_gu(1, 1, (2,))
            items = sp.value_load(cumi[0:1, 1:2], min_val=0, max_val=MAXIT)
            sp.wait_ge(dn_done, items)
            load_dn(1)
            with sp.Fori(1, E // 2) as pair:
                e = pair * 2
                for s in range(2):
                    through = sp.value_load(cumi[0:1, bass.ds(e + (s - 1), 1)], min_val=0, max_val=MAXIT)
                    sp.wait_ge(gu_done, through)
                    load_gu(s, e + s)
                    through = sp.value_load(cumi[0:1, bass.ds(e + s, 1)], min_val=0, max_val=MAXIT)
                    sp.wait_ge(dn_done, through)
                    load_dn(e + s)
            through = sp.value_load(cumi[0:1, E - 1:E], min_val=0, max_val=MAXIT)
            sp.wait_ge(gu_done, through)
            for t, (a, n) in enumerate(TILES):
                sp.dma_start(fx[0:n, t, :], res_dram[t, 0:n, :]).then_inc(final_in, 16)
            sp.dma_start(g2r[0:9, :, :], gate2_dram).then_inc(final_in, 16)
            for i in range(2):
                sp.dma_start(fln[:, i, :], io["ln"][2 + i:3 + i, :].to_broadcast([P, D])).then_inc(final_in, 16)
            sp.dma_start(bdn[0:E, :], io["b_dn"]).then_inc(final_in, 16)
            for t, (a, n) in enumerate(TILES):
                sp.wait_ge(out_ready, t + 1)
                sp.dma_start(io["y"][a:a + n, :], fr[0:n, t, :]).then_inc(stored, 16)
            sp.wait_ge(stored, 16 * 11)

        @block.gpsimd
        def _(pool):
            taps = par[:, PAR["cw"]:PAR["cw"] + CH * TAPS].rearrange("p (c k) -> p c k", c=CH)
            ptt = nc.gpsimd.tensor_tensor
            y = cat[:, CH:2 * CH, :]

            def windows(k):
                yield (cvp[:, :, 0:NPR], ue[:, :, bass.ds(k, NPR)],
                       taps[:, :, bass.ds(k, 1)].to_broadcast([P, CH, NPR]))
                for c in range(CH):
                    us = ue[:, c, PC:UW].rearrange("p (b s) -> p b s", b=NB)
                    yield (smp(cvp[:, c, NPR:N]), us[:, :, bass.ds(k, NT)],
                           taps[:, c, bass.ds(k, 1)].unsqueeze(2).to_broadcast([P, NB, NT]))

            pool.wait_ge(params_in, 32)
            pool.wait_ge(states_in, 16 * 6)
            pool.wait_ge(u_ready, 2 * CH)
            nc.gpsimd.tensor_copy(y, par[:, PAR["cb"]:PAR["cb"] + CH].unsqueeze(2).to_broadcast([P, CH, N])
                                  ).then_inc(conv_done, 1)
            with pool.Fori(0, TAPS) as k:
                for p, u, w in windows(k):
                    ptt(p, u, w, ALU.mult).then_inc(prod_done, 1)
                pool.wait_ge(prod_done, k * (1 + CH) + 1 + CH)
                pool.wait_ge(conv_done, k + 1)
                ptt(y, y, cvp, ALU.add).then_inc(conv_done, 1)
                pool.wait_ge(conv_done, k + 2)
            pool.wait_ge(table_ready, 5)
            total = pool.value_load(cumi[0:1, E:E + 1], min_val=0, max_val=MAXIT)
            mark = small[:, 314:315]
            nc.gpsimd.memset(mark, 0.0).then_inc(ring_free, 1)
            pool.wait_ge(ring_free, 1)
            pool.wait_ge(dn_done, total)
            nc.gpsimd.tensor_tensor(mark, mark, mark, ALU.add).then_inc(ring_free, 1)
            pool.wait_ge(ring_free, 2)
            pool.wait_ge(y_stored, total * 32 + 32)
            nc.gpsimd.tensor_tensor(mark, mark, mark, ALU.add).then_inc(ring_free, 1)
            pool.wait_ge(ring_free, 3)
            for t, (a, n) in enumerate(TILES):
                for k in range(4):
                    pool.indirect_dma_start(
                        out=yg[0:n, 4 * t + k, :], out_offset=None, in_=y_dram[:, :],
                        in_offset=bass.IndirectOffsetOnAxis(ap=slot_i[0:n, 4 * t + k:4 * t + k + 1], axis=0),
                    ).then_inc(rowsg_in[t], 16)

        @block.tensor
        def _(pe):
            def open_(name):
                b, i = unit[name]
                if i:
                    pe.wait_ge(emptied[b], i)
                return ps[:, b, :]

            def close(ins, name):
                ins.then_inc(filled[unit[name][0]], 1)

            def mm(out, lhsT, rhs, first=True, last=True):
                return nc.tensor.matmul(out, lhsT, rhs, start=first, stop=last)

            def turn(out, src, n=P):
                return nc.tensor.transpose(out, src, ident[0:n, 0:n])

            pe.wait_ge(cs_ready, 1)
            q = open_("first")
            for n in range(4):
                pe.wait_ge(ada_in[n % 2], 16 * (n // 2 + 1))
                for k in range(KD):
                    for j in range(4):
                        last = mm(q[32 * j:32 * j + 9, P * n:P * n + P], cs[:, k, :],
                                  ada_buf[n % 2][:, k, P * j:P * j + P], k == 0, k == KD - 1)
                if n == 3:
                    close(last, "first")
                else:
                    last.then_inc(ada_used, 1)
            pe.wait_ge(params_in, 32)
            evicted(pe, "first")
            for j in range(4):
                q = open_(f"modT{j}")
                s = slice(32 * j, 32 * j + 9)
                for n in range(4):
                    last = nc.tensor.transpose(q[:, 9 * n:9 * n + 9], rows[s, 0, P * n:P * n + P], ident[s, s])
                close(last, f"modT{j}")

            def condition_rows(r):
                q = open_(f"row{r}")
                for j in range(4):
                    n = 4 + 4 * r + j
                    pe.wait_ge(ada_in[n % 2], 16 * (n // 2 + 1))
                    for k in range(KD):
                        last = mm(q[32 * j:32 * j + 9, :], cs[:, k, :], ada_buf[n % 2][:, k, :], k == 0, k == KD - 1)
                    if j == 3:
                        close(last, f"row{r}")
                    else:
                        last.then_inc(ada_used, 1)

            pe.wait_ge(h_ready, 1)
            for b in range(ZB):
                q = open_(f"z{b}")
                pe.wait_ge(win_in[b % WB], 16 * (b // WB + 1))
                for k in range(KD):
                    last = mm(q[:, 0:N], win_buf[b % WB][:, k, :], hT[:, k, :], k == 0, k == KD - 1)
                close(last, f"z{b}")
            pe.wait_ge(lora_in, 16)
            pe.wait_ge(tanh_ready, 1)
            for b in range(CH):
                close(mm(open_(f"w{b}")[:, 0:N], lora[0:64, 0, P * b:P * b + P], lact[0:64, 0, :]), f"w{b}")
            for b in range(CH):
                close(mm(open_(f"a{b}")[:, 0:N], lora[64:128, 0, P * b:P * b + P], zm[64:128, 12, :]), f"a{b}")
            pe.wait_ge(gsig_ready, 1)
            for b in range(CH):
                close(mm(open_(f"g{b}")[:, 0:N], lora[:, 1, P * b:P * b + P], lact[:, 1, :]), f"g{b}")
            head = c_("head", P)
            pe.wait_ge(sq_ready, 1)
            for b in range(CH):
                close(mm(open_(f"kk{b}")[:, 0:N], head, t2[:, b, :]), f"kk{b}")
            condition_rows(0)
            pe.wait_ge(rk_ready, CH)
            for b in range(CH):
                close(mm(open_(f"rk{b}")[:, 0:N], head, t2[:, b, :]), f"rk{b}")
            condition_rows(1)
            pe.wait_ge(tilde_ready, 1)
            src = {"b": bb, "k": kb, "v": zm[:, 2 * CH:3 * CH, :], "a": AR[:, :, 0, :]}
            for t, (a, n) in enumerate(TILES):
                for x in "bkva":
                    q = open_(f"{x}tok{t}")
                    for b in range(CH):
                        last = turn(q[0:n, P * b:P * b + P], src[x][:, b, a:a + n])
                    close(last, f"{x}tok{t}")
            for x in "bkva":
                evicted(pe, f"{x}tok2")
            for t, (a, n) in enumerate(TILES):
                mkt = at(MK0, H, 4 * n)
                Nb, NTb, TTb = [[at(nbuf[2 * x + y], 2, CH, n) for y in range(2)] for x in range(3)]
                for h in range(H):
                    g, b = h % 2, h // 2
                    pr = slice(64 * g, 64 * g + 64)
                    q = open_(f"G{t}_{h}")
                    for i, x in enumerate((bt, kt)):
                        last = mm(q[0:n, 2 * n * i:2 * n * (i + 1)].rearrange("p (a b) -> p a b", a=2),
                                  x[pr, b, a:a + n], AR[pr, b, :, a:a + n])
                    close(last, f"G{t}_{h}")
                for g in range(2):
                    pr = slice(64 * g, 64 * g + 64)
                    q = open_(f"A{t}_{g}")
                    for b in range(CH):
                        last = mm(q[0:n, n * b:n * b + n], AR[pr, b, 0, a:a + n], bt[pr, b, a:a + n])
                    close(last, f"A{t}_{g}")
                for h in range(H):
                    evicted(pe, f"G{t}_{h}")
                for m in range(1, rounds(t) + 1):
                    for g in range(2):
                        evicted(pe, f"A{t}_{g}" if m == 1 else f"N{t}_{m - 1}_{g}")
                        if m > 1:
                            evicted(pe, f"NT{t}_{m - 1}_{g}")
                        q = open_(f"N{t}_{m}_{g}")
                        for b in range(CH):
                            NTp = mkt[0:n, 2 * b + g, 0:n] if m == 1 else NTb[(m - 1) % 2][0:n, g, b, :]
                            last = mm(q[0:n, n * b:n * b + n], NTp, Nb[(m - 1) % 2][0:n, g, b, :])
                        close(last, f"N{t}_{m}_{g}")
                    for g in range(2):
                        if m == rounds(t):
                            break
                        q = open_(f"NT{t}_{m}_{g}")
                        for b in range(CH):
                            NTp = mkt[0:n, 2 * b + g, 0:n] if m == 1 else NTb[(m - 1) % 2][0:n, g, b, :]
                            last = mm(q[0:n, n * b:n * b + n], Nb[(m - 1) % 2][0:n, g, b, :], NTp)
                        close(last, f"NT{t}_{m}_{g}")
                    for g in range(2):
                        evicted(pe, f"N{t}_{m}_{g}")
                        if m == 1:
                            pe.wait_ge(tt0_ready, 2 * t + g + 1)
                        else:
                            evicted(pe, f"TT{t}_{m - 1}_{g}")
                        q = open_(f"TT{t}_{m}_{g}")
                        for b in range(CH):
                            last = mm(q[0:n, n * b:n * b + n], Nb[m % 2][0:n, g, b, :],
                                      TTb[(m - 1) % 2][0:n, g, b, :])
                        close(last, f"TT{t}_{m}_{g}")
                TTf = TTb[rounds(t) % 2]
                q = open_(f"W{t}")
                for h in range(H):
                    last = mm(q[0:n, HD * h:HD * h + HD], mkt[0:n, h, 2 * n:3 * n], tok["v"][0:n, t, HD * h:HD * h + HD])
                close(last, f"W{t}")
                for g in range(2):
                    evicted(pe, f"TT{t}_{rounds(t)}_{g}")
                q = open_(f"ZA{t}")
                for h in range(H):
                    g, b = h % 2, h // 2
                    last = mm(q[64 * g:64 * g + 64, n * b:n * b + n], tok["a"][0:n, t, HD * h:HD * h + HD],
                              TTf[0:n, g, b, :])
                close(last, f"ZA{t}")
                evicted(pe, f"W{t}")
                q = open_(f"ZV{t}")
                for h in range(H):
                    last = mm(q[0:n, HD * h:HD * h + HD], TTf[0:n, h % 2, h // 2, :], W1[0:n, HD * h:HD * h + HD])
                close(last, f"ZV{t}")
                evicted(pe, f"ZA{t}")
                if t < 2:
                    for c in range(4):
                        rq = slice(32 * c, 32 * c + 32)
                        if t == 0 and c == 0:
                            pe.wait_ge(st_ready, 1)
                        else:
                            evicted(pe, f"S{t}_{c - 1}" if c else f"S{t - 1}_3")
                        for g in range(2):
                            pr = slice(64 * g, 64 * g + 64)
                            q = open_(f"U{t}_{c}_{g}")
                            for b in range(CH):
                                last = mm(q[rq, HD * b:HD * b + HD], ZAT[pr, P * b + 32 * c:P * b + 32 * c + 32],
                                          ST[pr, b, :])
                            close(last, f"U{t}_{c}_{g}")
                        for g in range(2):
                            pr = slice(64 * g, 64 * g + 64)
                            q = open_(f"Y{t}_{c}_{g}")
                            for b in range(CH):
                                last = mm(q[pr, L * b:L * b + L], ST[pr, b, :],
                                          AR[pr, b, 1, a + 32 * c:a + 32 * c + 32])
                            close(last, f"Y{t}_{c}_{g}")
                        for g in range(2):
                            evicted(pe, f"U{t}_{c}_{g}")
                        q = open_(f"S{t}_{c}")
                        for h in range(H):
                            g, b = h % 2, h // 2
                            hs = slice(HD * h, HD * h + HD)
                            o_ = q[64 * g:64 * g + 64, HD * b:HD * b + HD]
                            mm(o_, tok["b"][rq, t, hs], Ut[rq, hs], True, False)
                            last = mm(o_, tok["k"][rq, t, hs], tok["v"][rq, t, hs], False, True)
                        close(last, f"S{t}_{c}")
                else:
                    pe.wait_ge(wkv_in, 16)
                    pe.wait_ge(zr_ready, 1)
                    for g in range(2):
                        pr = slice(64 * g, 64 * g + 64)
                        q = open_(f"UY{g}")
                        qv = q[:, 0:2 * CH * NS].rearrange("p (b a n) -> p b a n", b=CH, a=2)
                        for b in range(CH):
                            for s in range(NB):
                                last = mm(qv[pr, b, :, NT * s:NT * s + NT], ST0[pr, b, s, :],
                                          ZR[pr, b, :, NT * s:NT * s + NT])
                        close(last, f"UY{g}")
                    for g in range(2):
                        evicted(pe, f"UY{g}")
                    q = open_("Us")
                    for b in range(CH):
                        last = turn(q[0:NS, P * b:P * b + P], Utr[:, b, :])
                    close(last, "Us")
                    for b in range(CH):
                        pe.wait_ge(um_ready, 4 * b + 4)
                        q = open_(f"Ss{b}")
                        for g in range(2):
                            hs = slice(HD * (2 * b + g), HD * (2 * b + g) + HD)
                            o_ = q[64 * g:64 * g + 64, :]
                            mm(o_, tok["b"][0:NS, t, hs], masked[b % 2][0:NS, 0, g, :], True, False)
                            last = mm(o_, tok["k"][0:NS, t, hs], masked[b % 2][0:NS, 1, g, :], False, True)
                        close(last, f"Ss{b}")
                q = open_(f"Y{t}")
                for h in range(H):
                    g, b = h % 2, h // 2
                    hs = slice(HD * h, HD * h + HD)
                    o_ = q[64 * g:64 * g + 64, n * b:n * b + n]
                    mm(o_, Ut[0:n, hs], mkt[0:n, h, n:2 * n], True, False)
                    last = mm(o_, tok["v"][0:n, t, hs], mkt[0:n, h, 3 * n:4 * n], False, True)
                close(last, f"Y{t}")
            for t in range(3):
                evicted(pe, f"Y{t}")
            for b in range(CH):
                close(mm(open_(f"gm{b}")[:, 0:N], head, YT[:, b, :]), f"gm{b}")
            pe.wait_ge(conv_done, TAPS + 1)
            q = open_("cm")
            for b in range(CH):
                last = mm(q[:, 0:N], c_("c512", P), cat[:, CH + b, :], b == 0, b == CH - 1)
            close(last, "cm")
            for b in range(CH):
                pe.wait_ge(ysq_ready, b + 1)
                close(mm(open_(f"gv{b}")[:, 0:N], head, ysq[:, b, :]), f"gv{b}")
            pe.wait_ge(cvsq_ready, 1)
            q = open_("cv")
            for b in range(CH):
                last = mm(q[:, 0:N], c_("c512", P), cvsq[:, b, :], b == 0, b == CH - 1)
            close(last, "cv")

            def picks(p0, t):
                c0, n = (0, P) if t < 2 else (P, NS)
                return c_("sel", P + NS, 9, p0)[:, c0:c0 + n]

            def spread(name, r, j, t):
                close(mm(open_(name)[0:TILES[t][1], :], picks(32 * j, t), rows[32 * j:32 * j + 9, r, :]), name)

            for r in range(2):
                evicted(pe, f"row{r}")
            pe.wait_ge(wout_in, 16)
            pe.wait_ge(cat_ready, 2 * CH)
            for t, (a, n) in enumerate(TILES):
                for j in range(2):
                    spread(f"g1_{t}_{j}", 0, j, t)
                for j in range(2):
                    q = open_(f"mix_{t}_{j}")
                    for k in range(KD):
                        last = mm(q[0:n, :], cat[:, k, a:a + n], w_out[:, k, 512 * j:512 * j + 512], k == 0, k == KD - 1)
                    close(last, f"mix_{t}_{j}")
            pe.wait_ge(tail_in, 16 * 7)
            for t, (a, n) in enumerate(TILES):
                for j in range(2):
                    spread(f"sc2_{t}_{j}", 1, j, t)
                for j in range(2):
                    spread(f"sh2_{t}_{j}", 0, 2 + j, t)
                for j in range(2):
                    evicted(pe, f"sh2_{t}_{j}")
                    q = open_(f"hT{t}_{j}")
                    for b in range(4):
                        last = turn(q[:, n * b:n * b + n], h2[0:n, t, 512 * j + P * b:512 * j + P * b + P], n)
                    close(last, f"hT{t}_{j}")
                for j in range(2):
                    evicted(pe, f"hT{t}_{j}")
                q = open_(f"lg{t}")
                for k in range(KD):
                    mm(q[0:n, 0:E], h2T[:, k, a:a + n], rw[:, k, :], k == 0, False)
                close(mm(q[0:n, 0:E], c_("ones", n, 1), rb[0:1, :], False, True), f"lg{t}")
            pe.wait_ge(mask_ready, 3)
            for t, (a, n) in enumerate(TILES):
                q = open_(f"rank{t}")
                for s in range(t):
                    mm(q[0:n, 0:E], c_("ones", n), mk[:, s, :], s == 0, False)
                close(mm(q[0:n, 0:E], c_("before", n, n), mk[0:n, t, :], t == 0, True), f"rank{t}")
            q = open_("count")
            for t, (a, n) in enumerate(TILES):
                last = mm(q[:, 0:E], c_("ones", P, n), mk[0:n, t, :], t == 0, t == 2)
            close(last, "count")
            pe.wait_ge(gd_ready, 3)
            for t, (a, n) in enumerate(TILES):
                close(turn(open_(f"gt{t}")[0:E, 0:n], Gd[0:n, t, :], n), f"gt{t}")
            for name in list(unit)[-8:]:
                evicted(pe, name)
            pe.wait_ge(table_ready, 5)
            pe.wait_ge(moe_in, 16)
            qG, qT, qY, qH = ps[:, 0, :], ps[:, 3, :], ps[:, 4, :], ps[:, 5, :]

            def gather(it):
                pe.wait_ge(pick_ready, it + 1)
                for t, (a, n) in enumerate(TILES):
                    for j in range(2):
                        last = mm(qG[64 * j:64 * j + 64, :], pick[0:n, t, :], h2[0:n, t, 512 * j:512 * j + 512],
                                  t == 0, t == 2)
                last.then_inc(gathered, 1)

            def bias(it):
                pe.wait_ge(gate_ready, it + 1)
                pe.wait_ge(lin_ready, it + 1)
                pe.wait_ge(sel_ready, it + 1)
                for x in range(2):
                    for j in range(2):
                        mm(ps[64 * j:64 * j + 64, 1 + x, :], sel_e[0:E, :],
                           b_gu[0:E, FF * x + 512 * j:FF * x + 512 * j + 512], True, False)

            def turn_tokens(it):
                pe.wait_ge(rows_read, it + 1)
                for b in range(4):
                    last = turn(qH[:, P * b:P * b + P], gS[:, P * b:P * b + P])
                last.then_inc(tokens_turned, 1)

            gather(0)
            bias(0)
            turn_tokens(0)
            with pe.Fori(0, E // 2) as pair:
                e = pair * 2
                for s in range(2):
                    first = pe.value_load(cumi[0:1, bass.ds(e + s, 1)], min_val=0, max_val=MAXIT)
                    end = pe.value_load(cumi[0:1, bass.ds(e + (s + 1), 1)], min_val=0, max_val=MAXIT)
                    with pe.Fori(first, end) as it:
                        pe.wait_ge(hTe_ready, it + 1)
                        for k in range(KD):
                            if k % 2 == 0:
                                pe.wait_ge(gu_in[s][k // 2], e * 8 + 16)
                            for x in range(2):
                                for j in range(2):
                                    last = mm(ps[64 * j:64 * j + 64, 1 + x, :],
                                              hTe[:, k % 4, C * (k // 4):C * (k // 4) + C],
                                              gu[s][:, k, FF * x + 512 * j:FF * x + 512 * j + 512], False, k == KD - 1)
                        last.then_inc(gu_done, 1)
                        gather(it + 1)
                        pe.wait_ge(act_ready, it + 1)
                        for b in range(4):
                            last = turn(qT[:, P * b:P * b + P], actS[:, P * b:P * b + P])
                        last.then_inc(act_turned, 1)
                        bias(it + 1)
                        turn_tokens(it + 1)
                        pe.wait_ge(actT_ready, it + 1)
                        pe.wait_ge(y_out, it + 1)
                        for k in range(KD):
                            if k % 4 == 0:
                                pe.wait_ge(dn_in[k // 4], e * 16 + 16 * (s + 1))
                            for j in range(2):
                                last = mm(qY[64 * j:64 * j + 64, :], actT[:, k % 4, C * (k // 4):C * (k // 4) + C],
                                          dn[:, k, 512 * j:512 * j + 512], k == 0, k == KD - 1)
                        last.then_inc(dn_done, 1)
            total = pe.value_load(cumi[0:1, E:E + 1], min_val=1, max_val=MAXIT)
            pe.wait_ge(y_out, total + 1)
            pe.wait_ge(final_in, 16 * 7)
            for t, (a, n) in enumerate(TILES):
                for j in range(2):
                    mm(ps[0:n, END_BANKS[2 * t + j], :], picks(0, t), g2r[0:9, j, :]).then_inc(gate2_ready, 1)
            for t, (a, n) in enumerate(TILES):
                for j in range(2):
                    pe.wait_ge(gate2_read, 2 * t + j + 1)
                    last = mm(ps[0:n, END_BANKS[2 * t + j], :], gT[0:E, a:a + n], bdn[0:E, 512 * j:512 * j + 512],
                              True, j == 1)
                last.then_inc(bias_ready, 1)
            pe.wait_ge(dgate_ready, 12)
            for t, (a, n) in enumerate(TILES):
                pe.wait_ge(rowsg_in[t], 64)
                for k in range(4):
                    last = mm(ps[0:n, END_BANKS[2 * t], :], dgate[0:n, 4 * t + k, 0:n], yg[0:n, 4 * t + k, 0:512],
                              False, k == 3)
                last.then_inc(sum_ready, 1)

        @block.scalar
        def _(act):
            run = Counted(act, astep)
            f = nc.scalar.activation
            roots = []

            def root(x):
                roots.append(0)
                act.wait_ge(var_ready, len(roots))
                run(f(x, x, ACT.Sqrt), root_ready, wait=False)

            act.wait_ge(cond_in, 16)
            run(f(cs, cT, ACT.Sigmoid), csig_ready, wait=False)
            act.wait_ge(x_in, 16)
            for b in range(ZB):
                q = arrived(act, f"z{b}")
                if b < SH:
                    run(nc.scalar.copy(zs[:, b, 1:1 + NPR], q[:, 0:NPR]), wait=False)
                    read(nc.scalar.copy(smp_ext(zs[:, b, 1 + NPR:EXT])[:, :, 1:1 + NT], smp(q[:, NPR:N])), f"z{b}")
                elif b % 2 == 0:
                    read(f(usg[:, (b - SH) // 2, :], q[:, 0:N], ACT.Sigmoid), f"z{b}")
            act.wait_ge(zm_ready, SH)
            run(f(lact[0:64, 0, :], zm[0:64, 12, :], ACT.Tanh), tanh_ready, wait=False)
            run(f(lact[:, 1, :], zm[:, 13, :], ACT.Sigmoid), gsig_ready, wait=False)
            for b in range(CH):
                read(f(sg[:, b, :], arrived(act, f"w{b}")[:, 0:N], ACT.Sigmoid, bias=p_("w0", b)), f"w{b}")
            for b in range(CH):
                read(f(aT[:, b, :], arrived(act, f"a{b}")[:, 0:N], ACT.Sigmoid, bias=p_("a0", b)), f"a{b}")
            for b in range(CH):
                read(nc.scalar.copy(gate[:, b, :], arrived(act, f"g{b}")[:, 0:N]), f"g{b}")
            root(kkn)
            act.wait_ge(cum_ready, 1)
            run(f(EI, cumI, ACT.Exp, scale=-C0), exp_ready, wait=False)
            run(f(EE, EE, ACT.Exp, scale=-C0), exp_ready, wait=False)
            run(f(EN, cumI, ACT.Exp, scale=C0), exp_ready, wait=False)
            for t, (a, n) in enumerate(TILES):
                for i, x in enumerate("bkva"):
                    if i % 2 == 0:
                        read(nc.scalar.copy(tok[x][0:n, t, :], arrived(act, f"{x}tok{t}")[0:n, :]), f"{x}tok{t}")
            for t, (a, n) in enumerate(TILES):
                Nb, NTb = [[at(nbuf[2 * x + y], 2, CH * n) for y in range(2)] for x in range(2)]
                for m in range(1, rounds(t) + 1):
                    for g in range(2):
                        u = f"N{t}_{m}_{g}"
                        read(nc.scalar.copy(Nb[m % 2][0:n, g, :], arrived(act, u)[0:n, 0:CH * n]), u)
                    for g in range(2):
                        if m < rounds(t):
                            u = f"NT{t}_{m}_{g}"
                            read(nc.scalar.copy(NTb[m % 2][0:n, g, :], arrived(act, u)[0:n, 0:CH * n]), u)
                read(nc.scalar.copy(W1[0:n, :], arrived(act, f"W{t}")[0:n, :]), f"W{t}")
                q = arrived(act, f"ZA{t}")
                if t < 2:
                    read(nc.scalar.copy(ZAT, q), f"ZA{t}")
                    for c in range(4):
                        for g in range(2):
                            pr = slice(64 * g, 64 * g + 64)
                            u = f"Y{t}_{c}_{g}"
                            read(nc.scalar.copy(YT[pr, :, a + L * c:a + L * c + L],
                                                arrived(act, u)[pr, 0:CH * L].rearrange("p (b n) -> p b n", b=CH)), u)
                else:
                    read(nc.scalar.copy(ZR[:, :, 0, :], q[:, 0:CH * n].rearrange("p (b n) -> p b n", b=CH)), f"ZA{t}")
                    for g in range(2):
                        pr = slice(64 * g, 64 * g + 64)
                        qv = arrived(act, f"UY{g}")[:, 0:2 * CH * NS].rearrange("p (b a n) -> p b a n", b=CH, a=2)
                        run(nc.scalar.copy(Utr[pr, :, :], qv[pr, :, 0, :]), wait=False)
                        read(nc.scalar.copy(YT[pr, :, NPR:N], qv[pr, :, 1, :]), f"UY{g}")
            for b in range(CH):
                act.wait_ge(yc_ready, b + 1)
                run(f(ysq[:, b, :], YT[:, b, :], ACT.Square), ysq_ready, wait=False)
            act.wait_ge(cvc_ready, 1)
            run(f(cvsq, cat[:, CH:2 * CH, :], ACT.Square), cvsq_ready, wait=False)
            root(yrs)
            root(cvr)
            for b in range(CH):
                act.wait_ge(cvn_ready, b + 1)
                run(f(cvsg[:, b, :], cat[:, CH + b, :], ACT.Sigmoid), cvsg_ready, wait=False)

            normed_n = []

            def normalise(x, t, n):
                normed_n.append(0)
                act.wait_ge(norm_ready, len(normed_n))
                run(f(x, x, ACT.Identity, scale=rstd[0:n, t:t + 1], bias=nmr[0:n, t:t + 1]), normed, wait=False)

            act.wait_ge(tail_in, 16 * 7)
            for t, (a, n) in enumerate(TILES):
                for j in range(2):
                    u = f"g1_{t}_{j}"
                    read(nc.scalar.copy(tA[0:n, t, 512 * j:512 * j + 512], arrived(act, u)[0:n, :]), u)
            for kind, t in NORM_STEPS:
                a, n = TILES[t]
                if kind == "stats":
                    root(rstd[0:n, t:t + 1])
                elif kind == "factors":
                    normalise(xa[0:n, t, :], t, n)
            for t, (a, n) in enumerate(TILES):
                for j in range(2):
                    u = f"hT{t}_{j}"
                    read(nc.scalar.copy(h2T[:, 4 * j:4 * j + 4, a:a + n],
                                        arrived(act, u)[:, 0:4 * n].rearrange("p (b n) -> p b n", b=4)), u)
                u = f"lg{t}"
                read(nc.scalar.copy(lgt[0:n, t, :], arrived(act, u)[0:n, 0:E]), u)
            for t, (a, n) in enumerate(TILES):
                act.wait_ge(delta_ready, t + 1)
                run(f(e4[0:n, :], e4[0:n, :], ACT.Exp), e4_ready, wait=False)
            for t, (a, n) in enumerate(TILES):
                read(nc.scalar.copy(gT[0:E, a:a + n], arrived(act, f"gt{t}")[0:E, 0:n]), f"gt{t}")
            nc.scalar.copy(small[:, 315:316], small[:, 313:314]).then_inc(y_out, 1)
            act.wait_ge(table_ready, 5)
            total = act.value_load(cumi[0:1, E:E + 1], min_val=1, max_val=MAXIT)
            act.wait_ge(gathered, 1)
            nc.scalar.copy(gS, ps[:, 0, :]).then_inc(rows_read, 1)
            with act.Fori(0, total) as it:
                act.wait_ge(gate_ready, it + 2)
                f(sigS, gateS, ACT.Sigmoid, scale=SWI).then_inc(sig_ready, 1)
                act.wait_ge(gathered, it + 2)
                nc.scalar.copy(gS, ps[:, 0, :]).then_inc(rows_read, 1)
                act.wait_ge(dn_done, it + 1)
                act.wait_ge(y_stored, it * 32 + 32)
                nc.scalar.copy(yS, ps[:, 4, :]).then_inc(y_out, 1)
                act.wait_ge(y_out, it + 2)
                for j in range(2):
                    act.dma_start(y_dram[bass.ds(it * C, C), 512 * j:512 * j + 512],
                                  yS[64 * j:64 * j + 64, :]).then_inc(y_stored, 16)
            for t, (a, n) in enumerate(TILES):
                for j in range(2):
                    act.wait_ge(gate2_ready, 2 * t + j + 1)
                    nc.scalar.copy(fg[0:n, t, 512 * j:512 * j + 512], ps[0:n, END_BANKS[2 * t + j], :]
                                   ).then_inc(gate2_read, 1)
            for kind, t in NORM_STEPS:
                a, n = TILES[t]
                if kind == "stats":
                    root(rstd[0:n, t:t + 1])
                elif kind == "factors":
                    normalise(fr[0:n, t, :], t, n)

        @block.vector
        def _(dve):
            run = Counted(dve, vstep)
            V = nc.vector
            tt, ts, stt = V.tensor_tensor, V.tensor_scalar, V.scalar_tensor_tensor

            def free(ins, name):
                read(ins, name)
                evicted(dve, name)

            def ask_root(count):
                count(V.memset(small[:, 313:314], 0.0), var_ready, wait=False)
                roots.append(0)
                return len(roots)

            def invert_root(x, count=run):
                n = ask_root(count)
                dve.wait_ge(root_ready, n)
                count(V.reciprocal(x, x))

            roots = []
            run(V.memset(zs[:, :, 0:1], 0.0))
            run(V.memset(gslot, -1.0))
            dve.wait_ge(cond_in, 16)
            dve.wait_ge(csig_ready, 1)
            run(tt(cs, cs, cT, ALU.mult), cs_ready)
            dve.wait_ge(params_in, 32)
            run(ts(omk, par[:, PAR["ka"]:PAR["ka"] + CH], -1.0, 1.0, ALU.mult, ALU.add))
            q = arrived(dve, "first")
            for j in range(4):
                ins = V.tensor_copy(rows[32 * j:32 * j + 9, 0, :], q[32 * j:32 * j + 9, :])
                if j == 3:
                    free(ins, "first")
                else:
                    run(ins, wait=False)
            ab = par[:, PAR["adab"]:PAR["adab"] + 16].unsqueeze(2).to_broadcast([P, 16, 9])
            for j in range(4):
                u = f"modT{j}"
                free(tt(modT[:, j:16:4, :], arrived(dve, u)[:, 0:36].rearrange("p (a b) -> p a b", a=4),
                        ab[:, j:16:4, :], ALU.add), u)
            run(ts(modT[:, 8:16, :], modT[:, 8:16, :], 1.0, None, ALU.add))
            dve.wait_ge(x_in, 16)
            for k in range(KD):
                run(ts(hT[:, k, 0:NPR], hT[:, k, 0:NPR], modT[:, 8 + k, 0:1], modT[:, k, 0:1], ALU.mult, ALU.add),
                    wait=False)
            for k in range(KD):
                hs = smp(hT[:, k, NPR:N])
                run(tt(hs, hs, modT[:, 8 + k, 1:9].unsqueeze(2).to_broadcast([P, NB, NT]), ALU.mult))
                run(tt(hs, hs, modT[:, k, 1:9].unsqueeze(2).to_broadcast([P, NB, NT]), ALU.add),
                    h_ready if k == KD - 1 else None)
            run(V.memset(zero, 0.0), zero_ready, wait=False)

            def condition_rows(r):
                if r == 0:
                    dve.wait_ge(rows_in, 64)
                q = arrived(dve, f"row{r}")
                for j in range(4):
                    s = slice(32 * j, 32 * j + 9)
                    ins = tt(rows[s, r, :], q[s, :], adab[s, r, :], ALU.add)
                    if j == 3:
                        free(ins, f"row{r}")
                    else:
                        run(ins, wait=False)

            dve.wait_ge(states_in, 16 * 6)
            zse = [smp_ext(zs[:, b, 1 + NPR:EXT]) for b in range(SH)]
            for b in range(SH):
                run(V.tensor_copy(zse[b][:, :, 0], shift_in[:, b, :]), wait=(b == SH - 1))
            for b in range(SH):
                evicted(dve, f"z{b}")
                run(tt(dprev[:, 0:NPR], zs[:, b, 0:NPR], zs[:, b, 1:1 + NPR], ALU.subtract), wait=False)
                run(tt(smp(dprev[:, NPR:N]), zse[b][:, :, 0:NT], zse[b][:, :, 1:1 + NT], ALU.subtract))
                run(stt(zm[:, b, 0:NPR], dprev[:, 0:NPR], p_("mu", b), zs[:, b, 1:1 + NPR], ALU.mult, ALU.add), wait=False)
                run(stt(smp(zm[:, b, NPR:N]), smp(dprev[:, NPR:N]), p_("mu", b), zse[b][:, :, 1:1 + NT], ALU.mult,
                        ALU.add), zm_ready)
            run(V.tensor_copy(shift_out[:, :, 0], zs[:, :, NPR]), shift_ready, wait=False)
            zse_all = zs[:, :, 1 + NPR:EXT].rearrange("p c (b t) -> p c b t", b=NB)
            run(V.tensor_copy(shift_out[:, :, 1:9], zse_all[:, :, :, NT]), shift_ready, wait=False)
            for c in range(CH):
                evicted(dve, f"z{SH + 2 * c}")
                u = f"z{SH + 2 * c + 1}"
                q = arrived(dve, u)
                run(tt(ue[:, c, TAPS - 1:PC], q[:, 0:NPR], usg[:, c, 0:NPR], ALU.mult), u_ready)
                us = ue[:, c, PC:UW].rearrange("p (b s) -> p b s", b=NB)
                run(tt(us[:, :, TAPS - 1:SC], smp(q[:, NPR:N]), smp(usg[:, c, NPR:N]), ALU.mult), u_ready)
                read(V.memset(small[:, 310:311], 0.0), u)
            r_, k_, v_ = zm[:, 0:CH, :], zm[:, CH:2 * CH, :], zm[:, 2 * CH:3 * CH, :]
            for b in range(CH):
                run(ts(t1[:, b, :], k_[:, b, :], p_("kk", b), None, ALU.mult))
            run(tt(t2, t1, t1, ALU.mult), sq_ready)
            for b in range(CH):
                u = f"kk{b}"
                free(ts(kkn[:, b, :], arrived(dve, u)[:, 0:N], 1e-24 / HD, None, ALU.max), u)
            invert_root(kkn)
            run(stt(kkn, kkn, 0.125, t1, ALU.mult, ALU.mult))
            for b in range(CH):
                evicted(dve, f"a{b}")
                run(ts(kp[:, b, :], aT[:, b, :], p_("ka", b), omk[:, b:b + 1], ALU.mult, ALU.add))
            run(tt(kp, kp, k_, ALU.mult))
            for b in range(CH):
                run(stt(t2[:, b, :], r_[:, b, :], p_("rk", b), kp[:, b, :], ALU.mult, ALU.mult), rk_ready)
            for b in range(CH):
                evicted(dve, f"w{b}")
                run(V.tensor_tensor_scan(cumI[:, b, :], c_("scan", N), sg[:, b, :], 0.0, ALU.mult, ALU.add))
            run(tt(EE, cumI, sg, ALU.subtract), cum_ready)
            for b in range(CH):
                u = f"rk{b}"
                free(stt(bonus[:, b, :], arrived(dve, u)[:, 0:N], float(HD), v_[:, b, :], ALU.mult, ALU.mult), u)
            condition_rows(0)
            run(tt(t1, kkn, aT, ALU.mult))
            dve.wait_ge(exp_ready, 3)
            run(stt(AR[:, :, 0, :], kkn, -1.0, EE, ALU.mult, ALU.mult), wait=False)
            run(tt(AR[:, :, 1, :], r_, EI, ALU.mult), wait=False)
            run(tt(bt, t1, EN, ALU.mult), wait=False)
            evicted(dve, f"g{CH - 1}")
            run(tt(kt, kp, EN, ALU.mult))
            for b in range(CH):
                for x, y in ((bb, bt), (kb, kt)):
                    lp = EI[:, b, L - 1:NPR:L].unsqueeze(2).to_broadcast([P, NPR // L, L])
                    ls = EI[:, b, NPR + NT - 1:N:NT].unsqueeze(2).to_broadcast([P, NB, NT])
                    run(tt(x[:, b, 0:NPR].rearrange("p (c l) -> p c l", l=L),
                           y[:, b, 0:NPR].rearrange("p (c l) -> p c l", l=L), lp, ALU.mult), wait=False)
                    run(tt(smp(x[:, b, NPR:N]), smp(y[:, b, NPR:N]), ls, ALU.mult))
            run(V.memset(small[:, 317:318], 0.0), tilde_ready)
            condition_rows(1)
            run(V.memset(ST, 0.0))
            run(V.memset(STd, 0.0), st_ready)
            for b in range(CH):
                run(ts(bonus[:, b, :], bonus[:, b, :], p_("lb", b), None, ALU.add))
            for t, (a, n) in enumerate(TILES):
                for i, x in enumerate("bkva"):
                    if i % 2:
                        free(V.tensor_copy(tok[x][0:n, t, :], arrived(dve, f"{x}tok{t}")[0:n, :]), f"{x}tok{t}")
            for t, (a, n) in enumerate(TILES):
                mkt = at(MK0, H, 4 * n)
                tri = c_("tri", 2 * n, n) if t < 2 else c_("tri_s", 2 * n, n)
                low = c_("low", n, n) if t < 2 else c_("low_s", n, n)
                N0 = at(nbuf[0], 2, CH, n)
                TTb = [at(nbuf[4 + y], 2, CH, n) for y in range(2)]
                for h in range(H):
                    u = f"G{t}_{h}"
                    free(tt(mkt[0:n, h, :].rearrange("p (a b) -> p a b", a=2),
                            arrived(dve, u)[0:n, 0:4 * n].rearrange("p (a b) -> p a b", a=2),
                            tri.unsqueeze(1).to_broadcast([n, 2, 2 * n]), ALU.mult), u)
                for g in range(2):
                    u = f"A{t}_{g}"
                    free(tt(N0[0:n, g, :, :], arrived(dve, u)[0:n, 0:CH * n].rearrange("p (b j) -> p b j", b=CH),
                            low.unsqueeze(1).to_broadcast([n, CH, n]), ALU.mult), u)
                for g in range(2):
                    run(tt(TTb[0][0:n, g, :, :], mkt[0:n, g:H:2, 0:n],
                           ident[0:n, 0:n].unsqueeze(1).to_broadcast([n, CH, n]), ALU.add), tt0_ready)
                for m in range(1, rounds(t) + 1):
                    for g in range(2):
                        u = f"TT{t}_{m}_{g}"
                        free(tt(TTb[m % 2][0:n, g, :, :], TTb[(m - 1) % 2][0:n, g, :, :],
                                arrived(dve, u)[0:n, 0:CH * n].rearrange("p (b j) -> p b j", b=CH), ALU.add), u)
                if t == 2:
                    run(V.tensor_copy(ZR[:, :, 1, :], AR[:, :, 1, NPR:N]), zr_ready)
                free(V.tensor_copy(ZV[0:n, :], arrived(dve, f"ZV{t}")[0:n, :]), f"ZV{t}")
                if t < 2:
                    for c in range(4):
                        rq = slice(32 * c, 32 * c + 32)
                        end = a + L * c + L - 1
                        run(tt(STd, ST, EI[:, :, end:end + 1].to_broadcast([P, CH, HD]), ALU.mult))
                        for g in range(2):
                            u = f"U{t}_{c}_{g}"
                            hv = "p (b g v) -> p g b v"
                            free(tt(Ut[rq, :].rearrange(hv, g=2, v=HD)[:, g],
                                    ZV[rq, :].rearrange(hv, g=2, v=HD)[:, g],
                                    arrived(dve, u)[rq, 0:CH * HD].rearrange("p (b v) -> p b v", b=CH), ALU.add), u)
                        u = f"S{t}_{c}"
                        free(tt(ST, STd, arrived(dve, u)[:, 0:CH * HD].rearrange("p (b v) -> p b v", b=CH), ALU.add), u)
                else:
                    free(tt(Ut[0:NS, :], ZV[0:NS, :], arrived(dve, "Us")[0:NS, :], ALU.add), "Us")
                    bm = c_("bmask", NB, NS).unsqueeze(2).to_broadcast([NS, NB, HD])
                    for b in range(CH):
                        if b >= 2:
                            arrived(dve, f"Ss{b - 2}")
                        for i, x in enumerate((Ut[0:NS, :], tok["v"][0:NS, 2, :])):
                            for g in range(2):
                                hs = slice(HD * (2 * b + g), HD * (2 * b + g) + HD)
                                run(tt(masked[b % 2][0:NS, i, g, :].rearrange("p (s v) -> p s v", s=NB),
                                       x[:, hs].unsqueeze(1).to_broadcast([NS, NB, HD]), bm, ALU.mult), um_ready)
                    for b in range(CH):
                        lam = EI[:, b, NPR + NT - 1:N:NT].unsqueeze(2).to_broadcast([P, NB, HD])
                        run(tt(ST0[:, b, :, :], ST0[:, b, :, :], lam, ALU.mult))
                        u = f"Ss{b}"
                        free(tt(ST0[:, b, :, :], ST0[:, b, :, :],
                                arrived(dve, u).rearrange("p (s v) -> p s v", s=NB), ALU.add), u)
                if t < 2:
                    for c in range(4):
                        for g in range(2):
                            evicted(dve, f"Y{t}_{c}_{g}")
                else:
                    for g in range(2):
                        evicted(dve, f"UY{g}")
                free(tt(YT[:, :, a:a + n], YT[:, :, a:a + n],
                        arrived(dve, f"Y{t}")[:, 0:CH * n].rearrange("p (b n) -> p b n", b=CH), ALU.add), f"Y{t}")
            for b in range(CH):
                free(tt(YT[:, b, :], YT[:, b, :], arrived(dve, f"gm{b}")[:, 0:N], ALU.subtract), f"gm{b}")
                run(V.memset(small[:, 311:312], 0.0), yc_ready, wait=False)
            dve.wait_ge(conv_done, TAPS + 1)
            cv = cat[:, CH:2 * CH, :]
            free(tt(cv, cv, arrived(dve, "cm")[:, 0:N].unsqueeze(1).to_broadcast([P, CH, N]), ALU.subtract), "cm")
            run(V.memset(small[:, 312:313], 0.0), cvc_ready, wait=False)
            for b in range(CH):
                free(ts(yrs[:, b, :], arrived(dve, f"gv{b}")[:, 0:N], GN_EPS, None, ALU.add), f"gv{b}")
            y_root = ask_root(run)
            free(ts(cvr, arrived(dve, "cv")[:, 0:N], LN_EPS, None, ALU.add), "cv")
            invert_root(cvr)
            run(tt(cv, cv, cvr.unsqueeze(1).to_broadcast([P, CH, N]), ALU.mult))
            for b in range(CH):
                run(ts(cv[:, b, :], cv[:, b, :], p_("cg", b), p_("cbt", b), ALU.mult, ALU.add), cvn_ready)
            dve.wait_ge(root_ready, y_root)
            run(V.reciprocal(yrs, yrs))
            run(tt(YT, YT, yrs, ALU.mult))
            for b in range(CH):
                run(stt(YT[:, b, :], YT[:, b, :], p_("lg", b), bonus[:, b, :], ALU.mult, ALU.add))
                run(tt(cat[:, b, :], YT[:, b, :], gate[:, b, :], ALU.mult), cat_ready)
            for b in range(CH):
                dve.wait_ge(cvsg_ready, b + 1)
                run(tt(cv[:, b, :], cv[:, b, :], cvsg[:, b, :], ALU.mult), cat_ready)

            asked, scaled = {}, []

            def norm_step(kind, t, x, g, b, step, ready):
                n = TILES[t][1]
                r1, m1 = rstd[0:n, t:t + 1], nmr[0:n, t:t + 1]
                if kind == "stats":
                    for j in range(2):
                        step(V.bn_stats(stats[0:n, t, j, :], x[:, 512 * j:512 * j + 512]), wait=(j == 1))
                    step(V.bn_aggr(mv[0:n, t, :], stats[0:n, t, :, :]))
                    step(ts(r1, mv[0:n, t, 1:2], LN_EPS, None, ALU.add))
                    asked[t] = ask_root(step)
                elif kind == "factors":
                    dve.wait_ge(root_ready, asked[t])
                    step(V.reciprocal(r1, r1))
                    step(stt(m1, mv[0:n, t, 0:1], -1.0, r1, ALU.mult, ALU.mult), norm_ready, wait=False)
                else:
                    scaled.append(0)
                    dve.wait_ge(normed, len(scaled))
                    step(tt(x, x, g[0:n, :], ALU.mult))
                    step(tt(x, x, b[0:n, :], ALU.add), ready)

            def mixed(t):
                n = TILES[t][1]
                for j in range(2):
                    js = slice(512 * j, 512 * j + 512)
                    evicted(dve, f"g1_{t}_{j}")
                    u = f"mix_{t}_{j}"
                    free(tt(tA[0:n, t, js], tA[0:n, t, js], arrived(dve, u)[0:n, :], ALU.mult), u)
                run(stt(xa[0:n, t, :], xin[0:n, t, :], ALPHA, tA[0:n, t, :], ALU.mult, ALU.add))

            def modulated(t):
                n = TILES[t][1]
                for j in range(2):
                    js = slice(512 * j, 512 * j + 512)
                    u = f"sc2_{t}_{j}"
                    free(stt(h2[0:n, t, js], arrived(dve, u)[0:n, :], 1.0, xa[0:n, t, js], ALU.add, ALU.mult), u)
                for j in range(2):
                    js = slice(512 * j, 512 * j + 512)
                    u = f"sh2_{t}_{j}"
                    free(tt(h2[0:n, t, js], h2[0:n, t, js], arrived(dve, u)[0:n, :], ALU.add), u)

            dve.wait_ge(tail_in, 16 * 7)
            for kind, t in NORM_STEPS:
                if kind == "stats":
                    mixed(t)
                norm_step(kind, t, xa[0:TILES[t][1], t, :], lnp[:, 0, :], lnp[:, 1, :], run, x1_ready)
                if kind == "out":
                    modulated(t)
            for t, (a, n) in enumerate(TILES):
                u = f"lg{t}"
                evicted(dve, u)
                run(V.max(top_v[0:n, :], lgt[0:n, t, :]))
                run(V.max_index(top_i[0:n, t, :], top_v[0:n, :], lgt[0:n, t, :]))
                run(V.tensor_copy(idxf[0:n, :], top_i[0:n, t, :]))
                run(ts(e4[0:n, :], top_v[0:n, 0:4], top_v[0:n, 0:1], None, ALU.subtract), delta_ready)
                o4 = oh[0:n, 4 * t:4 * t + 4, :]
                run(tt(o4, c_("item", E, n).unsqueeze(1).to_broadcast([n, 4, E]),
                       idxf[0:n, 0:4].unsqueeze(2).to_broadcast([n, 4, E]), ALU.is_equal))
                run(tt(mk[0:n, t, :], o4[:, 0, :], o4[:, 1, :], ALU.add))
                run(tt(mk[0:n, t, :], mk[0:n, t, :], o4[:, 2, :], ALU.add))
                run(tt(mk[0:n, t, :], mk[0:n, t, :], o4[:, 3, :], ALU.add), mask_ready)
                dve.wait_ge(e4_ready, t + 1)
                run(V.tensor_reduce(esum[0:n, :], e4[0:n, :], AX, ALU.add))
                run(V.reciprocal(esum[0:n, :], esum[0:n, :]))
                run(ts(gates[0:n, t, :], e4[0:n, :], esum[0:n, :], None, ALU.mult))
                run(ts(Gd[0:n, t, :], o4[:, 0, :], gates[0:n, t, 0:1], None, ALU.mult))
                for k in range(1, 4):
                    run(stt(Gd[0:n, t, :], o4[:, k, :], gates[0:n, t, k:k + 1], Gd[0:n, t, :], ALU.mult, ALU.add),
                        gd_ready if k == 3 else None)
            free(V.tensor_copy(cnt, arrived(dve, "count")[:, 0:E]), "count")
            run(ts(npf, cnt, float(C), 1.0, ALU.is_gt, ALU.add))
            for i in range(2, (N - 1) // C + 1):
                run(ts(npt, cnt, float(C * i), None, ALU.is_gt))
                run(tt(npf, npf, npt, ALU.add))
            run(V.memset(cumf[:, 0:1], 0.0))
            run(V.tensor_tensor_scan(cumf[:, 1:E + 1], c_("ones", E), npf, 0.0, ALU.mult, ALU.add))
            for t, (a, n) in enumerate(TILES):
                s = slotv[0:n, 0:E]
                u = f"rank{t}"
                free(stt(s, cumf[0:n, 0:E], float(C), arrived(dve, u)[0:n, 0:E], ALU.mult, ALU.add), u)
                run(stt(gslot[0:n, t, :], s, 1.0, mk[0:n, t, :], ALU.add, ALU.mult))
                run(ts(gslot[0:n, t, :], gslot[0:n, t, :], -1.0, None, ALU.add))
                o4 = ohs[0:n, 4 * t:4 * t + 4, :]
                run(tt(o4, oh[0:n, 4 * t:4 * t + 4, :], s.unsqueeze(1).to_broadcast([n, 4, E]), ALU.mult))
                run(V.tensor_reduce(sidx[0:n, 4 * t:4 * t + 4], o4, AX, ALU.add))
                run(V.tensor_copy(slot_i[0:n, 4 * t:4 * t + 4], sidx[0:n, 4 * t:4 * t + 4]), table_ready)
            run(V.tensor_copy(cumi[:, :], cumf), table_ready)
            run(tt(item_m, c_("item", MAXIT + 1).unsqueeze(2).to_broadcast([P, MAXIT + 1, E]),
                   cumf[:, 1:E + 1].unsqueeze(1).to_broadcast([P, MAXIT + 1, E]), ALU.is_ge))
            run(V.tensor_reduce(item_f, item_m, AX, ALU.add))
            run(ts(item_i[:, :], item_f, float(E - 1), None, ALU.min), table_ready)
            slot = c_("slot", C)
            for i, m in enumerate((gate_ready, lin_ready)):
                V.memset(small[:, 316 + i:317 + i], 0.0).then_inc(m, 1)

            def choose(it):
                e = dve.value_load(item_i[0:1, bass.ds(it, 1)], min_val=0, max_val=E - 1)
                ts(slot, slot, float(C), None, ALU.add).then_inc(slot_ready, 1)
                dve.wait_ge(slot_ready, it + 1)
                tt(pick, gslot[:, :, bass.ds(e, 1)].to_broadcast([P, 3, C]),
                   slot.unsqueeze(1).to_broadcast([P, 3, C]), ALU.is_equal).then_inc(pick_ready, 1)
                V.tensor_copy(sel_e[0:E, :], cst[0:E, bass.ds(e + CST["ident"], 1)].to_broadcast([E, C])
                              ).then_inc(sel_ready, 1)

            choose(0)
            total = dve.value_load(cumi[0:1, E:E + 1], min_val=1, max_val=MAXIT)
            with dve.Fori(0, total) as it:
                dve.wait_ge(tokens_turned, it + 1)
                V.tensor_copy(hTe, ps[:, 5, :].rearrange("p (b c) -> p b c", b=4)).then_inc(hTe_ready, 1)
                choose(it + 1)
                dve.wait_ge(gu_done, it + 1)
                ts(gateS, ps[:, 1, :], LIMIT, None, ALU.min).then_inc(gate_ready, 1)
                ts(linS, ps[:, 2, :], LIMIT, -LIMIT, ALU.min, ALU.max).then_inc(lin_ready, 1)
                dve.wait_ge(sig_ready, it + 1)
                tt(gateS, gateS, sigS, ALU.mult).then_inc(prod_ready, 1)
                dve.wait_ge(prod_ready, it + 1)
                stt(actS, linS, 1.0, gateS, ALU.add, ALU.mult).then_inc(act_ready, 1)
                dve.wait_ge(act_turned, it + 1)
                V.tensor_copy(actT, ps[:, 3, :].rearrange("p (b c) -> p b c", b=4)).then_inc(actT_ready, 1)
            fin = Counted(dve, fstep)
            dve.wait_ge(gu_done, total)
            for t, (a, n) in enumerate(TILES):
                for k in range(4):
                    ts(dgate[0:n, 4 * t + k, 0:n], ident[0:n, 0:n], gates[0:n, t, k:k + 1], None, ALU.mult
                       ).then_inc(dgate_ready, 1)
            dve.wait_ge(final_in, 16 * 7)
            for kind, t in NORM_STEPS:
                n = TILES[t][1]
                if kind == "stats":
                    right, left = fr[0:n, t, 512:D], fr[0:n, t, 0:512]
                    dve.wait_ge(bias_ready, t + 1)
                    dve.wait_ge(rowsg_in[t], 64)
                    for k in range(4):
                        fin(stt(right, yg[0:n, 4 * t + k, 512:D], gates[0:n, t, k:k + 1],
                                ps[0:n, END_BANKS[2 * t + 1], :] if k == 0 else right, ALU.mult, ALU.add))
                    fin(tt(right, right, fg[0:n, t, 512:D], ALU.mult))
                    dve.wait_ge(sum_ready, t + 1)
                    fin(tt(left, ps[0:n, END_BANKS[2 * t], :], fg[0:n, t, 0:512], ALU.mult))
                    fin(stt(fr[0:n, t, :], fx[0:n, t, :], ALPHA, fr[0:n, t, :], ALU.mult, ALU.add))
                norm_step(kind, t, fr[0:n, t, :], fln[:, 0, :], fln[:, 1, :], fin, out_ready)


def smp_ext(a):
    return a.rearrange("p (b t) -> p b t", b=NB)


def kernel(**inputs):
    import numpy as np
    import concourse.bacc as bacc
    from concourse.bass_utils import run_bass_kernel_spmd

    x = {k: np.asarray(v) for k, v in inputs.items()}
    f = np.float32

    def blocks(v):
        v = v.reshape(v.shape[:-1] + (-1, P))
        return np.moveaxis(v, (-1, -2), (0, 1))

    cst = np.zeros((P, NCST), f)

    def put(name, a):
        cst[0:a.shape[0], CST[name]:CST[name] + a.shape[1]] = a

    i = np.arange(P)
    same = (i[:, None] // L) == (i[None, :] // L)
    put("ident", np.eye(P, dtype=f))
    put("tri", np.concatenate([same & (i[:, None] < i[None, :]), same & (i[:, None] <= i[None, :])], 1).astype(f))
    put("low", (same & (i[:, None] > i[None, :])).astype(f))
    j = np.arange(NS)
    same_s = (j[:, None] // NT) == (j[None, :] // NT)
    put("tri_s", np.concatenate([same_s & (j[:, None] < j[None, :]), same_s & (j[:, None] <= j[None, :])], 1).astype(f))
    put("low_s", (same_s & (j[:, None] > j[None, :])).astype(f))
    reset = np.ones(N, f)
    reset[0:NPR:L] = 0
    reset[NPR:N:NT] = 0
    put("scan", np.tile(reset, (P, 1)))
    put("head", ((i[:, None] // HD) == (i[None, :] // HD)).astype(f) / f(HD))
    put("c512", np.full((P, P), 1.0 / 512, f))
    sel = np.zeros((P, P + NS), f)
    for g in range(4):
        sel[32 * g, 0:P] = 1
        for b in range(NB):
            sel[32 * g + 1 + b, P + NT * b:P + NT * b + NT] = 1
    put("sel", sel)
    put("before", (i[:, None] < i[None, :]).astype(f))
    put("ones", np.ones((P, P), f))
    put("slot", np.tile(np.arange(C, dtype=f) - C, (P, 1)))
    put("item", np.tile(np.arange(MAXIT + 1, dtype=f), (P, 1)))
    put("bmask", ((j[:, None] // NT) == np.arange(NB)[None, :]).astype(f))

    par = np.concatenate([blocks(x["tm_mu"][0]), blocks(x["w0"][0]), blocks(x["a0"][0]), blocks(x["k_k"][0]),
                          blocks(x["k_a"][0]), blocks(x["r_k"][0].reshape(-1)), blocks(x["lnx_g"][0]),
                          blocks(x["lnx_b"][0]), blocks(x["conv_w"][0]).reshape(P, -1), blocks(x["conv_b"][0]),
                          blocks(x["conv_ln_g"][0]), blocks(x["conv_ln_b"][0]), blocks(x["ada_b"][0][0:2 * D])], 1)
    tokens = np.concatenate([x["x_prompt"].reshape(NPR, D), x["x_sample"].reshape(NS, D)])
    cond = np.concatenate([x["c_prompt"], x["c_sample"]])

    def cols(w, width):
        return w.reshape(KD, P, -1, width).transpose(2, 1, 0, 3)

    win = cols(x["w_in"][0], P)
    order = list(range(SH)) + [b for c in range(CH) for b in (SH + CH + c, SH + c)]
    ada_b = x["ada_b"][0].reshape(12, 512)
    arrays = {
        "cst": cst, "par": par, "cT": blocks(cond), "xT": blocks(tokens), "x": tokens,
        "adab_rows": np.stack([np.tile(ada_b[[4 + g, 8 + g]][None], (9, 1, 1)) for g in range(4)]),
        "ada": cols(x["ada_w"][0], 512), "win": win[order],
        "lora": np.stack([np.concatenate([x["w2"][0], x["a2"][0]]), x["g2"][0]], 1),
        "shiftT": blocks(x["state_shift"][0]),
        "conv0": np.zeros((P, CH, TAPS - 1), f),
        "convs": blocks(x["state_conv"][0]),
        "w_out": x["w_out"][0].reshape(KD, P, D).transpose(1, 0, 2),
        "wkvT": x["state_wkv"][0].reshape(NB, CH, 2, HD, HD).transpose(2, 4, 1, 0, 3).reshape(P, CH, NB, HD),
        "ln": np.stack([x["ln1_g"][0], x["ln1_b"][0], x["ln2_g"][0], x["ln2_b"][0]]),
        "rw": x["router_w"][0].reshape(KD, P, E).transpose(1, 0, 2), "rb": x["router_b"],
        "w_gu": x["w_gu"][0], "b_gu": x["b_gu"][0], "w_dn": x["w_dn"][0], "b_dn": x["b_dn"][0],
    }
    outs = {"y": (N, D), "wkv_p": (P, CH, HD), "wkv_s": (P, CH, NB, HD), "shift_out": (P, SH, 9),
            "conv_p": (P, CH, TAPS - 1), "conv_s": (P, CH, NB, TAPS - 1)}
    nc = bacc.Bacc("TRN2", target_bir_lowering=False, num_devices=1)
    arrays = {f"in_{k}": np.ascontiguousarray(v) for k, v in arrays.items()}
    io = {k[3:]: nc.dram_tensor(k, v.shape, mybir.dt.from_np(v.dtype), kind="ExternalInput").ap()
          for k, v in arrays.items()}
    for k, shape in outs.items():
        io[k] = nc.dram_tensor(f"out_{k}", shape, F32, kind="ExternalOutput").ap()
    build(nc, io)
    r = run_bass_kernel_spmd(nc, [arrays], core_ids=[0]).results[0]
    r = {k: np.asarray(r[f"out_{k}"]) for k in outs}
    y = r["y"]
    wkv_p = r["wkv_p"].reshape(2, HD, CH, HD).transpose(2, 0, 3, 1).reshape(1, 1, H, HD, HD)
    wkv_s = r["wkv_s"].reshape(2, HD, CH, NB, HD).transpose(3, 2, 0, 4, 1).reshape(1, NB, H, HD, HD)
    shift = r["shift_out"].transpose(2, 1, 0).reshape(9, SH * P)
    conv_p = r["conv_p"].transpose(2, 1, 0).reshape(1, 1, TAPS - 1, CH * P)
    conv_s = r["conv_s"].transpose(2, 3, 1, 0).reshape(1, NB, TAPS - 1, CH * P)
    c = np.ascontiguousarray
    return (c(y[0:NPR].reshape(1, NPR, D)), c(y[NPR:N].reshape(NB, NT, D)), c(wkv_p), c(wkv_s),
            c(shift[0:1].reshape(1, 1, -1)), c(shift[1:9].reshape(1, NB, -1)), c(conv_p), c(conv_s))
```

```python
from contextlib import ExitStack

import concourse.bass as bass
from concourse import mybir

F32 = mybir.dt.float32
I32 = mybir.dt.int32
U32 = mybir.dt.uint32
ALU = mybir.AluOpType
ACT = mybir.ActivationFunctionType
AX = mybir.AxisListType.X

P = 128
D = 1024
KD = D // P
NPR = 256
NB, NT = 8, 4
NS = NB * NT
N = NPR + NS
TILES = [(0, P), (P, P), (NPR, NS)]
H, HD = 8, 64
CH = 4
SH = 14
ZB = 22
EXT = 1 + NPR + NB * (1 + NT)
TAPS = 31
PC = TAPS - 1 + NPR
SC = TAPS - 1 + NT
UW = PC + NB * SC
L = 32
E = 32
FF = D
C = 64
MAXIT = E + (N * 4) // (C + 1)
END_BANKS = [0, 3, 4, 5, 6, 7]
VECTOR_SUM = (0, 1)
ALPHA = 2.0 ** 0.25
C0 = 0.6065306597126334
SHIFT_ORDER = [4, 5, 6, 7, 12, 13, 0, 1, 2, 3, 8, 9, 10, 11]
Z_K, Z_LORA, Z_R = CH, CH + 2, 2 * CH + 2
POOL_CH = 2
WB = 6
NORM_STEPS = [("stats", 0), ("stats", 1), ("factors", 0), ("stats", 2), ("factors", 1), ("out", 0), ("factors", 2),
              ("out", 1), ("out", 2)]
LN_EPS, GN_EPS = 1e-5, 64e-5
LIMIT, SWI = 7.0, 1.702


def columns(*widths):
    at, table = 0, {}
    for name, width in widths:
        table[name] = at
        at += width
    return table, at


PAR, NPAR = columns(("mu", SH), ("w0", CH), ("a0", CH), ("kk", CH), ("ka", CH), ("rk", CH), ("lg", CH), ("lb", CH),
                    ("cw", CH * TAPS), ("cb", CH), ("cg", CH), ("cbt", CH), ("adab", 2 * KD))
CST, NCST = columns(("ident", P), ("tri", 2 * P), ("low", P), ("tri_s", 2 * NS), ("low_s", NS), ("scan", N),
                    ("head", P), ("c512", P), ("sel", P + NS), ("before", P), ("ones", P), 
                    ("slot", C), ("bmask", NB), ("item", MAXIT + 1))


def rounds(t):
    return 4 if t < 2 else 1


SLOTS = 10
FIRST = 4
PER_LOOP = 5
PEELED = E % PER_LOOP
FILLS = 6 * PER_LOOP // SLOTS


def place(j, c):
    p = FIRST + 6 * j + c
    return p % SLOTS, p // SLOTS + (p % SLOTS >= FIRST)


def psum_units():
    names = ["first"] + [f"modT{j}" for j in range(4)] + [f"z{b}" for b in range(Z_R)]
    names += [f"{x}{b}" for x in "wag" for b in range(CH)] + [f"kk{b}" for b in range(CH)]
    names += [f"z{b}" for b in range(Z_R, SH)] + [f"rk{b}" for b in range(CH)]
    names += [f"z{b}" for b in range(SH, ZB)]
    names += [f"{x}tok{t}" for t in range(3) for x in "bkva"]
    for t in range(3):
        names += ["cm"] if t == 2 else []
        names += [f"G{t}_{h}" for h in range(H)] + [f"A{t}_{g}" for g in range(2)]
        for m in range(1, rounds(t) + 1):
            names += [f"N{t}_{m}_{g}" for g in range(2)]
            if m < rounds(t):
                names += [f"NT{t}_{m}_{g}" for g in range(2)]
            names += [f"TT{t}_{m}_{g}" for g in range(2)]
        names += [f"W{t}", f"ZA{t}", f"ZV{t}"]
        if t < 2:
            for q in range(4):
                names += [f"U{t}_{q}_0", f"U{t}_{q}_1", f"Y{t}_{q}_0", f"Y{t}_{q}_1", f"S{t}_{q}"]
        else:
            names += ["cv", "UY0", "UY1", "Us"] + [f"Ss{b}" for b in range(CH)]
        names += [f"Y{t}"]
    names += [f"gm{b}" for b in range(CH)] + [f"gv{b}" for b in range(CH)]
    names += [f"{x}_{t}_{j}" for x in ("g1", "mix") for t in range(3) for j in range(2) if (x, t) != ("g1", 1)]
    for t in range(3):
        names += [f"{x}_{t}_{j}" for x in ("sc2", "sh2") for j in range(2)] if t != 1 else []
        names += [f"hT{t}_{j}" for j in range(2)] + [f"lg{t}"]
    names += ["rank0", "rank1", "rank2", "count"]
    table = {n: (i % 7, i // 7) for i, n in enumerate(names)}
    table.update(row0=(7, 0), row1=(7, 1), gt0=(7, 2), gt1=(7, 3), gt2=(7, 4))
    return table


class Counted:

    def __init__(self, eng, step):
        self.eng, self.step, self.n = eng, step, {}

    def __call__(self, ins, sem=None, wait=True):
        sem = self.step if sem is None else sem
        self.n[sem.name] = self.n.get(sem.name, 0) + 1
        ins.then_inc(sem, 1)
        if wait:
            self.eng.wait_ge(sem, self.n[sem.name])


def build(nc, io):
    unit = psum_units()
    with ExitStack() as ctx:
        def sem(name):
            return ctx.enter_context(nc.semaphore(name))

        arena = ctx.enter_context(nc.sbuf_tensor("arena", [P, 53000], F32))
        cumi = ctx.enter_context(nc.sbuf_tensor("cumi", [P, E + 1], I32))
        item_i = ctx.enter_context(nc.sbuf_tensor("item_i", [P, MAXIT + 1], I32))
        top_i = ctx.enter_context(nc.sbuf_tensor("top_i", [P, 3, 8], U32))
        slot_i = ctx.enter_context(nc.sbuf_tensor("slot_i", [P, 12], U32))
        ps = ctx.enter_context(nc.psum_tensor("ps", [P, 8, 512], F32))
        y_dram = nc.dram_tensor("y_slots", (MAXIT * C, D), F32, kind="Internal").ap()
        res_dram = nc.dram_tensor("residual", (3, P, D), F32, kind="Internal").ap()
        gate2_dram = nc.dram_tensor("gate2_rows", (9, 2, 512), F32, kind="Internal").ap()

        def at(off, *shape):
            n = 1
            for s in shape:
                n *= s
            a = arena[:, off:off + n]
            if len(shape) == 2:
                a = a.rearrange("p (a b) -> p a b", a=shape[0])
            if len(shape) == 3:
                a = a.rearrange("p (a b c) -> p a b c", a=shape[0], b=shape[1])
            return a

        W = CH * N
        gu_at = [at(4096 * i, 2, 2 * FF) for i in range(SLOTS)]
        dn_at = [at(4096 * i, 4, D) for i in range(SLOTS)]
        o = SLOTS * 4096
        par = at(o, NPAR)
        o += NPAR
        cst = at(o, NCST)
        o += NCST
        h2_at = o
        h2 = at(o, 3, D)
        o += 3 * D
        gslot = at(o, 3, E)
        o += 3 * E
        gates = at(o, 3, 4)
        o += 12
        gT = at(o, N)
        o += N
        small = at(o, 400)
        o += 400
        moe0 = o
        b_gu = at(o, 2 * FF)
        o += 2 * FF
        hTe = at(o, 4, P)
        o += 4 * P
        pick = at(o, 3, C)
        o += 3 * C
        sel_e = at(o, C)
        o += C
        gateS, sigS, linS, actS, yS = [at(o + 512 * i, 512) for i in range(5)]
        actT = at(o + 2560, 4, P)
        gS = at(SLOTS * 4096 + NPAR + CST["tri"], 512)
        item_m, item_f = at(o, MAXIT + 1, E), at(o + 2048, MAXIT + 1)
        assert o + 3072 <= 53000
        hT = at(0, KD, N)
        zs = at(2304, SH, EXT)
        zm = at(6462, SH, N)
        ue = at(10560, CH, UW)
        cat = at(12800, KD, N)
        rows = at(15104, 2, 512)
        adab = at(16128, 2, 512)
        aT, gate, kp, EI, bonus, bt, kt = [at(17152 + i * W, CH, N) for i in range(7)]
        lact, YT, ysq, yrs = kt, kp, bt, kt
        AR = at(25216, CH, 2, N)
        bb, kb = [at(27520 + i * W, CH, N) for i in range(2)]
        sg, kkn, t1, t2 = [at(moe0 + 1536 + i * W, CH, N) for i in range(4)]
        cumI, EE, EN = [at(2304 + i * W, CH, N) for i in range(3)]
        tok = {x: at(i * 1536, 3, 512) for i, x in enumerate("bkva")}
        W1, ZV, Ut, ZAT = [at(6462 + i * 512, 512) for i in range(4)]
        ZR, Utr = at(6462 + 1536, CH, 2, NS), at(6462 + 1792, CH, NS)
        ST0 = at(8510, CH, NB, HD)
        MK0 = 27520
        nbuf = [moe0 + i * 1024 for i in range(6)]
        masked = [at(MK0 + 1024, 2, 2, NB * HD), at(moe0, 2, 2, NB * HD)]
        dprev = at(32128, N)
        cs, cT, modT = at(32416, KD, 9), at(32488, KD, 9), at(32560, 16, 9)
        ST, STd = at(17152, CH, HD), at(17408, CH, HD)
        zero = h2[:, 2, 512:D]
        cvp, usg = [at(h2_at + i * W, CH, N) for i in range(2)]
        cvsq, cvsg = cvp, usg
        ada_buf = [at(32768 + i * 4096, KD, 512) for i in range(2)]
        ada_first = ada_buf + [at(16640 + i * 4096, KD, 512) for i in range(2)]
        win_buf = [at(25216 + i * 1024, KD, P) for i in range(WB)]
        w_out = at(32768, KD, D)
        lora = at(moe0 + 512, 2, 512)
        shift_in = at(moe0, SH, NB)
        shift_out = at(moe0 + 6144, SH, 9)
        cvr = at(MK0 + 3072, N)
        omk = small[:, 0:CH]
        xin, lnp, xa, tA = at(0, 3, D), at(3072, 2, D), at(5120, 3, D), at(moe0 + 2304, 2, D)
        oh, mk, lgt, Gd, ohs = at(11264, 12, E), at(11648, 3, E), at(11744, 3, E), at(11840, 3, E), at(moe0 + 2 * FF, 12, E)
        rw, rb, h2T = at(12288, KD, E), at(12544, E), at(moe0, KD, N)
        stats = small[:, 320:356].rearrange("p (t a b) -> p t a b", t=3, a=2)
        mv, rstd, nmr = small[:, 356:362].rearrange("p (t a) -> p t a", t=3), small[:, 362:365], small[:, 365:368]
        top_v, idxf, esum = small[:, 20:28], small[:, 28:36], small[:, 40:41]
        e4 = small[:, 370:382].rearrange("p (t k) -> p t k", t=3)
        cnt, npf, npt, cumf = small[:, 48:80], small[:, 80:112], small[:, 112:144], small[:, 144:177]
        sidx, slotv = small[:, 180:192], small[:, 192:288]
        yg, fr = at(0, 12, D), at(36352, 3, D)
        fx, fg, fln, bdn = at(24576, 3, D), at(27648, 2, D), at(30720, 2, D), at(32768, D)
        dgate = at(34816, 12, P)

        def c_(name, w, n=P, p0=0):
            return cst[p0:p0 + n, CST[name]:CST[name] + w]

        def p_(name, i):
            return par[:, PAR[name] + i:PAR[name] + i + 1]

        ident = c_("ident", P)

        def smp(a):
            return a.rearrange("p (b t) -> p b t", b=NB)

        filled = [sem(f"bank{b}_filled") for b in range(8)]
        emptied = [sem(f"bank{b}_emptied") for b in range(8)]
        (conv_rest_done, cond_in, sum_ready, norm_ready, normed, dgate_ready, prod_done, zero_ready,
         ring_free, var_ready, root_ready, params_in, x_in, rows_in, ada_used, states_in, lora_in, wkv_in,
         wout_in, tail_in, moe_in, csig_ready, cs_ready, h_ready, zm_ready, tanh_ready, gsig_ready, u_ready,
         sq_ready, rk_ready, cum_ready, exp_ready, tilde_ready, st_ready, tt0_ready, zr_ready, um_ready,
         conv_done, ysq_ready, yc_ready, cvc_ready, cvsq_ready, cvn_ready, cvsg_ready, cat_ready, x1_ready,
         h2_ready, delta_ready, e4_ready, mask_ready, gd_ready, shift_ready, table_ready, stored, spilled,
         vstep, astep) = [sem(n) for n in (
             "conv_rest_done cond_in sum_ready norm_ready normed dgate_ready conv_products zero_ready "
             "ring_free var_ready root_ready params_in x_in rows_in ada_used states_in lora_in wkv_in wout_in "
             "tail_in moe_in csig_ready cs_ready h_ready zm_ready tanh_ready gsig_ready u_ready sq_ready "
             "rk_ready cum_ready exp_ready tilde_ready st_ready tt0_ready zr_ready um_ready conv_done "
             "ysq_ready yc_ready cvc_ready cvsq_ready cvn_ready cvsg_ready cat_ready x1_ready h2_ready "
             "delta_ready e4_ready mask_ready gd_ready shift_ready table_ready stored spilled vector_step "
             "scalar_step").split()]
        first_in = [sem(f"ada_first_in{i}") for i in range(4)]
        ada_in = [sem(f"ada_in{i}") for i in range(2)]
        win_in = [sem(f"win_in{i}") for i in range(WB)]
        chunk_in = [sem(f"place{i}_in") for i in range(SLOTS)]
        (slot_ready, pick_ready, sel_ready, gathered, rows_read, tokens_turned, hTe_ready, gu_done,
         gate_ready, lin_ready, sig_ready, prod_ready, act_ready, act_turned, actT_ready, dn_done, y_out,
         y_stored, final_in, bias_ready, out_ready, fstep) = [sem(n) for n in (
             "slot_ready pick_ready sel_ready gathered rows_read tokens_turned hTe_ready gu_done gate_ready "
             "lin_ready sig_ready prod_ready act_ready act_turned actT_ready dn_done y_out y_stored final_in "
             "bias_ready out_ready final_step").split()]
        rowsg_in = [sem(f"rows_gathered{t}") for t in range(3)]

        def evicted(eng, name):
            b, i = unit[name]
            eng.wait_ge(emptied[b], i + 1)

        def arrived(eng, name):
            b, i = unit[name]
            eng.wait_ge(filled[b], i + 1)
            return ps[:, b, :]

        def read(ins, name):
            ins.then_inc(emptied[unit[name][0]], 1)
            return name

        block = ctx.enter_context(nc.Block())

        @block.sync
        def _(sp):
            sp.dma_start(cT, io["cT"]).then_inc(cond_in, 16)

            def load_ada(n):
                if n < 6:
                    arrived(sp, "first")
                elif n == 9:
                    arrived(sp, "row0")
                else:
                    sp.wait_ge(ada_used, n - 5 - (n > 9))
                sp.dma_start(ada_buf[n % 2], io["ada"][n]).then_inc(ada_in[n % 2], 16)

            for n in range(4):
                sp.dma_start(ada_first[n], io["ada"][n]).then_inc(first_in[n], 16)
                if n == 1:
                    sp.dma_start(cst, io["cst"]).then_inc(params_in, 16)
                    sp.dma_start(par, io["par"]).then_inc(params_in, 16)
            sp.dma_start(hT, io["xT"]).then_inc(x_in, 16)
            for b in range(ZB):
                if b >= WB:
                    arrived(sp, f"z{b - WB}")
                sp.dma_start(win_buf[b % WB], io["win"][b]).then_inc(win_in[b % WB], 16)
                if b == WB - 1:
                    load_ada(4)
                    load_ada(5)
                    sp.dma_start(lora, io["lora"]).then_inc(lora_in, 16)
                    sp.dma_start(shift_in, io["shiftT"]).then_inc(states_in, 16)
                    sp.dma_start(ue[:, :, 0:TAPS - 1], io["conv0"]).then_inc(states_in, 16)
                    for c in range(CH):
                        sp.dma_start(ue[:, c, PC:UW].rearrange("p (b s) -> p b s", b=NB)[:, :, 0:TAPS - 1],
                                     io["convs"][:, c, :, :]).then_inc(states_in, 16)
            for j in range(4):
                sp.dma_start(adab[32 * j:32 * j + 9, :, :], io["adab_rows"][j]).then_inc(rows_in, 16)
            for n in range(6, 8):
                load_ada(n)
            sp.wait_ge(zero_ready, 1)
            for j in range(2):
                sp.dma_start(y_dram[E * C:MAXIT * C, 512 * j:512 * j + 512].rearrange("(p a) n -> p a n", p=64),
                             zero[0:64, :].unsqueeze(1).to_broadcast([64, MAXIT - E, 512])).then_inc(y_stored, 16)
            sp.wait_ge(shift_ready, 2)
            sp.dma_start(io["shift_out"], shift_out).then_inc(stored, 16)
            sp.wait_ge(u_ready, 2 * CH)
            sp.dma_start(io["conv_p"], ue[:, :, NPR:PC]).then_inc(stored, 16)
            for c in range(CH):
                sp.dma_start(io["conv_s"][:, c, :, :],
                             ue[:, c, PC:UW].rearrange("p (b s) -> p b s", b=NB)[:, :, NT:SC]).then_inc(stored, 16)
            evicted(sp, "vtok2")
            sp.dma_start(ST0, io["wkvT"]).then_inc(wkv_in, 16)
            for n in range(8, 12):
                load_ada(n)
            arrived(sp, "row1")
            sp.dma_start(w_out, io["w_out"]).then_inc(wout_in, 16)
            evicted(sp, "S1_3")
            sp.dma_start(io["wkv_p"], ST).then_inc(stored, 16)
            evicted(sp, "row1")
            for j in range(2):
                sp.dma_start(gate2_dram[:, j, :], rows[32 * (2 + j):32 * (2 + j) + 9, 1, :]).then_inc(spilled, 16)
            for b in range(CH):
                evicted(sp, f"Ss{b}")
            sp.dma_start(io["wkv_s"], ST0).then_inc(stored, 16)
            evicted(sp, "Y2")
            sp.wait_ge(conv_done, TAPS + 1)
            sp.wait_ge(stored, 16 * 8)
            for t, (a, n) in enumerate(TILES):
                sp.dma_start(xin[0:n, t, :], io["x"][a:a + n, :]).then_inc(tail_in, 16)
            for i in range(2):
                sp.dma_start(lnp[:, i, :], io["ln"][i:i + 1, :].to_broadcast([P, D])).then_inc(tail_in, 16)
            sp.dma_start(rw, io["rw"]).then_inc(tail_in, 16)
            sp.dma_start(rb[0:1, :], io["rb"]).then_inc(tail_in, 16)
            wg, wd = io["w_gu"], io["w_dn"]

            def load(j, chunks, i=0):
                for c in chunks:
                    s = place(j, c)[0]
                    if c < 4:
                        to, w, n = gu_at[s], wg, 256
                    else:
                        to, w, n = dn_at[s], wd, 512
                    r0 = n * (c % 4)
                    sp.dma_start(to, w[bass.ds(i * PER_LOOP + j, 1), r0:r0 + n, :].rearrange("e (k p) n -> p (e k) n", p=P)
                                 ).then_inc(chunk_in[s], 16)

            def items_through(e):
                return sp.value_load(cumi[0:1, bass.ds(e, 1)], min_val=1, max_val=MAXIT)

            sp.wait_ge(cat_ready, 2 * CH)
            load(0, range(4))
            arrived(sp, "mix_2_1")
            load(0, (4, 5))
            for t, (a, n) in enumerate(TILES):
                sp.wait_ge(x1_ready, t + 1)
                sp.dma_start(res_dram[t, 0:n, :], xa[0:n, t, :]).then_inc(spilled, 16)
            arrived(sp, "lg2")
            sp.dma_start(b_gu[0:E, :], io["b_gu"]).then_inc(moe_in, 16)
            sp.wait_ge(spilled, 16 * 5)
            load(1, (0, 1, 3))
            sp.wait_ge(table_ready, 5)
            for n in ("gt0", "gt1", "gt2"):
                arrived(sp, n)
            load(1, (2,))
            sp.wait_ge(gu_done, items_through(1))
            load(1, (4, 5))
            with sp.Fori(0, E // PER_LOOP) as i:
                for j in range(PEELED, PEELED + PER_LOOP):
                    two_before = items_through(i * PER_LOOP + (j - 1))
                    sp.wait_ge(gu_done, two_before)
                    load(j, (0, 1), i)
                    sp.wait_ge(dn_done, two_before)
                    load(j, (2, 3), i)
                    sp.wait_ge(gu_done, items_through(i * PER_LOOP + j))
                    load(j, (4, 5), i)
            sp.wait_ge(dn_done, items_through(E - 1))
            sp.dma_start(bdn[0:E, :], io["b_dn"]).then_inc(moe_in, 16)
            for t, (a, n) in enumerate(TILES):
                sp.dma_start(fx[0:n, t, :], res_dram[t, 0:n, :]).then_inc(final_in, 16)
            g2 = gate2_dram.rearrange("c j n -> c (j n)")
            sp.dma_start(fg[:, 0, :], g2[0:1, :].to_broadcast([P, D])).then_inc(final_in, 16)
            for b in range(NB):
                sp.dma_start(fg[NT * b:NT * b + NT, 1, :], g2[1 + b:2 + b, :].to_broadcast([NT, D])).then_inc(final_in, 16)
            for i in range(2):
                sp.dma_start(fln[:, i, :], io["ln"][2 + i:3 + i, :].to_broadcast([P, D])).then_inc(final_in, 16)
            for t, (a, n) in enumerate(TILES):
                sp.wait_ge(out_ready, t + 1)
                sp.dma_start(io["y"][a:a + n, :], fr[0:n, t, :]).then_inc(stored, 16)
            sp.wait_ge(stored, 16 * 11)

        @block.gpsimd
        def _(pool):
            taps = par[:, PAR["cw"]:PAR["cw"] + CH * TAPS].rearrange("p (c k) -> p c k", c=CH)
            ptt = nc.gpsimd.tensor_tensor
            y = cat[:, CH:CH + POOL_CH, :]
            products = cvp[:, 0:POOL_CH, :]

            def windows(k):
                yield (products[:, :, 0:NPR], ue[:, 0:POOL_CH, bass.ds(k, NPR)],
                       taps[:, 0:POOL_CH, bass.ds(k, 1)].to_broadcast([P, POOL_CH, NPR]))
                for c in range(POOL_CH):
                    us = ue[:, c, PC:UW].rearrange("p (b s) -> p b s", b=NB)
                    yield (smp(products[:, c, NPR:N]), us[:, :, bass.ds(k, NT)],
                           taps[:, c, bass.ds(k, 1)].unsqueeze(2).to_broadcast([P, NB, NT]))

            pool.wait_ge(params_in, 32)
            pool.wait_ge(states_in, 16 * 6)
            pool.wait_ge(u_ready, 2 * POOL_CH)
            nc.gpsimd.tensor_copy(y, par[:, PAR["cb"]:PAR["cb"] + POOL_CH].unsqueeze(2).to_broadcast([P, POOL_CH, N])
                                  ).then_inc(conv_done, 1)
            with pool.Fori(0, TAPS) as k:
                for p, u, w in windows(k):
                    ptt(p, u, w, ALU.mult).then_inc(prod_done, 1)
                pool.wait_ge(prod_done, k * (1 + POOL_CH) + 1 + POOL_CH)
                pool.wait_ge(conv_done, k + 1)
                ptt(y, y, products, ALU.add).then_inc(conv_done, 1)
                pool.wait_ge(conv_done, k + 2)
            pool.wait_ge(table_ready, 5)
            total = pool.value_load(cumi[0:1, E:E + 1], min_val=0, max_val=MAXIT)
            mark = small[:, 314:315]
            nc.gpsimd.memset(mark, 0.0).then_inc(ring_free, 1)
            pool.wait_ge(ring_free, 1)
            pool.wait_ge(dn_done, total)
            nc.gpsimd.tensor_tensor(mark, mark, mark, ALU.add).then_inc(ring_free, 1)
            pool.wait_ge(ring_free, 2)
            pool.wait_ge(y_stored, total * 32 + 32)
            nc.gpsimd.tensor_tensor(mark, mark, mark, ALU.add).then_inc(ring_free, 1)
            pool.wait_ge(ring_free, 3)
            for t, (a, n) in enumerate(TILES):
                for k in range(4):
                    pool.indirect_dma_start(
                        out=yg[0:n, 4 * t + k, :], out_offset=None, in_=y_dram[:, :],
                        in_offset=bass.IndirectOffsetOnAxis(ap=slot_i[0:n, 4 * t + k:4 * t + k + 1], axis=0),
                    ).then_inc(rowsg_in[t], 16)

        @block.tensor
        def _(pe):
            def open_(name):
                b, i = unit[name]
                if i:
                    pe.wait_ge(emptied[b], i)
                return ps[:, b, :]

            def close(ins, name):
                ins.then_inc(filled[unit[name][0]], 1)

            def mm(out, lhsT, rhs, first=True, last=True):
                return nc.tensor.matmul(out, lhsT, rhs, start=first, stop=last)

            def turn(out, src, n=P):
                return nc.tensor.transpose(out, src, ident[0:n, 0:n])

            pe.wait_ge(cs_ready, 1)
            q = open_("first")
            for n in range(4):
                pe.wait_ge(first_in[n], 16)
                for k in range(KD):
                    for j in range(4):
                        last = mm(q[32 * j:32 * j + 9, P * n:P * n + P], cs[:, k, :],
                                  ada_first[n][:, k, P * j:P * j + P], k == 0, k == KD - 1)
            close(last, "first")
            pe.wait_ge(params_in, 32)
            evicted(pe, "first")
            for j in range(4):
                q = open_(f"modT{j}")
                s = slice(32 * j, 32 * j + 9)
                for n in range(4):
                    last = nc.tensor.transpose(q[:, 9 * n:9 * n + 9], rows[s, 0, P * n:P * n + P], ident[s, s])
                close(last, f"modT{j}")

            def condition_part(i):
                n = 4 + i // 4
                j, r = n % 4, n // 4 - 1
                if i % 16 == 0:
                    open_(f"row{r}")
                if i % 4 == 0:
                    pe.wait_ge(ada_in[n % 2], 16 * (n // 2 - 1))
                q = ps[:, 7, :]
                for k in range(2 * (i % 4), 2 * (i % 4) + 2):
                    last = mm(q[32 * j:32 * j + 9, :], cs[:, k, :], ada_buf[n % 2][:, k, :], k == 0, k == KD - 1)
                if i % 16 == 15:
                    close(last, f"row{r}")
                elif i % 4 == 3:
                    last.then_inc(ada_used, 1)

            pe.wait_ge(h_ready, 1)
            def project(b):
                q = open_(f"z{b}")
                pe.wait_ge(win_in[b % WB], 16 * (b // WB + 1))
                for k in range(KD):
                    last = mm(q[:, 0:N], win_buf[b % WB][:, k, :], hT[:, k, :], k == 0, k == KD - 1)
                close(last, f"z{b}")

            for b in range(Z_R):
                project(b)
            pe.wait_ge(lora_in, 16)
            pe.wait_ge(tanh_ready, 1)
            for b in range(CH):
                close(mm(open_(f"w{b}")[:, 0:N], lora[0:64, 0, P * b:P * b + P], lact[0:64, 0, :]), f"w{b}")
            for b in range(CH):
                close(mm(open_(f"a{b}")[:, 0:N], lora[64:128, 0, P * b:P * b + P], zm[64:128, 12, :]), f"a{b}")
            pe.wait_ge(gsig_ready, 1)
            for b in range(CH):
                close(mm(open_(f"g{b}")[:, 0:N], lora[:, 1, P * b:P * b + P], lact[:, 1, :]), f"g{b}")
            head = c_("head", P)
            pe.wait_ge(sq_ready, 1)
            for b in range(CH):
                close(mm(open_(f"kk{b}")[:, 0:N], head, t2[:, b, :]), f"kk{b}")
            for b in range(Z_R, SH):
                project(b)
            pe.wait_ge(rk_ready, CH)
            for b in range(CH):
                close(mm(open_(f"rk{b}")[:, 0:N], head, t2[:, b, :]), f"rk{b}")
            for b in range(SH, ZB):
                project(b)
            for i in range(8):
                condition_part(i)
            pe.wait_ge(tilde_ready, 1)
            src = {"b": bb, "k": kb, "v": zm[:, 2 * CH:3 * CH, :], "a": AR[:, :, 0, :]}
            for t, (a, n) in enumerate(TILES):
                for x in "bkva":
                    q = open_(f"{x}tok{t}")
                    for b in range(CH):
                        last = turn(q[0:n, P * b:P * b + P], src[x][:, b, a:a + n])
                    close(last, f"{x}tok{t}")
            for x in "bkva":
                evicted(pe, f"{x}tok2")
            for t, (a, n) in enumerate(TILES):
                mkt = at(MK0, H, 4 * n)
                Nb, NTb, TTb = [[at(nbuf[2 * x + y], 2, CH, n) for y in range(2)] for x in range(3)]
                if t == 2:
                    pe.wait_ge(conv_done, TAPS + 1)
                    pe.wait_ge(conv_rest_done, 1)
                    q = open_("cm")
                    for b in range(CH):
                        last = mm(q[:, 0:N], c_("c512", P), cat[:, CH + b, :], b == 0, b == CH - 1)
                    close(last, "cm")
                half = [slice(64 * g, 64 * g + 64) for g in range(2)]
                for b in range(CH):
                    q = [open_(f"G{t}_{2 * b + g}") for g in range(2)]
                    for i, x in enumerate((bt, kt)):
                        for g, pr in enumerate(half):
                            last = mm(q[g][0:n, 2 * n * i:2 * n * (i + 1)].rearrange("p (a b) -> p a b", a=2),
                                      x[pr, b, a:a + n], AR[pr, b, :, a:a + n])
                            if i:
                                close(last, f"G{t}_{2 * b + g}")
                q = [open_(f"A{t}_{g}") for g in range(2)]
                for b in range(CH):
                    for g, pr in enumerate(half):
                        last = mm(q[g][0:n, n * b:n * b + n], AR[pr, b, 0, a:a + n], bt[pr, b, a:a + n])
                        if b == CH - 1:
                            close(last, f"A{t}_{g}")
                for h in range(H):
                    evicted(pe, f"G{t}_{h}")
                for m in range(1, rounds(t) + 1):
                    for g in range(2):
                        evicted(pe, f"A{t}_{g}" if m == 1 else f"N{t}_{m - 1}_{g}")
                        if m > 1:
                            evicted(pe, f"NT{t}_{m - 1}_{g}")
                        q = open_(f"N{t}_{m}_{g}")
                        for b in range(CH):
                            NTp = mkt[0:n, 2 * b + g, 0:n] if m == 1 else NTb[(m - 1) % 2][0:n, g, b, :]
                            last = mm(q[0:n, n * b:n * b + n], NTp, Nb[(m - 1) % 2][0:n, g, b, :])
                        close(last, f"N{t}_{m}_{g}")
                    for g in range(2):
                        if m == rounds(t):
                            break
                        q = open_(f"NT{t}_{m}_{g}")
                        for b in range(CH):
                            NTp = mkt[0:n, 2 * b + g, 0:n] if m == 1 else NTb[(m - 1) % 2][0:n, g, b, :]
                            last = mm(q[0:n, n * b:n * b + n], Nb[(m - 1) % 2][0:n, g, b, :], NTp)
                        close(last, f"NT{t}_{m}_{g}")
                    if t < 2:
                        for i in range(2):
                            condition_part(8 + 12 * t + 2 * (m - 1) + i)
                    for g in range(2):
                        evicted(pe, f"N{t}_{m}_{g}")
                        if m == 1:
                            pe.wait_ge(tt0_ready, 2 * t + g + 1)
                        else:
                            evicted(pe, f"TT{t}_{m - 1}_{g}")
                        q = open_(f"TT{t}_{m}_{g}")
                        for b in range(CH):
                            last = mm(q[0:n, n * b:n * b + n], Nb[m % 2][0:n, g, b, :],
                                      TTb[(m - 1) % 2][0:n, g, b, :])
                        close(last, f"TT{t}_{m}_{g}")
                TTf = TTb[rounds(t) % 2]
                q = open_(f"W{t}")
                for h in range(H):
                    last = mm(q[0:n, HD * h:HD * h + HD], mkt[0:n, h, 2 * n:3 * n], tok["v"][0:n, t, HD * h:HD * h + HD])
                close(last, f"W{t}")
                for g in range(2):
                    evicted(pe, f"TT{t}_{rounds(t)}_{g}")
                q = open_(f"ZA{t}")
                for h in range(H):
                    g, b = h % 2, h // 2
                    last = mm(q[64 * g:64 * g + 64, n * b:n * b + n], tok["a"][0:n, t, HD * h:HD * h + HD],
                              TTf[0:n, g, b, :])
                close(last, f"ZA{t}")
                evicted(pe, f"W{t}")
                q = open_(f"ZV{t}")
                for h in range(H):
                    last = mm(q[0:n, HD * h:HD * h + HD], TTf[0:n, h % 2, h // 2, :], W1[0:n, HD * h:HD * h + HD])
                close(last, f"ZV{t}")
                evicted(pe, f"ZA{t}")
                if t < 2:
                    for c in range(4):
                        rq = slice(32 * c, 32 * c + 32)
                        if t == 0 and c == 0:
                            pe.wait_ge(st_ready, 1)
                        else:
                            evicted(pe, f"S{t}_{c - 1}" if c else f"S{t - 1}_3")
                        q = [open_(f"U{t}_{c}_{g}") for g in range(2)]
                        for b in range(CH):
                            for g, pr in enumerate(half):
                                last = mm(q[g][rq, HD * b:HD * b + HD], ZAT[pr, P * b + 32 * c:P * b + 32 * c + 32],
                                          ST[pr, b, :])
                                if b == CH - 1:
                                    close(last, f"U{t}_{c}_{g}")
                        q = [open_(f"Y{t}_{c}_{g}") for g in range(2)]
                        for b in range(CH):
                            for g, pr in enumerate(half):
                                last = mm(q[g][pr, L * b:L * b + L], ST[pr, b, :],
                                          AR[pr, b, 1, a + 32 * c:a + 32 * c + 32])
                                if b == CH - 1:
                                    close(last, f"Y{t}_{c}_{g}")
                        condition_part(16 + 12 * t + c)
                        for g in range(2):
                            evicted(pe, f"U{t}_{c}_{g}")
                        q = open_(f"S{t}_{c}")
                        for b in range(CH):
                            for x, (l, v) in enumerate(((tok["b"][rq, t], Ut[rq]), (tok["k"][rq, t], tok["v"][rq, t]))):
                                for g in range(2):
                                    hs = slice(HD * (2 * b + g), HD * (2 * b + g) + HD)
                                    last = mm(q[64 * g:64 * g + 64, HD * b:HD * b + HD], l[:, hs], v[:, hs], x == 0, x == 1)
                        close(last, f"S{t}_{c}")
                else:
                    pe.wait_ge(cvsq_ready, 1)
                    q = open_("cv")
                    for b in range(CH):
                        last = mm(q[:, 0:N], c_("c512", P), cvsq[:, b, :], b == 0, b == CH - 1)
                    close(last, "cv")
                    pe.wait_ge(wkv_in, 16)
                    pe.wait_ge(zr_ready, 1)
                    for g in range(2):
                        pr = slice(64 * g, 64 * g + 64)
                        q = open_(f"UY{g}")
                        qv = q[:, 0:2 * CH * NS].rearrange("p (b a n) -> p b a n", b=CH, a=2)
                        for b in range(CH):
                            for s in range(NB):
                                last = mm(qv[pr, b, :, NT * s:NT * s + NT], ST0[pr, b, s, :],
                                          ZR[pr, b, :, NT * s:NT * s + NT])
                        close(last, f"UY{g}")
                    for g in range(2):
                        evicted(pe, f"UY{g}")
                    q = open_("Us")
                    for b in range(CH):
                        last = turn(q[0:NS, P * b:P * b + P], Utr[:, b, :])
                    close(last, "Us")
                    for b in range(CH):
                        pe.wait_ge(um_ready, (6, 8, 12, 16)[b])
                        q = open_(f"Ss{b}")
                        for x in range(2):
                            for g in range(2):
                                hs = slice(HD * (2 * b + g), HD * (2 * b + g) + HD)
                                last = mm(q[64 * g:64 * g + 64, :], tok["bk"[x]][0:NS, t, hs],
                                          masked[b % 2][0:NS, x, g, :], x == 0, x == 1)
                        close(last, f"Ss{b}")
                q = open_(f"Y{t}")
                for b in range(CH):
                    for x, l in enumerate((Ut[0:n], tok["v"][0:n, t])):
                        for g in range(2):
                            h = 2 * b + g
                            last = mm(q[64 * g:64 * g + 64, n * b:n * b + n], l[:, HD * h:HD * h + HD],
                                      mkt[0:n, h, (2 * x + 1) * n:(2 * x + 2) * n], x == 0, x == 1)
                close(last, f"Y{t}")
            for t in range(3):
                evicted(pe, f"Y{t}")
            for b in range(CH):
                close(mm(open_(f"gm{b}")[:, 0:N], head, YT[:, b, :]), f"gm{b}")
            for b in range(CH):
                pe.wait_ge(ysq_ready, b + 1)
                close(mm(open_(f"gv{b}")[:, 0:N], head, ysq[:, b, :]), f"gv{b}")

            def picks(p0, t):
                c0, n = (0, P) if t < 2 else (P, NS)
                return c_("sel", P + NS, 9, p0)[:, c0:c0 + n]

            def spread(name, r, j, t):
                close(mm(open_(name)[0:TILES[t][1], :], picks(32 * j, t), rows[32 * j:32 * j + 9, r, :]), name)

            for r in range(2):
                evicted(pe, f"row{r}")
            pe.wait_ge(wout_in, 16)
            for t in (0, 2):
                for j in range(2):
                    spread(f"g1_{t}_{j}", 0, j, t)
            for part, k0 in enumerate((CH, 0)):
                pe.wait_ge(cat_ready, CH * (part + 1))
                for t, (a, n) in enumerate(TILES):
                    for j in range(2):
                        name = f"mix_{t}_{j}"
                        q = ps[:, unit[name][0], :] if part else open_(name)
                        for k in range(k0, k0 + CH):
                            last = mm(q[0:n, :], cat[:, k, a:a + n], w_out[:, k, 512 * j:512 * j + 512],
                                      k == CH, k == CH - 1)
                        if part:
                            close(last, name)
            pe.wait_ge(tail_in, 16 * 7)
            for t, (a, n) in enumerate(TILES):
                if t != 1:
                    for j in range(2):
                        spread(f"sc2_{t}_{j}", 1, j, t)
                    for j in range(2):
                        spread(f"sh2_{t}_{j}", 0, 2 + j, t)
                for j in range(2):
                    pe.wait_ge(h2_ready, 2 * t + j + 1)
                    q = open_(f"hT{t}_{j}")
                    for b in range(4):
                        last = turn(q[:, n * b:n * b + n], h2[0:n, t, 512 * j + P * b:512 * j + P * b + P], n)
                    close(last, f"hT{t}_{j}")
                for j in range(2):
                    evicted(pe, f"hT{t}_{j}")
                q = open_(f"lg{t}")
                for k in range(KD):
                    mm(q[0:n, 0:E], h2T[:, k, a:a + n], rw[:, k, :], k == 0, False)
                close(mm(q[0:n, 0:E], c_("ones", n, 1), rb[0:1, :], False, True), f"lg{t}")
            pe.wait_ge(mask_ready, 3)
            for t, (a, n) in enumerate(TILES):
                q = open_(f"rank{t}")
                for s in range(t):
                    mm(q[0:n, 0:E], c_("ones", n), mk[:, s, :], s == 0, False)
                close(mm(q[0:n, 0:E], c_("before", n, n), mk[0:n, t, :], t == 0, True), f"rank{t}")
            q = open_("count")
            for t, (a, n) in enumerate(TILES):
                last = mm(q[:, 0:E], c_("ones", P, n), mk[0:n, t, :], t == 0, t == 2)
            close(last, "count")
            for name in ("rank0", "rank1", "rank2", "count"):
                evicted(pe, name)
            pe.wait_ge(moe_in, 16)
            qG, qT, qY, qH = ps[:, 0, :], ps[:, 3, :], ps[:, 4, :], ps[:, 5, :]

            def gather(it):
                pe.wait_ge(pick_ready, it + 1)
                for t, (a, n) in enumerate(TILES):
                    for j in range(2):
                        last = mm(qG[64 * j:64 * j + 64, :], pick[0:n, t, :], h2[0:n, t, 512 * j:512 * j + 512],
                                  t == 0, t == 2)
                last.then_inc(gathered, 1)

            def bias(it):
                pe.wait_ge(gate_ready, it + 1)
                pe.wait_ge(lin_ready, it + 1)
                pe.wait_ge(sel_ready, it + 1)
                for x in range(2):
                    for j in range(2):
                        mm(ps[64 * j:64 * j + 64, 1 + x, :], sel_e[0:E, :],
                           b_gu[0:E, FF * x + 512 * j:FF * x + 512 * j + 512], True, False)

            def turn_tokens(it):
                pe.wait_ge(rows_read, it + 1)
                for b in range(4):
                    last = turn(qH[:, P * b:P * b + P], gS[:, P * b:P * b + P])
                last.then_inc(tokens_turned, 1)

            gather(0)
            bias(0)
            turn_tokens(0)
            pe.wait_ge(gd_ready, 3)
            for t, (a, n) in enumerate(TILES):
                close(turn(open_(f"gt{t}")[0:E, 0:n], Gd[0:n, t, :], n), f"gt{t}")
            pe.wait_ge(table_ready, 5)

            def expert(j, i=0):
                e = i * PER_LOOP + j
                first = pe.value_load(cumi[0:1, bass.ds(e, 1)], min_val=0, max_val=MAXIT)
                end = pe.value_load(cumi[0:1, bass.ds(e + 1, 1)], min_val=0, max_val=MAXIT)
                with pe.Fori(first, end) as it:
                    pe.wait_ge(hTe_ready, it + 1)
                    for k in range(KD):
                        s, fills = place(j, k // 2)
                        if k % 2 == 0:
                            pe.wait_ge(chunk_in[s], i * (16 * FILLS) + 16 * fills)
                        for x in range(2):
                            for h in range(2):
                                last = mm(ps[64 * h:64 * h + 64, 1 + x, :], hTe[:, k % 4, C * (k // 4):C * (k // 4) + C],
                                          gu_at[s][:, k % 2, FF * x + 512 * h:FF * x + 512 * h + 512], False, k == KD - 1)
                    last.then_inc(gu_done, 1)
                    gather(it + 1)
                    pe.wait_ge(act_ready, it + 1)
                    for b in range(4):
                        last = turn(qT[:, P * b:P * b + P], actS[:, P * b:P * b + P])
                    last.then_inc(act_turned, 1)
                    bias(it + 1)
                    turn_tokens(it + 1)
                    pe.wait_ge(actT_ready, it + 1)
                    pe.wait_ge(y_out, it + 1)
                    for k in range(KD):
                        s, fills = place(j, 4 + k // 4)
                        if k % 4 == 0:
                            pe.wait_ge(chunk_in[s], i * (16 * FILLS) + 16 * fills)
                        for h in range(2):
                            last = mm(qY[64 * h:64 * h + 64, :], actT[:, k % 4, C * (k // 4):C * (k // 4) + C],
                                      dn_at[s][:, k % 4, 512 * h:512 * h + 512], k == 0, k == KD - 1)
                    last.then_inc(dn_done, 1)

            for j in range(PEELED):
                expert(j)
            with pe.Fori(0, E // PER_LOOP) as i:
                for j in range(PEELED, PEELED + PER_LOOP):
                    expert(j, i)
            total = pe.value_load(cumi[0:1, E:E + 1], min_val=1, max_val=MAXIT)
            pe.wait_ge(y_out, total + 1)
            pe.wait_ge(moe_in, 32)
            for t, (a, n) in enumerate(TILES):
                for j in range(2):
                    last = mm(ps[0:n, END_BANKS[2 * t + j], :], gT[0:E, a:a + n], bdn[0:E, 512 * j:512 * j + 512],
                              True, (t, j) == VECTOR_SUM)
                    if (t, j) == VECTOR_SUM:
                        last.then_inc(bias_ready, 1)
            pe.wait_ge(dgate_ready, 12)
            for t, (a, n) in enumerate(TILES):
                pe.wait_ge(rowsg_in[t], 64)
                for j in range(2):
                    if (t, j) == VECTOR_SUM:
                        continue
                    for k in range(4):
                        last = mm(ps[0:n, END_BANKS[2 * t + j], :], dgate[0:n, 4 * t + k, 0:n],
                                  yg[0:n, 4 * t + k, 512 * j:512 * j + 512], False, k == 3)
                    last.then_inc(sum_ready, 1)

        @block.scalar
        def _(act):
            run = Counted(act, astep)
            f = nc.scalar.activation
            roots = []

            def root(x):
                roots.append(0)
                act.wait_ge(var_ready, len(roots))
                run(f(x, x, ACT.Sqrt), root_ready, wait=False)

            act.wait_ge(cond_in, 16)
            run(f(cs, cT, ACT.Sigmoid), csig_ready, wait=False)
            act.wait_ge(x_in, 16)

            def keep(p):
                b = SHIFT_ORDER[p]
                q = arrived(act, f"z{p}")
                run(nc.scalar.copy(zs[:, b, 1:1 + NPR], q[:, 0:NPR]), wait=False)
                read(nc.scalar.copy(smp_ext(zs[:, b, 1 + NPR:EXT])[:, :, 1:1 + NT], smp(q[:, NPR:N])), f"z{p}")

            def glu_gate(c):
                u = f"z{SH + 2 * c}"
                read(f(usg[:, c, :], arrived(act, u)[:, 0:N], ACT.Sigmoid), u)

            for p in range(Z_R):
                keep(p)
            act.wait_ge(zm_ready, Z_LORA)
            run(f(lact[0:64, 0, :], zm[0:64, 12, :], ACT.Tanh), tanh_ready, wait=False)
            run(f(lact[:, 1, :], zm[:, 13, :], ACT.Sigmoid), gsig_ready, wait=False)
            for b in range(CH):
                read(f(sg[:, b, :], arrived(act, f"w{b}")[:, 0:N], ACT.Sigmoid, bias=p_("w0", b)), f"w{b}")
            for b in range(CH):
                read(f(aT[:, b, :], arrived(act, f"a{b}")[:, 0:N], ACT.Sigmoid, bias=p_("a0", b)), f"a{b}")
            for b in range(CH):
                read(nc.scalar.copy(gate[:, b, :], arrived(act, f"g{b}")[:, 0:N]), f"g{b}")
            root(kkn)
            for p in range(Z_R, SH):
                keep(p)
            glu_gate(0)
            glu_gate(1)
            act.wait_ge(cum_ready, 1)
            run(f(EI, cumI, ACT.Exp, scale=-C0), exp_ready, wait=False)
            run(f(EE, EE, ACT.Exp, scale=-C0), exp_ready, wait=False)
            run(f(EN, cumI, ACT.Exp, scale=C0), exp_ready, wait=False)
            glu_gate(2)
            glu_gate(3)
            for t, (a, n) in enumerate(TILES):
                for i, x in enumerate("bkva"):
                    if i % 2 == 0:
                        read(nc.scalar.copy(tok[x][0:n, t, :], arrived(act, f"{x}tok{t}")[0:n, :]), f"{x}tok{t}")
            for t, (a, n) in enumerate(TILES):
                Nb, NTb = [[at(nbuf[2 * x + y], 2, CH * n) for y in range(2)] for x in range(2)]
                if t == 2:
                    act.wait_ge(cvc_ready, 1)
                    run(f(cvsq, cat[:, CH:2 * CH, :], ACT.Square), cvsq_ready, wait=False)
                for m in range(1, rounds(t) + 1):
                    for g in range(2):
                        u = f"N{t}_{m}_{g}"
                        read(nc.scalar.copy(Nb[m % 2][0:n, g, :], arrived(act, u)[0:n, 0:CH * n]), u)
                    for g in range(2):
                        if m < rounds(t):
                            u = f"NT{t}_{m}_{g}"
                            read(nc.scalar.copy(NTb[m % 2][0:n, g, :], arrived(act, u)[0:n, 0:CH * n]), u)
                read(nc.scalar.copy(W1[0:n, :], arrived(act, f"W{t}")[0:n, :]), f"W{t}")
                q = arrived(act, f"ZA{t}")
                if t < 2:
                    read(nc.scalar.copy(ZAT, q), f"ZA{t}")
                    for c in range(4):
                        for g in range(2):
                            pr = slice(64 * g, 64 * g + 64)
                            u = f"Y{t}_{c}_{g}"
                            read(nc.scalar.copy(YT[pr, :, a + L * c:a + L * c + L],
                                                arrived(act, u)[pr, 0:CH * L].rearrange("p (b n) -> p b n", b=CH)), u)
                else:
                    read(nc.scalar.copy(ZR[:, :, 0, :], q[:, 0:CH * n].rearrange("p (b n) -> p b n", b=CH)), f"ZA{t}")
                    root(cvr)
                    for g in range(2):
                        pr = slice(64 * g, 64 * g + 64)
                        qv = arrived(act, f"UY{g}")[:, 0:2 * CH * NS].rearrange("p (b a n) -> p b a n", b=CH, a=2)
                        run(nc.scalar.copy(Utr[pr, :, :], qv[pr, :, 0, :]), wait=False)
                        read(nc.scalar.copy(YT[pr, :, NPR:N], qv[pr, :, 1, :]), f"UY{g}")
                    for b in range(CH):
                        act.wait_ge(cvn_ready, b + 1)
                        run(f(cvsg[:, b, :], cat[:, CH + b, :], ACT.Sigmoid), cvsg_ready, wait=False)
            for b in range(CH):
                act.wait_ge(yc_ready, b + 1)
                run(f(ysq[:, b, :], YT[:, b, :], ACT.Square), ysq_ready, wait=False)
            root(yrs)

            normed_n = []

            def normalise(x, t, n):
                normed_n.append(0)
                act.wait_ge(norm_ready, len(normed_n))
                run(f(x, x, ACT.Identity, scale=rstd[0:n, t:t + 1], bias=nmr[0:n, t:t + 1]), normed, wait=False)

            for i, t in enumerate((0, 2)):
                n = TILES[t][1]
                for j in range(2):
                    u = f"g1_{t}_{j}"
                    read(nc.scalar.copy(tA[0:n, i, 512 * j:512 * j + 512], arrived(act, u)[0:n, :]), u)
            for kind, t in NORM_STEPS:
                a, n = TILES[t]
                if kind == "stats":
                    root(rstd[0:n, t:t + 1])
                elif kind == "factors":
                    normalise(xa[0:n, t, :], t, n)
            for t, (a, n) in enumerate(TILES):
                for j in range(2):
                    u = f"hT{t}_{j}"
                    read(nc.scalar.copy(h2T[:, 4 * j:4 * j + 4, a:a + n],
                                        arrived(act, u)[:, 0:4 * n].rearrange("p (b n) -> p b n", b=4)), u)
                u = f"lg{t}"
                read(nc.scalar.copy(lgt[0:n, t, :], arrived(act, u)[0:n, 0:E]), u)
                for i in ((), (0,), (1, 2))[t]:
                    act.wait_ge(delta_ready, i + 1)
                    m = TILES[i][1]
                    run(f(e4[0:m, i, :], e4[0:m, i, :], ACT.Exp), e4_ready, wait=False)
            nc.scalar.copy(small[:, 315:316], small[:, 313:314]).then_inc(y_out, 1)
            act.wait_ge(gathered, 1)
            nc.scalar.copy(gS, ps[:, 0, :]).then_inc(rows_read, 1)
            for t, (a, n) in enumerate(TILES):
                read(nc.scalar.copy(gT[0:E, a:a + n], arrived(act, f"gt{t}")[0:E, 0:n]), f"gt{t}")
            act.wait_ge(table_ready, 5)
            total = act.value_load(cumi[0:1, E:E + 1], min_val=1, max_val=MAXIT)
            with act.Fori(0, total) as it:
                act.wait_ge(gate_ready, it + 2)
                f(sigS, gateS, ACT.Sigmoid, scale=SWI).then_inc(sig_ready, 1)
                act.wait_ge(gathered, it + 2)
                nc.scalar.copy(gS, ps[:, 0, :]).then_inc(rows_read, 1)
                act.wait_ge(dn_done, it + 1)
                act.wait_ge(y_stored, it * 32 + 32)
                nc.scalar.copy(yS, ps[:, 4, :]).then_inc(y_out, 1)
                act.wait_ge(y_out, it + 2)
                for j in range(2):
                    act.dma_start(y_dram[bass.ds(it * C, C), 512 * j:512 * j + 512],
                                  yS[64 * j:64 * j + 64, :]).then_inc(y_stored, 16)
            for kind, t in NORM_STEPS:
                a, n = TILES[t]
                if kind == "stats":
                    root(rstd[0:n, t:t + 1])
                elif kind == "factors":
                    normalise(fr[0:n, t, :], t, n)

        @block.vector
        def _(dve):
            run = Counted(dve, vstep)
            V = nc.vector
            tt, ts, stt = V.tensor_tensor, V.tensor_scalar, V.scalar_tensor_tensor

            def free(ins, name):
                read(ins, name)
                evicted(dve, name)

            def ask_root(count):
                count(V.memset(small[:, 313:314], 0.0), var_ready, wait=False)
                roots.append(0)
                return len(roots)

            def invert_root(x, count=run):
                n = ask_root(count)
                dve.wait_ge(root_ready, n)
                count(V.reciprocal(x, x))

            roots = []
            run(V.memset(zs[:, :, 0:1], 0.0))
            run(V.memset(gslot, -1.0))
            dve.wait_ge(cond_in, 16)
            dve.wait_ge(csig_ready, 1)
            run(tt(cs, cs, cT, ALU.mult), cs_ready)
            dve.wait_ge(params_in, 32)
            run(ts(omk, par[:, PAR["ka"]:PAR["ka"] + CH], -1.0, 1.0, ALU.mult, ALU.add))
            q = arrived(dve, "first")
            for j in range(4):
                ins = V.tensor_copy(rows[32 * j:32 * j + 9, 0, :], q[32 * j:32 * j + 9, :])
                if j == 3:
                    free(ins, "first")
                else:
                    run(ins, wait=False)
            ab = par[:, PAR["adab"]:PAR["adab"] + 16].unsqueeze(2).to_broadcast([P, 16, 9])
            for j in range(4):
                u = f"modT{j}"
                free(tt(modT[:, j:16:4, :], arrived(dve, u)[:, 0:36].rearrange("p (a b) -> p a b", a=4),
                        ab[:, j:16:4, :], ALU.add), u)
            run(ts(modT[:, 8:16, :], modT[:, 8:16, :], 1.0, None, ALU.add))
            dve.wait_ge(x_in, 16)
            for k in range(KD):
                run(ts(hT[:, k, 0:NPR], hT[:, k, 0:NPR], modT[:, 8 + k, 0:1], modT[:, k, 0:1], ALU.mult, ALU.add),
                    wait=False)
            hs = hT[:, :, NPR:N].rearrange("p k (b t) -> p k b t", b=NB)
            run(tt(hs, hs, modT[:, 8:16, 1:9].unsqueeze(3).to_broadcast([P, KD, NB, NT]), ALU.mult))
            run(tt(hs, hs, modT[:, 0:8, 1:9].unsqueeze(3).to_broadcast([P, KD, NB, NT]), ALU.add), h_ready)
            run(V.memset(zero, 0.0), zero_ready, wait=False)

            def condition_rows(r):
                if r == 0:
                    dve.wait_ge(rows_in, 64)
                q = arrived(dve, f"row{r}")
                for j in range(4):
                    s = slice(32 * j, 32 * j + 9)
                    ins = tt(rows[s, r, :], q[s, :], adab[s, r, :], ALU.add)
                    if j == 3:
                        free(ins, f"row{r}")
                    else:
                        run(ins, wait=False)

            dve.wait_ge(states_in, 16 * 6)
            zse = [smp_ext(zs[:, b, 1 + NPR:EXT]) for b in range(SH)]
            for b in range(SH):
                run(V.tensor_copy(zse[b][:, :, 0], shift_in[:, b, :]), wait=(b == SH - 1))
            def shift(p):
                b = SHIFT_ORDER[p]
                evicted(dve, f"z{p}")
                run(tt(dprev[:, 0:NPR], zs[:, b, 0:NPR], zs[:, b, 1:1 + NPR], ALU.subtract), wait=False)
                run(tt(smp(dprev[:, NPR:N]), zse[b][:, :, 0:NT], zse[b][:, :, 1:1 + NT], ALU.subtract))
                run(stt(zm[:, b, 0:NPR], dprev[:, 0:NPR], p_("mu", b), zs[:, b, 1:1 + NPR], ALU.mult, ALU.add), wait=False)
                run(stt(smp(zm[:, b, NPR:N]), smp(dprev[:, NPR:N]), p_("mu", b), zse[b][:, :, 1:1 + NT], ALU.mult,
                        ALU.add), zm_ready)

            def glu(c):
                evicted(dve, f"z{SH + 2 * c}")
                u = f"z{SH + 2 * c + 1}"
                q = arrived(dve, u)
                run(tt(ue[:, c, TAPS - 1:PC], q[:, 0:NPR], usg[:, c, 0:NPR], ALU.mult), u_ready)
                us = ue[:, c, PC:UW].rearrange("p (b s) -> p b s", b=NB)
                run(tt(us[:, :, TAPS - 1:SC], smp(q[:, NPR:N]), smp(usg[:, c, NPR:N]), ALU.mult), u_ready)
                read(V.memset(small[:, 310:311], 0.0), u)

            r_, k_, v_ = zm[:, 0:CH, :], zm[:, CH:2 * CH, :], zm[:, 2 * CH:3 * CH, :]
            for p in range(Z_K):
                shift(p)
            for p in range(Z_K, Z_LORA):
                shift(p)
            for b in range(CH):
                run(ts(t1[:, b, :], k_[:, b, :], p_("kk", b), None, ALU.mult))
            run(tt(t2, t1, t1, ALU.mult), sq_ready)
            for p in range(Z_LORA, Z_R):
                shift(p)
            for b in range(CH):
                u = f"kk{b}"
                free(ts(kkn[:, b, :], arrived(dve, u)[:, 0:N], 1e-24 / HD, None, ALU.max), u)
            invert_root(kkn)
            run(stt(kkn, kkn, 0.125, t1, ALU.mult, ALU.mult))
            for b in range(CH):
                evicted(dve, f"a{b}")
                run(ts(kp[:, b, :], aT[:, b, :], p_("ka", b), omk[:, b:b + 1], ALU.mult, ALU.add))
            run(tt(kp, kp, k_, ALU.mult))
            for b in range(CH):
                run(stt(t2[:, b, :], r_[:, b, :], p_("rk", b), kp[:, b, :], ALU.mult, ALU.mult), rk_ready)
            for p in range(Z_R, SH):
                shift(p)
            run(V.tensor_copy(shift_out[:, :, 0], zs[:, :, NPR]), shift_ready, wait=False)
            zse_all = zs[:, :, 1 + NPR:EXT].rearrange("p c (b t) -> p c b t", b=NB)
            run(V.tensor_copy(shift_out[:, :, 1:9], zse_all[:, :, :, NT]), shift_ready)
            for b in range(CH):
                evicted(dve, f"w{b}")
                run(V.tensor_tensor_scan(cumI[:, b, :], c_("scan", N), sg[:, b, :], 0.0, ALU.mult, ALU.add))
            run(tt(EE, cumI, sg, ALU.subtract), cum_ready)
            for b in range(CH):
                u = f"rk{b}"
                free(stt(bonus[:, b, :], arrived(dve, u)[:, 0:N], float(HD), v_[:, b, :], ALU.mult, ALU.mult), u)
            glu(0)
            run(tt(t1, kkn, aT, ALU.mult))
            glu(1)
            dve.wait_ge(exp_ready, 3)
            run(tt(bt, t1, EN, ALU.mult), wait=False)
            evicted(dve, f"g{CH - 1}")
            run(tt(kt, kp, EN, ALU.mult))
            glu(2)
            glu(3)
            run(stt(AR[:, :, 0, :], kkn, -1.0, EE, ALU.mult, ALU.mult), wait=False)
            run(tt(AR[:, :, 1, :], r_, EI, ALU.mult), wait=False)
            for b in range(CH):
                for x, y in ((bb, bt), (kb, kt)):
                    lp = EI[:, b, L - 1:NPR:L].unsqueeze(2).to_broadcast([P, NPR // L, L])
                    ls = EI[:, b, NPR + NT - 1:N:NT].unsqueeze(2).to_broadcast([P, NB, NT])
                    run(tt(x[:, b, 0:NPR].rearrange("p (c l) -> p c l", l=L),
                           y[:, b, 0:NPR].rearrange("p (c l) -> p c l", l=L), lp, ALU.mult), wait=False)
                    run(tt(smp(x[:, b, NPR:N]), smp(y[:, b, NPR:N]), ls, ALU.mult),
                        tilde_ready if b == CH - 1 and x is kb else None)
            run(V.memset(ST, 0.0))
            run(V.memset(STd, 0.0), st_ready)
            for b in range(CH):
                run(ts(bonus[:, b, :], bonus[:, b, :], p_("lb", b), None, ALU.add))
            for t, (a, n) in enumerate(TILES):
                for i, x in enumerate("bkva"):
                    if i % 2:
                        free(V.tensor_copy(tok[x][0:n, t, :], arrived(dve, f"{x}tok{t}")[0:n, :]), f"{x}tok{t}")

            def convolve(k0, n):
                for k in range(k0, min(k0 + n, TAPS)):
                    for c in range(POOL_CH, CH):
                        w = PAR["cw"] + c * TAPS + k
                        us = ue[:, c, PC:UW].rearrange("p (b s) -> p b s", b=NB)
                        for x, (y, u) in enumerate(((cat[:, CH + c, 0:NPR], ue[:, c, k:k + NPR]),
                                                    (smp(cat[:, CH + c, NPR:N]), us[:, :, k:k + NT]))):
                            ends = c == CH - 1 and x == 1
                            if k == 0:
                                ins = ts(y, u, par[:, w:w + 1], p_("cb", c), ALU.mult, ALU.add)
                            else:
                                ins = stt(y, u, par[:, w:w + 1], y, ALU.mult, ALU.add)
                            run(ins, conv_rest_done if ends and k == TAPS - 1 else None, wait=ends)

            for t, (a, n) in enumerate(TILES):
                mkt = at(MK0, H, 4 * n)
                tri = c_("tri", 2 * n, n) if t < 2 else c_("tri_s", 2 * n, n)
                low = c_("low", n, n) if t < 2 else c_("low_s", n, n)
                N0 = at(nbuf[0], 2, CH, n)
                if t == 2:
                    condition_rows(1)
                    dve.wait_ge(conv_done, TAPS + 1)
                    cv = cat[:, CH:2 * CH, :]
                    free(tt(cv, cv, arrived(dve, "cm")[:, 0:N].unsqueeze(1).to_broadcast([P, CH, N]), ALU.subtract), "cm")
                    run(V.memset(small[:, 312:313], 0.0), cvc_ready, wait=False)
                TTb = [at(nbuf[4 + y], 2, CH, n) for y in range(2)]
                for h in range(H):
                    u = f"G{t}_{h}"
                    free(tt(mkt[0:n, h, :].rearrange("p (a b) -> p a b", a=2),
                            arrived(dve, u)[0:n, 0:4 * n].rearrange("p (a b) -> p a b", a=2),
                            tri.unsqueeze(1).to_broadcast([n, 2, 2 * n]), ALU.mult), u)
                for g in range(2):
                    u = f"A{t}_{g}"
                    free(tt(N0[0:n, g, :, :], arrived(dve, u)[0:n, 0:CH * n].rearrange("p (b j) -> p b j", b=CH),
                            low.unsqueeze(1).to_broadcast([n, CH, n]), ALU.mult), u)
                for g in range(2):
                    run(tt(TTb[0][0:n, g, :, :], mkt[0:n, g:H:2, 0:n],
                           ident[0:n, 0:n].unsqueeze(1).to_broadcast([n, CH, n]), ALU.add), tt0_ready)
                for m in range(1, rounds(t) + 1):
                    if t < 2:
                        convolve(16 * t + 3 * (m - 1), 3)
                    for g in range(2):
                        u = f"TT{t}_{m}_{g}"
                        free(tt(TTb[m % 2][0:n, g, :, :], TTb[(m - 1) % 2][0:n, g, :, :],
                                arrived(dve, u)[0:n, 0:CH * n].rearrange("p (b j) -> p b j", b=CH), ALU.add), u)
                if t == 0:
                    condition_rows(0)
                if t == 2:
                    run(V.tensor_copy(ZR[:, :, 1, :], AR[:, :, 1, NPR:N]), zr_ready)
                free(V.tensor_copy(ZV[0:n, :], arrived(dve, f"ZV{t}")[0:n, :]), f"ZV{t}")
                if t < 2:
                    for c in range(4):
                        rq = slice(32 * c, 32 * c + 32)
                        end = a + L * c + L - 1
                        run(tt(STd, ST, EI[:, :, end:end + 1].to_broadcast([P, CH, HD]), ALU.mult))
                        convolve(16 * t + 12 + c, 1)
                        for g in range(2):
                            u = f"U{t}_{c}_{g}"
                            hv = "p (b g v) -> p g b v"
                            free(tt(Ut[rq, :].rearrange(hv, g=2, v=HD)[:, g],
                                    ZV[rq, :].rearrange(hv, g=2, v=HD)[:, g],
                                    arrived(dve, u)[rq, 0:CH * HD].rearrange("p (b v) -> p b v", b=CH), ALU.add), u)
                        u = f"S{t}_{c}"
                        free(tt(ST, STd, arrived(dve, u)[:, 0:CH * HD].rearrange("p (b v) -> p b v", b=CH), ALU.add), u)
                else:
                    free(ts(cvr, arrived(dve, "cv")[:, 0:N], LN_EPS, None, ALU.add), "cv")
                    root_n = ask_root(run)
                    bm = c_("bmask", NB, NS).unsqueeze(2).to_broadcast([NS, NB, HD])

                    def spread_samples(b, i, x):
                        for g in range(2):
                            hs = slice(HD * (2 * b + g), HD * (2 * b + g) + HD)
                            run(tt(masked[b % 2][0:NS, i, g, :].rearrange("p (s v) -> p s v", s=NB),
                                   x[:, hs].unsqueeze(1).to_broadcast([NS, NB, HD]), bm, ALU.mult), um_ready)

                    for b in range(2):
                        spread_samples(b, 1, tok["v"][0:NS, 2, :])
                    dve.wait_ge(root_ready, root_n)
                    run(V.reciprocal(cvr, cvr))
                    run(tt(cv, cv, cvr.unsqueeze(1).to_broadcast([P, CH, N]), ALU.mult))
                    for b in range(CH):
                        run(ts(cv[:, b, :], cv[:, b, :], p_("cg", b), p_("cbt", b), ALU.mult, ALU.add), cvn_ready)
                    free(tt(Ut[0:NS, :], ZV[0:NS, :], arrived(dve, "Us")[0:NS, :], ALU.add), "Us")
                    for b in range(CH):
                        if b >= 2:
                            arrived(dve, f"Ss{b - 2}")
                            spread_samples(b, 1, tok["v"][0:NS, 2, :])
                        spread_samples(b, 0, Ut[0:NS, :])
                    for b in range(CH):
                        lam = EI[:, b, NPR + NT - 1:N:NT].unsqueeze(2).to_broadcast([P, NB, HD])
                        run(tt(ST0[:, b, :, :], ST0[:, b, :, :], lam, ALU.mult))
                        u = f"Ss{b}"
                        free(tt(ST0[:, b, :, :], ST0[:, b, :, :],
                                arrived(dve, u).rearrange("p (s v) -> p s v", s=NB), ALU.add), u)
                if t < 2:
                    for c in range(4):
                        for g in range(2):
                            evicted(dve, f"Y{t}_{c}_{g}")
                else:
                    for g in range(2):
                        evicted(dve, f"UY{g}")
                free(tt(YT[:, :, a:a + n], YT[:, :, a:a + n],
                        arrived(dve, f"Y{t}")[:, 0:CH * n].rearrange("p (b n) -> p b n", b=CH), ALU.add), f"Y{t}")
            for b in range(CH):
                dve.wait_ge(cvsg_ready, b + 1)
                run(tt(cv[:, b, :], cv[:, b, :], cvsg[:, b, :], ALU.mult), cat_ready)
            for b in range(CH):
                free(tt(YT[:, b, :], YT[:, b, :], arrived(dve, f"gm{b}")[:, 0:N], ALU.subtract), f"gm{b}")
                run(V.memset(small[:, 311:312], 0.0), yc_ready, wait=False)
            for b in range(CH):
                free(ts(yrs[:, b, :], arrived(dve, f"gv{b}")[:, 0:N], GN_EPS, None, ALU.add), f"gv{b}")
            y_root = ask_root(run)
            dve.wait_ge(root_ready, y_root)
            run(V.reciprocal(yrs, yrs))
            run(tt(YT, YT, yrs, ALU.mult))
            for b in range(CH):
                run(stt(YT[:, b, :], YT[:, b, :], p_("lg", b), bonus[:, b, :], ALU.mult, ALU.add))
                run(tt(cat[:, b, :], YT[:, b, :], gate[:, b, :], ALU.mult), cat_ready)

            asked, scaled = {}, []

            def norm_step(kind, t, x, g, b, step, ready):
                n = TILES[t][1]
                r1, m1 = rstd[0:n, t:t + 1], nmr[0:n, t:t + 1]
                if kind == "stats":
                    for j in range(2):
                        step(V.bn_stats(stats[0:n, t, j, :], x[:, 512 * j:512 * j + 512]), wait=(j == 1))
                    step(V.bn_aggr(mv[0:n, t, :], stats[0:n, t, :, :]))
                    step(ts(r1, mv[0:n, t, 1:2], LN_EPS, None, ALU.add))
                    asked[t] = ask_root(step)
                elif kind == "factors":
                    dve.wait_ge(root_ready, asked[t])
                    step(V.reciprocal(r1, r1))
                    step(stt(m1, mv[0:n, t, 0:1], -1.0, r1, ALU.mult, ALU.mult), norm_ready, wait=False)
                else:
                    scaled.append(0)
                    dve.wait_ge(normed, len(scaled))
                    step(tt(x, x, g[0:n, :], ALU.mult))
                    step(tt(x, x, b[0:n, :], ALU.add), ready)

            def mixed(t):
                n = TILES[t][1]
                for j in range(2):
                    js = slice(512 * j, 512 * j + 512)
                    evicted(dve, f"g1_{2 * (t // 2)}_{j}")
                    u = f"mix_{t}_{j}"
                    free(tt(xa[0:n, t, js], tA[0:n, t // 2, js], arrived(dve, u)[0:n, :], ALU.mult), u)
                run(stt(xa[0:n, t, :], xin[0:n, t, :], ALPHA, xa[0:n, t, :], ALU.mult, ALU.add))

            def modulated(t):
                n = TILES[t][1]
                for j in range(2):
                    js = slice(512 * j, 512 * j + 512)
                    u = f"sc2_{2 * (t // 2)}_{j}"
                    run(stt(h2[0:n, t, js], arrived(dve, u)[0:n, :], 1.0, xa[0:n, t, js], ALU.add, ALU.mult))
                for j in range(2):
                    js = slice(512 * j, 512 * j + 512)
                    u = f"sh2_{2 * (t // 2)}_{j}"
                    run(tt(h2[0:n, t, js], h2[0:n, t, js], arrived(dve, u)[0:n, :], ALU.add), h2_ready)
                if t > 0:
                    for i, x in enumerate(("sc2", "sh2")):
                        for j in range(2):
                            c0 = 378 + 4 * t + 2 * i + j
                            read(V.memset(small[:, c0:c0 + 1], 0.0), f"{x}_{2 * (t // 2)}_{j}")

            def choose_experts(t):
                n = TILES[t][1]
                u = f"lg{t}"
                evicted(dve, u)
                run(V.max(top_v[0:n, :], lgt[0:n, t, :]))
                run(V.max_index(top_i[0:n, t, :], top_v[0:n, :], lgt[0:n, t, :]))
                run(V.tensor_copy(idxf[0:n, :], top_i[0:n, t, :]))
                run(ts(e4[0:n, t, :], top_v[0:n, 0:4], top_v[0:n, 0:1], None, ALU.subtract), delta_ready)
                o4 = oh[0:n, 4 * t:4 * t + 4, :]
                run(tt(o4, c_("item", E, n).unsqueeze(1).to_broadcast([n, 4, E]),
                       idxf[0:n, 0:4].unsqueeze(2).to_broadcast([n, 4, E]), ALU.is_equal))
                run(tt(mk[0:n, t, :], o4[:, 0, :], o4[:, 1, :], ALU.add))
                run(tt(mk[0:n, t, :], mk[0:n, t, :], o4[:, 2, :], ALU.add))
                run(tt(mk[0:n, t, :], mk[0:n, t, :], o4[:, 3, :], ALU.add), mask_ready)

            def weigh_experts(t):
                n = TILES[t][1]
                o4 = oh[0:n, 4 * t:4 * t + 4, :]
                dve.wait_ge(e4_ready, t + 1)
                run(V.tensor_reduce(esum[0:n, :], e4[0:n, t, :], AX, ALU.add))
                run(V.reciprocal(esum[0:n, :], esum[0:n, :]))
                run(ts(gates[0:n, t, :], e4[0:n, t, :], esum[0:n, :], None, ALU.mult))
                run(ts(Gd[0:n, t, :], o4[:, 0, :], gates[0:n, t, 0:1], None, ALU.mult))
                for k in range(1, 4):
                    run(stt(Gd[0:n, t, :], o4[:, k, :], gates[0:n, t, k:k + 1], Gd[0:n, t, :], ALU.mult, ALU.add),
                        gd_ready if k == 3 else None)

            dve.wait_ge(tail_in, 16 * 7)
            for kind, t in NORM_STEPS:
                if kind == "stats":
                    mixed(t)
                norm_step(kind, t, xa[0:TILES[t][1], t, :], lnp[:, 0, :], lnp[:, 1, :], run, x1_ready)
                if kind == "out":
                    modulated(t)
                    if t:
                        choose_experts(t - 1)
            weigh_experts(0)
            choose_experts(2)
            weigh_experts(1)
            free(V.tensor_copy(cnt, arrived(dve, "count")[:, 0:E]), "count")
            run(ts(npf, cnt, float(C), 1.0, ALU.is_gt, ALU.add))
            for i in range(2, (N - 1) // C + 1):
                run(ts(npt, cnt, float(C * i), None, ALU.is_gt))
                run(tt(npf, npf, npt, ALU.add))
            run(V.memset(cumf[:, 0:1], 0.0))
            run(V.tensor_tensor_scan(cumf[:, 1:E + 1], c_("ones", E), npf, 0.0, ALU.mult, ALU.add))
            for t, (a, n) in enumerate(TILES):
                s = slotv[0:n, E * t:E * t + E]
                u = f"rank{t}"
                free(stt(s, cumf[0:n, 0:E], float(C), arrived(dve, u)[0:n, 0:E], ALU.mult, ALU.add), u)
                run(stt(gslot[0:n, t, :], s, 1.0, mk[0:n, t, :], ALU.add, ALU.mult))
                run(ts(gslot[0:n, t, :], gslot[0:n, t, :], -1.0, None, ALU.add))
            slot = c_("slot", C)
            for i, m in enumerate((gate_ready, lin_ready)):
                V.memset(small[:, 316 + i:317 + i], 0.0).then_inc(m, 1)

            def choose(it, e):
                ts(slot, slot, float(C), None, ALU.add).then_inc(slot_ready, 1)
                dve.wait_ge(slot_ready, it + 1)
                tt(pick, gslot[:, :, bass.ds(e, 1)].to_broadcast([P, 3, C]),
                   slot.unsqueeze(1).to_broadcast([P, 3, C]), ALU.is_equal).then_inc(pick_ready, 1)
                V.tensor_copy(sel_e[0:E, :], cst[0:E, bass.ds(e + CST["ident"], 1)].to_broadcast([E, C])
                              ).then_inc(sel_ready, 1)

            choose(0, 0)
            weigh_experts(2)
            for t, (a, n) in enumerate(TILES):
                s = slotv[0:n, E * t:E * t + E]
                o4 = ohs[0:n, 4 * t:4 * t + 4, :]
                run(tt(o4, oh[0:n, 4 * t:4 * t + 4, :], s.unsqueeze(1).to_broadcast([n, 4, E]), ALU.mult))
                run(V.tensor_reduce(sidx[0:n, 4 * t:4 * t + 4], o4, AX, ALU.add))
                run(V.tensor_copy(slot_i[0:n, 4 * t:4 * t + 4], sidx[0:n, 4 * t:4 * t + 4]), table_ready)
            run(V.tensor_copy(cumi[:, :], cumf), table_ready)
            run(tt(item_m, c_("item", MAXIT + 1).unsqueeze(2).to_broadcast([P, MAXIT + 1, E]),
                   cumf[:, 1:E + 1].unsqueeze(1).to_broadcast([P, MAXIT + 1, E]), ALU.is_ge))
            run(V.tensor_reduce(item_f, item_m, AX, ALU.add))
            run(ts(item_i[:, :], item_f, float(E - 1), None, ALU.min), table_ready)
            total = dve.value_load(cumi[0:1, E:E + 1], min_val=1, max_val=MAXIT)
            with dve.Fori(0, total) as it:
                dve.wait_ge(tokens_turned, it + 1)
                V.tensor_copy(hTe, ps[:, 5, :].rearrange("p (b c) -> p b c", b=4)).then_inc(hTe_ready, 1)
                choose(it + 1, dve.value_load(item_i[0:1, bass.ds(it + 1, 1)], min_val=0, max_val=E - 1))
                dve.wait_ge(gu_done, it + 1)
                ts(gateS, ps[:, 1, :], LIMIT, None, ALU.min).then_inc(gate_ready, 1)
                ts(linS, ps[:, 2, :], LIMIT, -LIMIT, ALU.min, ALU.max).then_inc(lin_ready, 1)
                dve.wait_ge(sig_ready, it + 1)
                tt(gateS, gateS, sigS, ALU.mult).then_inc(prod_ready, 1)
                dve.wait_ge(prod_ready, it + 1)
                stt(actS, linS, 1.0, gateS, ALU.add, ALU.mult).then_inc(act_ready, 1)
                dve.wait_ge(act_turned, it + 1)
                V.tensor_copy(actT, ps[:, 3, :].rearrange("p (b c) -> p b c", b=4)).then_inc(actT_ready, 1)
            fin = Counted(dve, fstep)
            dve.wait_ge(gu_done, total)
            for t, (a, n) in enumerate(TILES):
                for k in range(4):
                    ts(dgate[0:n, 4 * t + k, 0:n], ident[0:n, 0:n], gates[0:n, t, k:k + 1], None, ALU.mult
                       ).then_inc(dgate_ready, 1)
            dve.wait_ge(final_in, 16 * 14)
            for kind, t in NORM_STEPS:
                n = TILES[t][1]
                if kind == "stats":
                    for j in (1, 0):
                        js = slice(512 * j, 512 * j + 512)
                        x, q = fr[0:n, t, js], ps[0:n, END_BANKS[2 * t + j], :]
                        if (t, j) == VECTOR_SUM:
                            dve.wait_ge(bias_ready, 1)
                            dve.wait_ge(rowsg_in[t], 64)
                            for k in range(4):
                                fin(stt(x, yg[0:n, 4 * t + k, js], gates[0:n, t, k:k + 1], q if k == 0 else x,
                                        ALU.mult, ALU.add))
                            q = x
                        else:
                            dve.wait_ge(sum_ready, 2 * t + 1)
                        fin(tt(x, q, fg[0:n, t // 2, js], ALU.mult))
                    fin(stt(fr[0:n, t, :], fx[0:n, t, :], ALPHA, fr[0:n, t, :], ALU.mult, ALU.add))
                norm_step(kind, t, fr[0:n, t, :], fln[:, 0, :], fln[:, 1, :], fin, out_ready)


def smp_ext(a):
    return a.rearrange("p (b t) -> p b t", b=NB)


def kernel(**inputs):
    import numpy as np
    import concourse.bacc as bacc
    from concourse.bass_utils import run_bass_kernel_spmd

    x = {k: np.asarray(v) for k, v in inputs.items()}
    f = np.float32

    def blocks(v):
        v = v.reshape(v.shape[:-1] + (-1, P))
        return np.moveaxis(v, (-1, -2), (0, 1))

    cst = np.zeros((P, NCST), f)

    def put(name, a):
        cst[0:a.shape[0], CST[name]:CST[name] + a.shape[1]] = a

    i = np.arange(P)
    same = (i[:, None] // L) == (i[None, :] // L)
    put("ident", np.eye(P, dtype=f))
    put("tri", np.concatenate([same & (i[:, None] < i[None, :]), same & (i[:, None] <= i[None, :])], 1).astype(f))
    put("low", (same & (i[:, None] > i[None, :])).astype(f))
    j = np.arange(NS)
    same_s = (j[:, None] // NT) == (j[None, :] // NT)
    put("tri_s", np.concatenate([same_s & (j[:, None] < j[None, :]), same_s & (j[:, None] <= j[None, :])], 1).astype(f))
    put("low_s", (same_s & (j[:, None] > j[None, :])).astype(f))
    reset = np.ones(N, f)
    reset[0:NPR:L] = 0
    reset[NPR:N:NT] = 0
    put("scan", np.tile(reset, (P, 1)))
    put("head", ((i[:, None] // HD) == (i[None, :] // HD)).astype(f) / f(HD))
    put("c512", np.full((P, P), 1.0 / 512, f))
    sel = np.zeros((P, P + NS), f)
    for g in range(4):
        sel[32 * g, 0:P] = 1
        for b in range(NB):
            sel[32 * g + 1 + b, P + NT * b:P + NT * b + NT] = 1
    put("sel", sel)
    put("before", (i[:, None] < i[None, :]).astype(f))
    put("ones", np.ones((P, P), f))
    put("slot", np.tile(np.arange(C, dtype=f) - C, (P, 1)))
    put("item", np.tile(np.arange(MAXIT + 1, dtype=f), (P, 1)))
    put("bmask", ((j[:, None] // NT) == np.arange(NB)[None, :]).astype(f))

    par = np.concatenate([blocks(x["tm_mu"][0]), blocks(x["w0"][0]), blocks(x["a0"][0]), blocks(x["k_k"][0]),
                          blocks(x["k_a"][0]), blocks(x["r_k"][0].reshape(-1)), blocks(x["lnx_g"][0]),
                          blocks(x["lnx_b"][0]), blocks(x["conv_w"][0]).reshape(P, -1), blocks(x["conv_b"][0]),
                          blocks(x["conv_ln_g"][0]), blocks(x["conv_ln_b"][0]), blocks(x["ada_b"][0][0:2 * D])], 1)
    tokens = np.concatenate([x["x_prompt"].reshape(NPR, D), x["x_sample"].reshape(NS, D)])
    cond = np.concatenate([x["c_prompt"], x["c_sample"]])

    def cols(w, width):
        return w.reshape(KD, P, -1, width).transpose(2, 1, 0, 3)

    win = cols(x["w_in"][0], P)
    order = SHIFT_ORDER + [b for c in range(CH) for b in (SH + CH + c, SH + c)]
    ada_b = x["ada_b"][0].reshape(12, 512)
    arrays = {
        "cst": cst, "par": par, "cT": blocks(cond), "xT": blocks(tokens), "x": tokens,
        "adab_rows": np.stack([np.tile(ada_b[[4 + g, 8 + g]][None], (9, 1, 1)) for g in range(4)]),
        "ada": cols(x["ada_w"][0], 512), "win": win[order],
        "lora": np.stack([np.concatenate([x["w2"][0], x["a2"][0]]), x["g2"][0]], 1),
        "shiftT": blocks(x["state_shift"][0]),
        "conv0": np.zeros((P, CH, TAPS - 1), f),
        "convs": blocks(x["state_conv"][0]),
        "w_out": x["w_out"][0].reshape(KD, P, D).transpose(1, 0, 2),
        "wkvT": x["state_wkv"][0].reshape(NB, CH, 2, HD, HD).transpose(2, 4, 1, 0, 3).reshape(P, CH, NB, HD),
        "ln": np.stack([x["ln1_g"][0], x["ln1_b"][0], x["ln2_g"][0], x["ln2_b"][0]]),
        "rw": x["router_w"][0].reshape(KD, P, E).transpose(1, 0, 2), "rb": x["router_b"],
        "w_gu": x["w_gu"][0], "b_gu": x["b_gu"][0], "w_dn": x["w_dn"][0], "b_dn": x["b_dn"][0],
    }
    outs = {"y": (N, D), "wkv_p": (P, CH, HD), "wkv_s": (P, CH, NB, HD), "shift_out": (P, SH, 9),
            "conv_p": (P, CH, TAPS - 1), "conv_s": (P, CH, NB, TAPS - 1)}
    nc = bacc.Bacc("TRN2", target_bir_lowering=False, num_devices=1)
    arrays = {f"in_{k}": np.ascontiguousarray(v) for k, v in arrays.items()}
    io = {k[3:]: nc.dram_tensor(k, v.shape, mybir.dt.from_np(v.dtype), kind="ExternalInput").ap()
          for k, v in arrays.items()}
    for k, shape in outs.items():
        io[k] = nc.dram_tensor(f"out_{k}", shape, F32, kind="ExternalOutput").ap()
    build(nc, io)
    r = run_bass_kernel_spmd(nc, [arrays], core_ids=[0]).results[0]
    r = {k: np.asarray(r[f"out_{k}"]) for k in outs}
    y = r["y"]
    wkv_p = r["wkv_p"].reshape(2, HD, CH, HD).transpose(2, 0, 3, 1).reshape(1, 1, H, HD, HD)
    wkv_s = r["wkv_s"].reshape(2, HD, CH, NB, HD).transpose(3, 2, 0, 4, 1).reshape(1, NB, H, HD, HD)
    shift = r["shift_out"].transpose(2, 1, 0).reshape(9, SH * P)
    conv_p = r["conv_p"].transpose(2, 1, 0).reshape(1, 1, TAPS - 1, CH * P)
    conv_s = r["conv_s"].transpose(2, 3, 1, 0).reshape(1, NB, TAPS - 1, CH * P)
    c = np.ascontiguousarray
    return (c(y[0:NPR].reshape(1, NPR, D)), c(y[NPR:N].reshape(NB, NT, D)), c(wkv_p), c(wkv_s),
            c(shift[0:1].reshape(1, 1, -1)), c(shift[1:9].reshape(1, NB, -1)), c(conv_p), c(conv_s))
```
